# Optimizing a Trainium2 kernel written in Bass

```python
import numpy as np
import jax, jax.numpy as jnp
from jax import lax

D_MODEL = 2048
BATCH = 1
SEQ = 256
DEPTH = 1

EPS = 1e-6
NEG_INF = -1e30
FORCE = 1e9
ROPE_THETA = 500000.0
Q_BLOCK = 128

MLA_HEADS = 16
MLA_NOPE = 128
MLA_ROPE = 64
MLA_QK = MLA_NOPE + MLA_ROPE
MLA_V = 128
MLA_Q_RANK = 512
MLA_KV_RANK = 512

NSA_HEADS = 16
NSA_GROUPS = 4
NSA_HPG = NSA_HEADS // NSA_GROUPS
NSA_DK = 192
NSA_DV = 128
NSA_ROPE = NSA_DK // 4
CMP_LEN = 32
CMP_STRIDE = 16
CMP_HIDDEN_K = 4 * NSA_DK
CMP_HIDDEN_V = 4 * NSA_DV
SLC_LEN = 64
SLC_TOPK = 16
WINDOW = 512
SLC_Q_CHUNK = 32

N_BRANCHES = 2
D_FF = -(-8 * D_MODEL // (3 * 256)) * 256

IN_SIZES = (
    MLA_Q_RANK, MLA_KV_RANK, MLA_ROPE,
    NSA_HEADS * NSA_DK,
    NSA_GROUPS * NSA_DK, NSA_GROUPS * NSA_DV,
    NSA_GROUPS * NSA_DK, NSA_GROUPS * NSA_DV,
    NSA_GROUPS * NSA_DK, NSA_GROUPS * NSA_DV,
    NSA_HEADS * 3,
    N_BRANCHES * D_MODEL,
)
D_IN = sum(IN_SIZES)

kernel_name = "hybrid_mla_nsa_gated_swiglu"

def rmsnorm(x, g):
    xf = x.astype(jnp.float32)
    y = xf * lax.rsqrt(jnp.mean(xf * xf, axis=-1, keepdims=True) + EPS)
    return (y * g.astype(jnp.float32)).astype(x.dtype)

def rope_tables(pos, rot_dim):
    inv = ROPE_THETA ** (-jnp.arange(0, rot_dim, 2, dtype=jnp.float32) / rot_dim)
    ang = pos.astype(jnp.float32)[:, None] * inv[None, :]
    return jnp.cos(ang), jnp.sin(ang)

def apply_rope(x, cos, sin, start, rot_dim):
    half = rot_dim // 2
    xr = x[..., start:start + rot_dim].astype(jnp.float32)
    x1, x2 = xr[..., :half], xr[..., half:]
    rot = jnp.concatenate([x1 * cos - x2 * sin, x2 * cos + x1 * sin], axis=-1).astype(x.dtype)
    return jnp.concatenate([x[..., :start], rot, x[..., start + rot_dim:]], axis=-1)

def masked_softmax(s, mask):
    s = jnp.where(mask, s, NEG_INF)
    m = jnp.max(s, axis=-1, keepdims=True)
    p = jnp.where(mask, jnp.exp(s - m), 0.0)
    return p / jnp.maximum(jnp.sum(p, axis=-1, keepdims=True), 1e-30)

def dense_causal_attention(q, k, v, scale):
    T = q.shape[2]
    outs = []
    for c in range(T // Q_BLOCK):
        s0, e = c * Q_BLOCK, (c + 1) * Q_BLOCK
        s = jnp.einsum('bhqd,bhkd->bhqk', q[:, :, s0:e], k[:, :, :e]).astype(jnp.float32) * scale
        mask = jnp.arange(e)[None, :] <= jnp.arange(s0, e)[:, None]
        p = masked_softmax(s, mask)
        outs.append(jnp.einsum('bhqk,bhkd->bhqd', p.astype(v.dtype), v[:, :, :e]))
    return jnp.concatenate(outs, axis=2)

def sliding_window_attention(q, k, v, scale):
    B, G, R, T, _ = q.shape
    span = Q_BLOCK + WINDOW
    k_pad = jnp.pad(k, ((0, 0), (0, 0), (WINDOW, 0), (0, 0)))
    v_pad = jnp.pad(v, ((0, 0), (0, 0), (WINDOW, 0), (0, 0)))

    def block(c):
        s0 = c * Q_BLOCK
        qb = lax.dynamic_slice_in_dim(q, s0, Q_BLOCK, axis=3)
        kb = lax.dynamic_slice_in_dim(k_pad, s0, span, axis=2)
        vb = lax.dynamic_slice_in_dim(v_pad, s0, span, axis=2)
        t = s0 + jnp.arange(Q_BLOCK)
        pk = s0 - WINDOW + jnp.arange(span)
        d = t[:, None] - pk[None, :]
        mask = (pk[None, :] >= 0) & (d >= 0) & (d < WINDOW)
        s = jnp.einsum('bgrqd,bgkd->bgrqk', qb, kb).astype(jnp.float32) * scale
        p = masked_softmax(s, mask)
        return jnp.einsum('bgrqk,bgkd->bgrqd', p.astype(vb.dtype), vb)

    o = lax.map(block, jnp.arange(T // Q_BLOCK))
    o = jnp.moveaxis(o, 0, 3)
    return o.reshape(B, G, R, T, o.shape[-1])

def compress_blocks(x, pe, w1, b1, w2, b2):
    T = x.shape[2]
    ncmp = (T - CMP_LEN) // CMP_STRIDE + 1
    idx = np.arange(ncmp)[:, None] * CMP_STRIDE + np.arange(CMP_LEN)[None, :]
    blocks = x[:, :, idx] + pe
    flat = blocks.reshape(blocks.shape[:3] + (-1,))
    return jax.nn.gelu(flat @ w1 + b1) @ w2 + b2

def select_blocks(p_cmp, T):
    nb = T // SLC_LEN
    ncmp = p_cmp.shape[-1]
    cs = np.arange(ncmp)[:, None] * CMP_STRIDE
    ss = np.arange(nb)[None, :] * SLC_LEN
    overlap = np.clip(np.minimum(cs + CMP_LEN, ss + SLC_LEN) - np.maximum(cs, ss), 0, None) / CMP_LEN
    imp = jnp.einsum('bgrtc,cj->bgtj', p_cmp, jnp.asarray(overlap, jnp.float32))
    tb = jnp.arange(T)[:, None] // SLC_LEN
    jb = jnp.arange(nb)[None, :]
    forced = (jb == 0) | (jb == tb) | (jb == tb - 1)
    valid = jb <= tb
    score = jnp.where(forced, FORCE, jnp.where(valid, imp, -FORCE))
    _, idx = lax.top_k(score, min(SLC_TOPK, nb))
    return idx

def selected_block_attention(q, k, v, sel_idx, scale):
    B, G, R, T, _ = q.shape
    nb = T // SLC_LEN
    n = sel_idx.shape[-1]
    kb_all = k.reshape(B, G, nb, SLC_LEN, k.shape[-1])
    vb_all = v.reshape(B, G, nb, SLC_LEN, v.shape[-1])
    bi = jnp.arange(B)[:, None, None, None]
    gi = jnp.arange(G)[None, :, None, None]

    def chunk(c):
        s0 = c * SLC_Q_CHUNK
        qc = lax.dynamic_slice_in_dim(q, s0, SLC_Q_CHUNK, axis=3)
        idx = lax.dynamic_slice_in_dim(sel_idx, s0, SLC_Q_CHUNK, axis=2)
        kg = kb_all[bi, gi, idx]
        vg = vb_all[bi, gi, idx]
        s = jnp.einsum('bgrqd,bgqnld->bgrqnl', qc, kg).astype(jnp.float32) * scale
        t = s0 + jnp.arange(SLC_Q_CHUNK)
        pk = idx[..., None] * SLC_LEN + jnp.arange(SLC_LEN)
        mask = (pk <= t[None, None, :, None, None])[:, :, None].reshape(B, G, 1, SLC_Q_CHUNK, n * SLC_LEN)
        p = masked_softmax(s.reshape(B, G, R, SLC_Q_CHUNK, n * SLC_LEN), mask)
        p = p.reshape(B, G, R, SLC_Q_CHUNK, n, SLC_LEN)
        return jnp.einsum('bgrqnl,bgqnld->bgrqd', p.astype(vg.dtype), vg)

    o = lax.map(chunk, jnp.arange(T // SLC_Q_CHUNK))
    o = jnp.moveaxis(o, 0, 3)
    return o.reshape(B, G, R, T, o.shape[-1])

def hybrid_layer(x, attn_norm_g, w_in, mla_q_lat_g, mla_kv_lat_g, mla_w_uq, mla_w_uk, mla_w_uv,
                 mla_q_norm_g, mla_k_norm_g, nsa_q_norm_g, nsa_k_norm_g, cmp_pe_k, cmp_pe_v,
                 cmp_k_w1, cmp_k_b1, cmp_k_w2, cmp_k_b2, cmp_v_w1, cmp_v_b1, cmp_v_w2, cmp_v_b2,
                 w_proj_mla, w_proj_nsa, w_out, ffn_norm_g, w_ffn_gate, w_ffn_up, w_ffn_down):
    B, T, _ = x.shape
    pos = jnp.arange(T)
    xn = rmsnorm(x, attn_norm_g)
    proj = xn @ w_in
    offsets = [int(o) for o in np.cumsum(IN_SIZES)[:-1]]
    (cq, ckv, kr, q_nsa, kc, vc, ks, vs, kw, vw, g_nsa, g_merge) = jnp.split(proj, offsets, axis=-1)

    cq = rmsnorm(cq, mla_q_lat_g)
    q = (cq @ mla_w_uq).reshape(B, T, MLA_HEADS, MLA_QK).transpose(0, 2, 1, 3)
    ckv = rmsnorm(ckv, mla_kv_lat_g)
    k_nope = (ckv @ mla_w_uk).reshape(B, T, MLA_HEADS, MLA_NOPE).transpose(0, 2, 1, 3)
    v = (ckv @ mla_w_uv).reshape(B, T, MLA_HEADS, MLA_V).transpose(0, 2, 1, 3)
    k_rope = jnp.broadcast_to(kr[:, None], (B, MLA_HEADS, T, MLA_ROPE))
    k = jnp.concatenate([k_nope, k_rope], axis=-1)
    cos_m, sin_m = rope_tables(pos, MLA_ROPE)
    q = apply_rope(rmsnorm(q, mla_q_norm_g), cos_m, sin_m, MLA_NOPE, MLA_ROPE)
    k = apply_rope(rmsnorm(k, mla_k_norm_g), cos_m, sin_m, MLA_NOPE, MLA_ROPE)
    o_mla = dense_causal_attention(q, k, v, MLA_QK ** -0.5)
    y_mla = o_mla.transpose(0, 2, 1, 3).reshape(B, T, MLA_HEADS * MLA_V) @ w_proj_mla

    scale = NSA_DK ** -0.5
    cos_n, sin_n = rope_tables(pos, NSA_ROPE)
    qn = q_nsa.reshape(B, T, NSA_HEADS, NSA_DK).transpose(0, 2, 1, 3)
    qn = apply_rope(rmsnorm(qn, nsa_q_norm_g), cos_n, sin_n, 0, NSA_ROPE)
    qn = qn.reshape(B, NSA_GROUPS, NSA_HPG, T, NSA_DK)

    def kv_heads(t, d):
        return t.reshape(B, T, NSA_GROUPS, d).transpose(0, 2, 1, 3)

    k_c = compress_blocks(kv_heads(kc, NSA_DK), cmp_pe_k, cmp_k_w1, cmp_k_b1, cmp_k_w2, cmp_k_b2)
    v_c = compress_blocks(kv_heads(vc, NSA_DV), cmp_pe_v, cmp_v_w1, cmp_v_b1, cmp_v_w2, cmp_v_b2)
    ncmp = k_c.shape[2]
    cmp_end = jnp.arange(ncmp) * CMP_STRIDE + CMP_LEN - 1
    cos_c, sin_c = rope_tables(cmp_end, NSA_ROPE)
    k_c = apply_rope(rmsnorm(k_c, nsa_k_norm_g[0]), cos_c, sin_c, 0, NSA_ROPE)
    s_c = jnp.einsum('bgrtd,bgcd->bgrtc', qn, k_c).astype(jnp.float32) * scale
    p_c = masked_softmax(s_c, cmp_end[None, :] <= pos[:, None])
    o_c = jnp.einsum('bgrtc,bgcd->bgrtd', p_c.astype(v_c.dtype), v_c)

    sel_idx = select_blocks(p_c, T)
    k_s = apply_rope(rmsnorm(kv_heads(ks, NSA_DK), nsa_k_norm_g[1]), cos_n, sin_n, 0, NSA_ROPE)
    o_s = selected_block_attention(qn, k_s, kv_heads(vs, NSA_DV), sel_idx, scale)

    k_w = apply_rope(rmsnorm(kv_heads(kw, NSA_DK), nsa_k_norm_g[2]), cos_n, sin_n, 0, NSA_ROPE)
    o_w = sliding_window_attention(qn, k_w, kv_heads(vw, NSA_DV), scale)

    g = jax.nn.sigmoid(g_nsa.astype(jnp.float32)).astype(x.dtype)
    g = g.reshape(B, T, NSA_GROUPS, NSA_HPG, 3).transpose(0, 2, 3, 1, 4)
    o_nsa = g[..., 0:1] * o_c + g[..., 1:2] * o_s + g[..., 2:3] * o_w
    y_nsa = o_nsa.transpose(0, 3, 1, 2, 4).reshape(B, T, NSA_HEADS * NSA_DV) @ w_proj_nsa

    gm = jax.nn.sigmoid(g_merge.astype(jnp.float32)).astype(x.dtype).reshape(B, T, N_BRANCHES, D_MODEL)
    h = x + (gm[:, :, 0] * y_mla + gm[:, :, 1] * y_nsa) @ w_out

    hn = rmsnorm(h, ffn_norm_g)
    ff = (jax.nn.silu(hn @ w_ffn_gate) * (hn @ w_ffn_up)) @ w_ffn_down
    return h + ff

def setup_inputs(seed: int = 0) -> dict:
    key = jax.random.key(seed)
    keys = iter(jax.random.split(key, 32))

    def w(shape, fan_in):
        return jax.random.normal(next(keys), (DEPTH,) + shape, jnp.float32) * fan_in ** -0.5

    def gain(shape):
        return 1.0 + 0.01 * jax.random.normal(next(keys), (DEPTH,) + shape, jnp.float32)

    def small(shape, s):
        return s * jax.random.normal(next(keys), (DEPTH,) + shape, jnp.float32)

    x = jax.random.normal(next(keys), (BATCH, SEQ, D_MODEL), jnp.float32)
    return {
        "x": x,
        "attn_norm_g": gain((D_MODEL,)),
        "w_in": w((D_MODEL, D_IN), D_MODEL),
        "mla_q_lat_g": gain((MLA_Q_RANK,)),
        "mla_kv_lat_g": gain((MLA_KV_RANK,)),
        "mla_w_uq": w((MLA_Q_RANK, MLA_HEADS * MLA_QK), MLA_Q_RANK),
        "mla_w_uk": w((MLA_KV_RANK, MLA_HEADS * MLA_NOPE), MLA_KV_RANK),
        "mla_w_uv": w((MLA_KV_RANK, MLA_HEADS * MLA_V), MLA_KV_RANK),
        "mla_q_norm_g": gain((MLA_QK,)),
        "mla_k_norm_g": gain((MLA_QK,)),
        "nsa_q_norm_g": gain((NSA_DK,)),
        "nsa_k_norm_g": gain((3, NSA_DK)),
        "cmp_pe_k": small((CMP_LEN, NSA_DK), 0.1),
        "cmp_pe_v": small((CMP_LEN, NSA_DV), 0.1),
        "cmp_k_w1": w((CMP_LEN * NSA_DK, CMP_HIDDEN_K), CMP_LEN * NSA_DK),
        "cmp_k_b1": small((CMP_HIDDEN_K,), 0.01),
        "cmp_k_w2": w((CMP_HIDDEN_K, NSA_DK), CMP_HIDDEN_K),
        "cmp_k_b2": small((NSA_DK,), 0.01),
        "cmp_v_w1": w((CMP_LEN * NSA_DV, CMP_HIDDEN_V), CMP_LEN * NSA_DV),
        "cmp_v_b1": small((CMP_HIDDEN_V,), 0.01),
        "cmp_v_w2": w((CMP_HIDDEN_V, NSA_DV), CMP_HIDDEN_V),
        "cmp_v_b2": small((NSA_DV,), 0.01),
        "w_proj_mla": w((MLA_HEADS * MLA_V, D_MODEL), MLA_HEADS * MLA_V),
        "w_proj_nsa": w((NSA_HEADS * NSA_DV, D_MODEL), NSA_HEADS * NSA_DV),
        "w_out": w((D_MODEL, D_MODEL), D_MODEL),
        "ffn_norm_g": gain((D_MODEL,)),
        "w_ffn_gate": w((D_MODEL, D_FF), D_MODEL),
        "w_ffn_up": w((D_MODEL, D_FF), D_MODEL),
        "w_ffn_down": w((D_FF, D_MODEL), D_FF),
    }

def reference(x, attn_norm_g, w_in, mla_q_lat_g, mla_kv_lat_g, mla_w_uq, mla_w_uk, mla_w_uv,
              mla_q_norm_g, mla_k_norm_g, nsa_q_norm_g, nsa_k_norm_g, cmp_pe_k, cmp_pe_v,
              cmp_k_w1, cmp_k_b1, cmp_k_w2, cmp_k_b2, cmp_v_w1, cmp_v_b1, cmp_v_w2, cmp_v_b2,
              w_proj_mla, w_proj_nsa, w_out, ffn_norm_g, w_ffn_gate, w_ffn_up, w_ffn_down):
    h = x
    for l in range(DEPTH):
        h = hybrid_layer(h, attn_norm_g[l], w_in[l], mla_q_lat_g[l], mla_kv_lat_g[l], mla_w_uq[l],
                         mla_w_uk[l], mla_w_uv[l], mla_q_norm_g[l], mla_k_norm_g[l], nsa_q_norm_g[l],
                         nsa_k_norm_g[l], cmp_pe_k[l], cmp_pe_v[l], cmp_k_w1[l], cmp_k_b1[l], cmp_k_w2[l],
                         cmp_k_b2[l], cmp_v_w1[l], cmp_v_b1[l], cmp_v_w2[l], cmp_v_b2[l], w_proj_mla[l],
                         w_proj_nsa[l], w_out[l], ffn_norm_g[l], w_ffn_gate[l], w_ffn_up[l], w_ffn_down[l])
    return h


_drawn_inputs = setup_inputs


def setup_inputs(seed=0):
    import zlib

    import numpy as np

    out = dict(_drawn_inputs(seed))
    spreads = {}
    factors = {'attn_norm_g': 8.0,
     'mla_q_lat_g': 8.0,
     'mla_kv_lat_g': 8.0,
     'mla_q_norm_g': 8.0,
     'mla_k_norm_g': 8.0,
     'nsa_q_norm_g': 8.0,
     'nsa_k_norm_g': 8.0,
     'cmp_pe_k': 8.0,
     'cmp_pe_v': 10.367,
     'cmp_k_b1': 34.562,
     'cmp_k_b2': 59.297,
     'cmp_v_b1': 64.0,
     'cmp_v_b2': 64.0,
     'ffn_norm_g': 29.253}
    for name, (base, spread) in spreads.items():
        noise = np.random.default_rng([zlib.crc32(name.encode()), seed]).standard_normal(out[name].shape)
        drawn = base * np.exp(spread * noise) if base else spread * noise
        out[name] = __import__('jax').numpy.asarray(drawn.astype(out[name].dtype))
    for name, factor in factors.items():
        out[name] = (out[name] * factor).astype(out[name].dtype)
    return out
```

```python
from contextlib import ExitStack, nullcontext

import concourse.bass as bass
from concourse import mybir

F32 = mybir.dt.float32
F32R = mybir.dt.float32r
BF16 = mybir.dt.bfloat16
ALU = mybir.AluOpType
ACT = mybir.ActivationFunctionType
AXX = mybir.AxisListType.X

P = 128
D = 2048
SEQ = 256
TT = SEQ // P
KD = D // P
EPS = 1e-6
HEADS, GROUPS = 16, 4
HPG = HEADS // GROUPS
DK, DV = 192, 128
RANK = 512
MLA_NOPE, MLA_ROT, NSA_ROT = 128, 64, 48
CMP_LEN, CMP_STRIDE = 32, 16
NCMP = (SEQ - CMP_LEN) // CMP_STRIDE + 1
CROWS = GROUPS * NCMP
HID_K, HID_V = 4 * DK, 4 * DV
HALF = DK // 2
D_FF = -(-8 * D // (3 * 256)) * 256
KF = D_FF // P
N = 512
NT = D // N
FT = D_FF // N
SCALE = DK ** -0.5
MASKED = -1e30
FLOOR = 1e28

O_KR = 2 * RANK
O_Q = O_KR + MLA_ROT
O_KC = O_Q + HEADS * DK
O_VC = O_KC + GROUPS * DK
O_KS = O_VC + GROUPS * DV
O_VS = O_KS + GROUPS * DK
O_KW = O_VS + GROUPS * DV
O_VW = O_KW + GROUPS * DK
O_GN = O_VW + GROUPS * DV
O_GM = O_GN + HEADS * 3
D_IN = O_GM + 2 * D

RING = 4
SLOT = 1024
AHEAD = 2
NCONST, NFIRST = 22, 5


class Step:
    def __init__(self, kind, kinds=(), bank=None, which=None, tile=None, pair=None, slot=None, job=None, lo=None, hi=None,
                 weight=None, col=None, lhs=None, chunk=None, m=None, width=None, rows=None, step=0, start=0,
                 first=False, last=False, off=None, w=None, c0=None, c1=None, h=None):
        self.kind, self.kinds, self.bank, self.which, self.tile, self.pair = kind, kinds, bank, which, tile, pair
        self.slot, self.job, self.lo, self.hi, self.h = slot, job, lo, hi, h
        self.weight, self.col, self.lhs, self.chunk, self.m, self.width, self.rows = weight, col, lhs, chunk, m, width, rows
        self.step, self.start, self.first, self.last = step, start, first, last
        self.off, self.w, self.c0, self.c1 = off, w, c0, c1
        self.base, self.per, self.ahead = {}, {}, None


class Phase:
    def __init__(self, steps, times=1):
        self.steps, self.times = steps, times


def number(phases):
    seen = {}
    for ph in phases:
        local = dict(seen)
        for s in ph.steps:
            s.base = dict(local)
            for k in s.kinds:
                local[k] = local.get(k, 0) + 1
        per = {k: local[k] - seen.get(k, 0) for k in local}
        for s in ph.steps:
            s.per = per if ph.times > 1 else {}
        for k in local:
            seen[k] = seen.get(k, 0) + per[k] * ph.times
    return phases


def walk(eng, phases):
    for ph in phases:
        with (eng.Fori(0, ph.times) if ph.times > 1 else nullcontext(0)) as i:
            for s in ph.steps:
                yield s, i


def count(s, i, kind, more=0):
    n, per = s.base.get(kind, 0) + more, s.per.get(kind, 0)
    return i * per + n if per else n


def wait(eng, sem, value):
    if isinstance(value, int) and value <= 0:
        return
    eng.wait_ge(sem, value)



def tile_units(out, weight, col, lhs, chunks, width, per_unit, rows=P, k0=0, **about):
    steps = []
    for c in range(0, chunks, per_unit):
        m = min(per_unit, chunks - c)
        steps.append(Step("unit", ("unit",), bank=out, weight=weight, col=col, lhs=lhs, chunk=k0 + c, m=m,
                          width=width, rows=rows, first=c == 0, last=c + m == chunks, **about))
    return steps


def weave(units, extras):
    steps = []
    for k, u in enumerate(units):
        steps.append(u)
        steps += extras.get(k, [])
    for k in sorted(extras):
        if k >= len(units):
            steps += extras[k]
    return steps


def done(bank, what, **about):
    return Step("done_" + what, ("tile" + bank,), bank=bank, **about)


def piece(which, lo, hi, part):
    kinds = {"a": ("norm_a",), "b": ("norm_b", "rope")}[part]
    return Step("norm_" + part, kinds, which=which, lo=lo, hi=hi)


def turn_head(which, slot):
    return Step("turn_head", ("fill",), which=which, slot=slot)


def jobs(which, njobs, at):
    extras = {}
    for k in range(njobs + 2):
        st = extras.setdefault(at[k], [])
        if 1 <= k <= njobs:
            st.append(Step("probs", ("probs",), which=which, job=k - 1))
        if k < njobs:
            st.append(Step("scores", ("scores",), which=which, job=k))
        if k >= 2:
            last = which == "mla" or (k - 2) % 2 == 1
            st.append(Step("values", ("values",) + ("head",) * last, which=which, job=k - 2, last=last))
        if 1 <= k <= njobs:
            st.append(Step("turn_probs", ("turn_probs",), which=which, job=k - 1))
    return extras


def merge_extras(*many):
    out = {}
    for e in many:
        for k, v in e.items():
            out.setdefault(k, []).extend(v)
    return out


def schedule():
    phases = [Phase([Step("setup", ("fill",))] +
                    [Step("turn_x", ("fill", "sfill"), pair=c, bank=c % 4) for c in range(KD // 2)])]

    b = tile_units("A", "w_in", O_KC, "x", KD, N, 2) + [done("A", "kv", off=0, w=N)]
    b += tile_units("B", "w_in", O_KC + N, "x", KD, N, 2) + [done("B", "kv", off=N, w=N)]
    b += tile_units("A", "w_in", O_KC + 2 * N, "x", KD, 256, 4) + [done("A", "kv", off=2 * N, w=256)]
    krg = tile_units("B", "kr_gates", 0, "x", KD, MLA_ROT + 3 * HEADS, 8)
    b += krg + [done("B", "krg")]
    cq = tile_units("A", "w_in", 0, "x", KD, N, 2)
    b += weave(cq, {0: [Step("turn_kc", ("fill",), slot=0)], 1: [Step("turn_kc", ("fill",), slot=1)],
                    2: [Step("turn_kc", ("fill",), slot=2), Step("turn_vc", ("fill",), slot=0)],
                    3: [Step("turn_vc", ("fill",), slot=1), Step("flat", ("flat",), which="v")], 4: [Step("turn_kc", ("fill",), slot=3)],
                    5: [Step("flat", ("flat",), which="k0")], 6: [Step("flat", ("flat",), which="k1")]})
    b += [done("A", "lat", which=0)]
    phases.append(Phase(b))

    fv = tile_units("B", "cmp_v_w1", 0, "fv", CMP_LEN, HID_V, 2)
    c = weave(fv, {2: [Step("lat_a", ("norm_a",), which=0)], 5: [Step("lat_b", ("norm_b",), which=0)],
                   8: [Step("turn_lat", ("fill", "sfill"), which=0, pair=0)], 10: [Step("turn_lat", ("fill", "sfill"), which=0, pair=1)],
                   12: [Step("load_b")]})
    fk = tile_units("A", "cmp_k_w1", 0, "fk", CMP_LEN * 2, HID_K, 1, rows=HALF)
    c += weave(fk, {0: [done("B", "hidden_v")],
                    20: [Step("turn_hidden", ("fill", "sfill"), c0=6, c1=10)]})
    ckv = tile_units("B", "w_in", RANK, "x", KD, N, 2)
    w2v = tile_units("A", "cmp_v_w2", 0, "hv", HID_V // P, DV, 4)
    w2k = tile_units("A", "cmp_k_w2", 0, "hk", HID_K // P, DK, 3)
    c += weave(ckv, {0: [done("A", "hidden_k")], 1: w2v + [done("A", "cmp_v")],
                     4: [Step("turn_hidden", ("fill", "sfill"), c0=0, c1=4)], 5: [Step("turn_hidden", ("fill", "sfill"), c0=4, c1=6)],
                     6: w2k + [done("A", "cmp_k")],
                     7: [done("B", "lat", which=1), Step("cmp_norm", ("cmp_norm",)), Step("lat_a", ("norm_a",), which=1),
                         Step("lat_b", ("norm_b",), which=1),
                         Step("turn_lat", ("fill", "sfill"), which=1, pair=0), Step("turn_lat", ("fill", "sfill"), which=1, pair=1),
                         Step("turn_cmp", ("fill",))]})
    phases.append(Phase(c))

    u = tile_units("A", "mla_w_uk", 0, "ckv", 4, N, 2, step=N)
    u += tile_units("B", "mla_w_uq", 0, "cq", 4, 2 * DK, 2, step=4 * DK)
    u += tile_units("A", "mla_w_uq", 2 * DK, "cq", 4, 2 * DK, 2, step=4 * DK)
    u += tile_units("B", "mla_w_uv", 0, "ckv", 4, N, 2, step=N)
    u += tile_units("A", "w_in", O_GM, "x", KD, N, 2, step=N)
    ex = {1: [done("A", "mla_k")],
          2: [piece("mla", 4, 8, "a")],
          3: [done("B", "mla_q", h=0)],
          4: [piece("mla", 4, 8, "b")],
          5: [done("A", "mla_q", h=2), piece("mla", 0, 2, "a")],
          7: [done("B", "mla_v"), piece("mla", 0, 2, "b"), piece("mla", 2, 4, "a")],
          8: [turn_head("mla", 4), piece("mla", 2, 4, "b")],
          9: [turn_head("mla", 0), turn_head("mla", 5)],
          10: [turn_head("mla", 1)],
          11: [turn_head("mla", 6), turn_head("mla", 2)],
          12: [turn_head("mla", 7)], 13: [turn_head("mla", 3)],
          16: [done("A", "gate_m")]}
    phases.append(Phase(weave(u, merge_extras(ex, jobs("mla", HPG, [10, 11, 12, 13, 14, 15]))), GROUPS))

    u = tile_units("A", "ks_kw", 0, "x", KD, 2 * DK, 2, step=DK)
    u += tile_units("B", "vs_vw", 0, "x", KD, 2 * DV, 4, step=DV)
    u += tile_units("A", "w_in", O_Q, "x", KD, 2 * DK, 2, step=4 * DK)
    u += tile_units("B", "w_in", O_Q + 2 * DK, "x", KD, 2 * DK, 2, step=4 * DK)
    u += tile_units("A", "w_proj_mla", 0, "om", KD, N, 2, step=N)
    ex = {7: [done("A", "nsa_k")],
          8: [piece("nsa", 4, 6, "a")],
          10: [piece("nsa", 4, 6, "b")],
          11: [done("B", "nsa_v")],
          16: [turn_head("nsa", 4)], 17: [turn_head("nsa", 5)],
          19: [done("A", "nsa_q", h=0), piece("nsa", 0, 2, "a")],
          21: [piece("nsa", 0, 2, "b")],
          25: [turn_head("nsa", 0)], 26: [turn_head("nsa", 1)],
          27: [done("B", "nsa_q", h=2), piece("nsa", 2, 4, "a")],
          28: [piece("nsa", 2, 4, "b")],
          30: [turn_head("nsa", 2)], 31: [turn_head("nsa", 3)],
          40: [done("A", "y_m")]}
    jb = jobs("nsa", 2 * HPG, [27, 28, 29, 30, 31, 32, 33, 34, 35, 35])
    phases.append(Phase(weave(u, merge_extras(ex, jb)), GROUPS))

    def merged(back):
        u = tile_units("A", "w_in", O_GM + D, "x", KD, N, 2, step=N, start=0 if not back else N)
        u += tile_units("B", "w_proj_nsa", 0, "on", KD, N, 2, step=N, start=0 if not back else N)
        ex = {7: [done("A", "gate_n")], 15: [Step("done_y_n", ("tileB", "merged"), bank="B", tile=back)]}
        if back:
            ex[1] = [Step("turn_merged", ("fill", "sfill"), pair=0)]
            ex[2] = [Step("turn_merged", ("fill", "sfill"), pair=1)]
        return weave(u, ex)
    phases.append(Phase([Step("load_x")] + merged(0)))
    phases.append(Phase(merged(1), NT - 1))

    g = []
    for n in range(NT):
        bank = "AB"[n % 2]
        what, t = ("turn_h", n - 1) if n else ("turn_merged", NT - 1)
        ex = {k + 1: [Step(what, ("fill", "sfill"), pair=k, tile=t)] for k in range(2)}
        g += weave(tile_units(bank, "w_out", n * N, "m", KD, N, 2), ex) + [done(bank, "h", tile=n)]
    phases.append(Phase(g))

    def ffn(back):
        u = tile_units("A", "w_ffn_gate", 0, "x", KD, N, 2, step=N, start=N if back else 0)
        u += tile_units("B", "w_ffn_up", 0, "x", KD, N, 2, step=N, start=N if back else 0)
        ex = {7: [Step("done_ff_gate", ("tileA", "ff"), bank="A")], 15: [done("B", "ff_up")]}
        if back:
            ex[1] = [Step("turn_ff", ("fill", "sfill"), pair=0)]
            ex[2] = [Step("turn_ff", ("fill", "sfill"), pair=1)]
        else:
            ex[1] = [Step("turn_h", ("fill", "sfill"), pair=0, tile=NT - 1)]
            ex[2] = [Step("turn_h", ("fill", "sfill"), pair=1, tile=NT - 1), Step("h_norm")]
        return weave(u, ex)
    phases.append(Phase(ffn(0)))
    phases.append(Phase(ffn(1), FT - 1))
    d = []
    for n in range(NT):
        bank = "AB"[n % 2]
        u = tile_units(bank, "w_ffn_down", n * N, "ff", KF, N, 2)
        ex = {2: [Step("turn_ff", ("fill", "sfill"), pair=0, tile=FT - 1)], 3: [Step("turn_ff", ("fill", "sfill"), pair=1, tile=FT - 1)]} if n == 0 else {}
        d += weave(u, ex) + [done(bank, "down", tile=n)]
    phases.append(Phase(d))
    return number(phases)


def build(nc, A, out):
    PH = schedule()
    with ExitStack() as ctx:
        def sem(name):
            return ctx.enter_context(nc.semaphore(name))

        base = [nc.sbuf_base]

        def at(name, shape, dt, off):
            off = (off + 31) // 32 * 32
            n = 2 if dt == BF16 else 4
            for s in shape[1:]:
                n *= s
            base[0] = off + n
            return nc.alloc_sbuf_tensor_at(name, list(shape), dt, offset=off)

        def sb(name, shape, dt=F32):
            return at(name, shape, dt, base[0])

        raw = sb("raw", [P, RING, SLOT])
        whi = sb("whi", [P, RING, SLOT], F32R)
        wlo = sb("wlo", [P, RING, SLOT], F32R)
        xT_hi = sb("xT_hi", [P, KD, SEQ], F32R)
        xT_lo = sb("xT_lo", [P, KD, SEQ], F32R)
        PB_OFF = base[0]
        Pbs = sb("probs", [P, 2, N])
        pT = sb("pT", [P, N])
        rot = sb("rot", [P, 4, 256])
        ident = sb("ident", [P, P])
        identb = sb("identb", [P, P], BF16)
        maskb = sb("maskb", [P, P], BF16)
        cmaskb = sb("cmaskb", [P, TT, GROUPS, CROWS], BF16)
        cos_m = sb("cos_m", [P, TT, MLA_ROT // 2])
        sin_m = sb("sin_m", [P, TT, MLA_ROT // 2])
        cos_n = sb("cos_n", [P, TT, NSA_ROT // 2])
        sin_n = sb("sin_n", [P, TT, NSA_ROT // 2])
        cos_c = sb("cos_c", [CROWS, NSA_ROT // 2])
        sin_c = sb("sin_c", [CROWS, NSA_ROT // 2])
        g_head = sb("g_head", [P, 6, DK])
        gcols = sb("gcols", [P, 2 * KD])
        peT_k = sb("peT_k", [HALF, 2, CMP_LEN])
        peT_v = sb("peT_v", [P, CMP_LEN])
        kr = sb("kr", [P, TT, MLA_ROT])
        gates = sb("gates", [P, HEADS, 2, 3])
        kcT = sb("kcT_cmp", [HALF, 2, CROWS])
        v_c = sb("v_c", [CROWS, DV])
        junk = sb("junk", [P, DK])
        small = sb("small", [P, 192])
        FIXED = base[0]
        KB = 1024

        def over(name, shape, dt, kb):
            return at(name, shape, dt, FIXED + int(kb * KB))

        latT = [[over(f"lat{w}_{p}", [P, 4, SEQ], F32R, 4 * (2 * w + k)) for k, p in enumerate(("hi", "lo"))] for w in range(2)]
        x_sb = over("x_sb", [P, TT, D], F32, 16)
        rows_sb = over("rows_sb", [2 * KD, P], F32, 32)
        pe_k_sb = over("pe_k_sb", [CMP_LEN, DK], F32, 32.5)
        pe_v_sb = over("pe_v_sb", [CMP_LEN, DV], F32, 33.25)
        fk = [over(f"fk_{p}", [HALF, 2 * CMP_LEN, CROWS], F32R, 16 + 15 * k) for k, p in enumerate(("hi", "lo"))]
        fv = [over(f"fv_{p}", [P, CMP_LEN, CROWS], F32R, 46 + 7.5 * k) for k, p in enumerate(("hi", "lo"))]
        lat = over("lat", [P, TT, 2, RANK], F32, 61)
        kv = over("kv", [P, TT, 1280], F32, 69)
        kc_turned = over("kc_turned", [HALF, GROUPS, 2, SEQ], F32, 79)
        vc_turned = over("vc_turned", [P, GROUPS, SEQ], F32, 87)
        flat = over("flat", [P, CMP_LEN, CROWS], F32, 91)
        g_lat = over("g_lat", [P, 2, RANK], F32, 98.5)
        hid = over("hid", [CROWS, HID_K + HID_V], F32, 69)
        hid_a = over("hid_a", [CROWS, HID_K + HID_V], F32, 74)
        b1 = over("b1", [CROWS, HID_K + HID_V], F32, 79)
        hT = [over(f"hT_{p}", [P, 10, CROWS], F32R, 84 + 2.5 * k) for k, p in enumerate(("hi", "lo"))]
        kc = over("kc", [CROWS, DK], F32, 89)
        b2 = over("b2", [CROWS, DK + DV], F32, 90)
        M = over("M", [P, TT, D], F32, 16)
        om = [over(f"om_{p}", [P, HEADS, SEQ], F32R, 32 + 16 * k) for k, p in enumerate(("hi", "lo"))]
        qk_m = over("qk_m", [P, TT, 8, DK], F32, 64)
        qkT_m = over("qkT_m", [HALF, 8, 2 * SEQ], F32, 76)
        v_m = over("v_m", [P, TT, HPG, DV], F32, 92)
        on = [over(f"on_{p}", [P, HEADS, SEQ], F32R, 64 + 16 * k) for k, p in enumerate(("hi", "lo"))]
        qkT_n = over("qkT_n", [HALF, 6, 2 * SEQ], F32, 0)
        v_n = over("v_n", [P, TT, 2, DV], F32, 12)
        qk_n = over("qk_n", [P, TT, 6, DK], F32, 96)
        mT = [over(f"mT_{p}", [P, KD, SEQ], F32R, 32 + 16 * k) for k, p in enumerate(("hi", "lo"))]
        mt = over("mt", [P, TT, N], F32, 96)
        h = over("h", [P, TT, D], F32, 0)
        fT = [over(f"fT_{p}", [P, KF, SEQ], F32R, 16 + 44 * k) for k, p in enumerate(("hi", "lo"))]
        ft = at("ft", [P, TT, N], F32, PB_OFF)
        assert FIXED + 105 * KB <= nc.sbuf_usable_end

        ps = [ctx.enter_context(nc.psum_tensor(f"ps{b}", [P, 512], F32)) for b in range(8)]
        BANK = {"A": (ps[0], ps[1]), "B": (ps[2], ps[3])}
        S, TP, OP, QT = ps[4], ps[5], ps[6], ps[7]

        rx, hrx, msx = small[:, 0:2], small[:, 2:4], small[:, 4:6]
        ms, rs = small[:, 8:24], small[:, 24:40]
        mhalf = small[:, 40:56]
        mx, nm, sm, rc = small[:, 56:59], small[:, 59:62], small[:, 62:65], small[:, 65:68]
        hss, rh, rh2 = small[:, 72:80], small[:, 80:82], small[:, 82:84]
        gsig = small[:, 88:88 + 96]
        msh = small[:, 84:86]
        hs2 = small[:, 86:88]

        const = sem("const")
        const0 = sem("const0")
        bias_in = sem("bias_in")
        x_in = [sem(f"x_in{q}") for q in range(NT)]
        xt_in = sem("xt_in")
        ready = sem("ready")
        loaded = [sem(f"loaded{k}") for k in range(RING)]
        hi_made, split, used = sem("hi_made"), sem("split"), sem("used")
        free = {"A": sem("freeA"), "B": sem("freeB")}
        filled, fill_hi, fill_out = sem("filled"), sem("fill_hi"), sem("fill_out")
        ms_ready, rstd_ready, scaled, roped = sem("ms_ready"), sem("rstd_ready"), sem("scaled"), sem("roped")
        x_rstd = sem("x_rstd")
        ms_x = sem("ms_x")
        flat_made, flat_hi, flat_out = sem("flat_made"), sem("flat_hi"), sem("flat_out")
        scored, negmax, exped, probs = sem("scored"), sem("negmax"), sem("exped"), sem("probs_ready")
        turned, pt_out, valued, o_hi, o_free = sem("turned"), sem("pt_out"), sem("valued"), sem("o_hi"), sem("o_free")
        act_tmp, dve_tmp = {}, {}
        acted = {k: sem("acted_" + k) for k in ("hidden_k", "hidden_v", "gate_m", "gate_n", "ff", "krg")}
        made = {k: sem("made_" + k) for k in ("hidden_k", "hidden_v", "cmp_k", "cmp_v", "merged", "h", "ff", "gates", "arg_k", "arg_v")}
        cmp_normed = sem("cmp_normed")
        h_rstd = sem("h_rstd")
        h_ms, h_pow, cmp_rstd = sem("h_ms"), sem("h_pow"), sem("cmp_rstd")
        out_ready, stored = sem("out_ready"), sem("stored")

        block = ctx.enter_context(nc.Block())

        LHS = {"x": (xT_hi, xT_lo), "cq": latT[0], "ckv": latT[1], "fk": fk, "fv": fv, "om": om, "on": on, "m": mT, "ff": fT}

        def lhsT(u, part, c, t):
            if u.lhs == "hk":
                return hT[part][:, c, :]
            if u.lhs == "hv":
                return hT[part][:, HID_K // P + c, :]
            if u.lhs in ("fk", "fv"):
                return LHS[u.lhs][part][:, c, :]
            return LHS[u.lhs][part][:, c, t * P:(t + 1) * P]

        def pieces(u, i, k):
            r0, r1 = u.chunk * u.rows, (u.chunk + u.m) * u.rows
            step = u.step
            dst = raw[0:u.rows, k, 0:u.m * u.width].rearrange("p (c n) -> p c n", c=u.m)

            def src(name, col, width):
                w = A[name][r0:r1]
                w = w[:, bass.ds(i * step + col, width)] if step else w[:, col:col + width]
                return w.rearrange("(c p) n -> p c n", p=u.rows)

            if u.weight == "kr_gates":
                g = HEADS * 3
                return [(dst[:, :, 0:MLA_ROT], src("w_in", O_KR, MLA_ROT)),
                        (dst[:, :, MLA_ROT:], src("w_in", O_GN, g))]
            if u.weight in ("ks_kw", "vs_vw"):
                s0, w0 = (O_KS, O_KW) if u.weight == "ks_kw" else (O_VS, O_VW)
                n = u.width // 2
                return [(dst[:, :, 0:n], src("w_in", s0, n)), (dst[:, :, n:], src("w_in", w0, n))]
            c0 = u.col + u.start
            if u.m % 2:
                n = u.width // 2
                return [(dst[:, :, 0:n], src(u.weight, c0, n)), (dst[:, :, n:], src(u.weight, c0 + n, n))]
            w, n = src(u.weight, c0, u.width), u.m // 2
            return [(dst[:, 0:n, :], w[:, 0:n, :]), (dst[:, n:, :], w[:, n:, :])]

        def slot_of(s, more=0):
            assert s.per.get("unit", 0) % RING == 0
            return (s.base.get("unit", 0) + more) % RING

        def halves(u):
            b = BANK[u.bank]
            if u.lhs == "fk":
                return [(0, 0, 512, b[0]), (0, 512, HID_K, b[1])]
            if u.lhs in ("fv", "hk", "hv"):
                return [(0, 0, u.width, b[0])]
            return [(t, 0, u.width, b[t]) for t in range(TT)]

        @block.sync
        def _(sp):
            for q in range(NT):
                sp.dma_start(x_sb[:, :, q * N:(q + 1) * N], A["x"].rearrange("(t p) n -> p t n", p=P)[:, :, q * N:(q + 1) * N]).then_inc(x_in[q], 16)
            for u, i in walk(sp, PH):
                if u.kind != "unit":
                    continue
                k = slot_of(u)
                wait(sp, split, count(u, i, "unit", 1 - RING))
                for dst, src in pieces(u, i, k):
                    sp.dma_start(dst, src).then_inc(loaded[k], 16)

        for n, ph in enumerate(PH):
            us = [s for s in ph.steps if s.kind == "unit"]
            nxt = []
            for q in PH[n + 1:]:
                nxt += [s for s in q.steps if s.kind == "unit"]
                if len(nxt) >= AHEAD:
                    break
            for j, s in enumerate(us):
                if j + AHEAD < len(us):
                    t = us[j + AHEAD]
                    s.ahead = (t.rows, t.m * t.width)
                elif ph.times > 1:
                    s.ahead = (P, SLOT)
                elif j + AHEAD - len(us) < len(nxt):
                    t = nxt[j + AHEAD - len(us)]
                    s.ahead = (t.rows, t.m * t.width)
                else:
                    s.ahead = None

        def load_count(s, i, more):
            n = s.base.get("unit", 0) + more
            per = s.per.get("unit", 0)
            v = 32 * (n // RING + 1)
            return i * (32 * per // RING) + v if per else v

        def split_hi(act, s, i, more, rows, n):
            k = slot_of(s, more)
            act.wait_ge(loaded[k], load_count(s, i, more))
            wait(act, used, count(s, i, "unit", more + 1 - RING))
            nc.scalar.activation(whi[0:rows, k, 0:n], raw[0:rows, k, 0:n], ACT.Copy).then_inc(hi_made, 1)

        def split_lo(dve, s, i, more, rows, n):
            k = slot_of(s, more)
            wait(dve, hi_made, count(s, i, "unit", more + 1))
            nc.vector.tensor_tensor(wlo[0:rows, k, 0:n], raw[0:rows, k, 0:n], whi[0:rows, k, 0:n].bitcast(F32),
                                    ALU.subtract).then_inc(split, 1)

        FB = [QT, TP, S, OP]
        PAIRED = ("turn_merged", "turn_h", "turn_ff")

        def head_view(which):
            return (qk_m, qkT_m, cos_m, sin_m, MLA_NOPE, MLA_ROT // 2) if which == "mla" else (qk_n, qkT_n, cos_n, sin_n, 0, NSA_ROT // 2)

        @block.scalar
        def _(act):
            consts = (
                (rows_sb[0:KD, :], A["attn_norm_g"].rearrange("(c p) -> c p", p=P)),
                (rows_sb[KD:2 * KD, :], A["ffn_norm_g"].rearrange("(c p) -> c p", p=P)),
                (pe_k_sb[:], A["cmp_pe_k"]), (pe_v_sb[:], A["cmp_pe_v"]), (ident[:], A["ident"]),
                (identb[:], A["identb"]), (maskb[:], A["maskb"]),
                (cmaskb[:], A["cmaskb"].rearrange("(t p) g c -> p t g c", p=P)),
                (cos_m[:], A["cos_m"].rearrange("(t p) c -> p t c", p=P)), (sin_m[:], A["sin_m"].rearrange("(t p) c -> p t c", p=P)),
                (cos_n[:], A["cos_n"].rearrange("(t p) c -> p t c", p=P)), (sin_n[:], A["sin_n"].rearrange("(t p) c -> p t c", p=P)),
                (cos_c[:], A["cos_c"]), (sin_c[:], A["sin_c"]),
                (g_head[:, 0, :], A["mla_q_norm_g"].partition_broadcast(P)), (g_head[:, 1, :], A["mla_k_norm_g"].partition_broadcast(P)),
                (g_head[:, 2, :], A["nsa_q_norm_g"].partition_broadcast(P)),
                (g_head[:, 3, :], A["nsa_k_norm_g"][0].partition_broadcast(P)),
                (g_head[:, 4, :], A["nsa_k_norm_g"][1].partition_broadcast(P)),
                (g_head[:, 5, :], A["nsa_k_norm_g"][2].partition_broadcast(P)),
                (g_lat[:, 0, :], A["mla_q_lat_g"].partition_broadcast(P)), (g_lat[:, 1, :], A["mla_kv_lat_g"].partition_broadcast(P)),
            )
            assert len(consts) == NCONST
            for n, (dst, src) in enumerate(consts):
                act.dma_start(dst, src).then_inc(const0 if n < NFIRST else const, 16)

            def copy(dst, src, **kw):
                return nc.scalar.activation(dst, src, ACT.Copy, **kw)

            def turn_split(s, i, src, hi, gain=None):
                wait(act, filled, count(s, i, "fill", 1))
                for c in range(src.shape[1]):
                    kw = {"scale": gain[:, c:c + 1]} if gain is not None else {}
                    ins = copy(hi[:, c, :], src[:, c, :], **kw)
                ins.then_inc(fill_hi, 1)

            first = True
            for s, i in walk(act, PH):
                k = s.kind
                if k == "unit":
                    if first:
                        for m in range(AHEAD):
                            split_hi(act, s, i, m, P, SLOT)
                        first = False
                    if s.ahead:
                        split_hi(act, s, i, AHEAD, *s.ahead)
                elif k == "turn_x":
                    f = FB[s.bank][:, :].rearrange("p (c n) -> p c n", c=2)
                    act.wait_ge(fill_out, 1)
                    turn_split(s, i, f, xT_hi[:, 2 * s.pair:2 * s.pair + 2, :], gcols[:, 2 * s.pair:2 * s.pair + 2])
                elif k == "done_kv":
                    act.wait_ge(x_rstd, 1)
                    act.wait_ge(used, count(s, i, "unit"))
                    for t in range(TT):
                        ins = copy(kv[:, t, s.off:s.off + s.w], BANK[s.bank][t][:, 0:s.w], scale=rx[:, t:t + 1])
                    ins.then_inc(free[s.bank], 1)
                elif k == "done_krg":
                    act.wait_ge(used, count(s, i, "unit"))
                    for t in range(TT):
                        copy(kr[:, t, :], BANK[s.bank][t][:, 0:MLA_ROT], scale=rx[:, t:t + 1])
                        ins = nc.scalar.activation(gsig[:, t * 48:t * 48 + 48], BANK[s.bank][t][:, MLA_ROT:MLA_ROT + 48],
                                                   ACT.Tanh, scale=hrx[:, t:t + 1])
                    ins.then_inc(free[s.bank], 1)
                elif k == "done_lat":
                    act.wait_ge(used, count(s, i, "unit"))
                    for t in range(TT):
                        ins = copy(lat[:, t, s.which, :], BANK[s.bank][t][:, :], scale=rx[:, t:t + 1])
                    ins.then_inc(free[s.bank], 1)
                elif k == "turn_kc":
                    wait(act, filled, count(s, i, "fill", 1))
                    copy(kc_turned[:, s.slot, :, :].rearrange("p c n -> p (c n)"), QT[0:HALF, :]).then_inc(fill_out, 1)
                elif k == "turn_vc":
                    wait(act, filled, count(s, i, "fill", 1))
                    copy(vc_turned[:, 2 * s.slot:2 * s.slot + 2, :].rearrange("p c n -> p (c n)"), QT[:, :]).then_inc(fill_out, 1)
                elif k == "flat":
                    act.wait_ge(flat_made, count(s, i, "flat", 1))
                    if s.which == "v":
                        copy(fv[0][:], flat[:]).then_inc(flat_hi, 1)
                    else:
                        c = int(s.which[1])
                        copy(fk[0][:, c::2, :], flat[0:HALF]).then_inc(flat_hi, 1)
                elif k == "turn_lat":
                    turn_split(s, i, QT[:, :].rearrange("p (c n) -> p c n", c=2), latT[s.which][0][:, 2 * s.pair:2 * s.pair + 2, :])
                elif k in ("done_hidden_k", "done_hidden_v"):
                    kk = k[-1]
                    cols = slice(0, HID_K) if kk == "k" else slice(HID_K, HID_K + HID_V)
                    act.wait_ge(made["arg_" + kk], 1)
                    nc.scalar.activation(hid_a[:, cols], hid_a[:, cols], ACT.Tanh,
                                         scale=0.7978845608028654).then_inc(acted["hidden_" + kk], 1)
                elif k == "turn_hidden":
                    wait(act, filled, count(s, i, "fill", 1))
                    n = s.c1 - s.c0
                    copy(hT[0][:, s.c0:s.c1, :], QT[:, 0:n * CROWS].rearrange("p (c n) -> p c n", c=n)).then_inc(fill_hi, 1)
                elif k == "turn_cmp":
                    wait(act, filled, count(s, i, "fill", 1))
                    copy(kcT[:], QT[0:HALF, 0:2 * CROWS].rearrange("p (c n) -> p c n", c=2)).then_inc(fill_out, 1)
                elif k == "done_mla_k":
                    act.wait_ge(used, count(s, i, "unit"))
                    for t in range(TT):
                        ins = copy(qk_m[:, t, 4:8, 0:MLA_NOPE], BANK[s.bank][t][:, :].rearrange("p (h n) -> p h n", h=HPG))
                    ins.then_inc(free[s.bank], 1)
                elif k == "done_mla_q":
                    act.wait_ge(used, count(s, i, "unit"))
                    for t in range(TT):
                        ins = copy(qk_m[:, t, s.h:s.h + 2, :], BANK[s.bank][t][:, 0:2 * DK].rearrange("p (h n) -> p h n", h=2))
                    ins.then_inc(free[s.bank], 1)
                elif k == "done_mla_v":
                    act.wait_ge(used, count(s, i, "unit"))
                    for t in range(TT):
                        ins = copy(v_m[:, t, :, :], BANK[s.bank][t][:, :].rearrange("p (h n) -> p h n", h=HPG))
                    ins.then_inc(free[s.bank], 1)
                elif k in ("done_nsa_k", "done_nsa_q"):
                    act.wait_ge(used, count(s, i, "unit"))
                    h0 = 4 if k == "done_nsa_k" else s.h
                    for t in range(TT):
                        ins = copy(qk_n[:, t, h0:h0 + 2, :], BANK[s.bank][t][:, 0:2 * DK].rearrange("p (h n) -> p h n", h=2),
                                   scale=rx[:, t:t + 1])
                    ins.then_inc(free[s.bank], 1)
                elif k == "done_nsa_v":
                    act.wait_ge(used, count(s, i, "unit"))
                    for t in range(TT):
                        ins = copy(v_n[:, t, :, :], BANK[s.bank][t][:, 0:2 * DV].rearrange("p (h n) -> p h n", h=2),
                                   scale=rx[:, t:t + 1])
                    ins.then_inc(free[s.bank], 1)
                elif k == "done_gate_m":
                    act.wait_ge(used, count(s, i, "unit"))
                    for t in range(TT):
                        ins = nc.scalar.activation(M[:, t, bass.ds(i * N, N)], BANK[s.bank][t][:, :], ACT.Tanh, scale=hrx[:, t:t + 1])
                    ins.then_inc(free[s.bank], 1)
                elif k == "done_gate_n":
                    act.wait_ge(used, count(s, i, "unit"))
                    for t in range(TT):
                        ins = nc.scalar.activation(mt[:, t, :], BANK[s.bank][t][:, :], ACT.Tanh, scale=hrx[:, t:t + 1])
                    ins.then_inc(free[s.bank], 1)
                elif k == "turn_head":
                    if s.slot % 2 == 0:
                        wait(act, filled, count(s, i, "fill", 1))
                        copy(head_view(s.which)[1][:, s.slot, :], QT[0:HALF, :]).then_inc(fill_out, 1)
                elif k == "scores":
                    Pb = Pbs[:, s.job % 2, :]
                    act.wait_ge(negmax, count(s, i, "scores", 1))
                    nc.scalar.activation(Pb[:, 0:P], S[:, 0:P], ACT.Exp, bias=nm[:, 0:1], scale=SCALE, accum_out=sm[:, 0:1])
                    ins = nc.scalar.activation(Pb[:, P:3 * P], S[:, P:3 * P], ACT.Exp, bias=nm[:, 1:2], scale=SCALE, accum_out=sm[:, 1:2])
                    if s.which == "nsa":
                        ins = nc.scalar.activation(Pb[:, 3 * P:3 * P + CROWS], S[:, 3 * P:3 * P + CROWS], ACT.Exp, bias=nm[:, 2:3],
                                                   scale=SCALE, accum_out=sm[:, 2:3])
                    ins.then_inc(exped, 1)
                elif k == "turn_probs":
                    act.wait_ge(turned, count(s, i, "turn_probs", 1))
                    if s.which == "mla":
                        copy(pT[:, 0:3 * P], TP[:, 0:3 * P]).then_inc(pt_out, 1)
                    else:
                        copy(pT[:, 0:3 * P], TP[:, 0:3 * P])
                        copy(pT[0:CROWS, 3 * P:4 * P], TP[0:CROWS, 3 * P:4 * P]).then_inc(pt_out, 1)
                elif k == "values":
                    if s.last:
                        act.wait_ge(valued, count(s, i, "values", 1))
                        r = s.job if s.which == "mla" else s.job // 2
                        o = (om if s.which == "mla" else on)[0]
                        copy(o[:, bass.ds(i * HPG + r, 1), :].rearrange("p a n -> p (a n)"), OP[:, 0:SEQ]).then_inc(o_hi, 1)
                elif k == "turn_merged":
                    hi = mT[0]
                    c0 = (i * 4 if s.tile is None else s.tile * 4) + 2 * s.pair
                    turn_split(s, i, FB[s.pair][:, :].rearrange("p (c n) -> p c n", c=2), hi[:, bass.ds(c0, 2), :])
                elif k == "turn_h":
                    c0 = s.tile * 4 + 2 * s.pair
                    turn_split(s, i, FB[s.pair][:, :].rearrange("p (c n) -> p c n", c=2), xT_hi[:, c0:c0 + 2, :], gcols[:, KD + c0:KD + c0 + 2])
                elif k == "turn_ff":
                    c0 = (i * 4 if s.tile is None else s.tile * 4) + 2 * s.pair
                    turn_split(s, i, FB[s.pair][:, :].rearrange("p (c n) -> p c n", c=2), fT[0][:, bass.ds(c0, 2), :])
                elif k == "done_ff_gate":
                    act.wait_ge(h_rstd, 1)
                    act.wait_ge(used, count(s, i, "unit"))
                    act.wait_ge(filled, count(s, i, "fill"))
                    for t in range(TT):
                        ins = nc.scalar.activation(ft[:, t, :], BANK["A"][t][:, :], ACT.Tanh, scale=rh2[:, t:t + 1])
                    ins.then_inc(acted["ff"], 1)
                elif k == "load_b":
                    act.wait_ge(flat_out, 3)
                    for dst, src in ((b1[:, 0:HID_K], A["cmp_k_b1"]), (b1[:, HID_K:], A["cmp_v_b1"]),
                                     (b2[:, 0:DK], A["cmp_k_b2"]), (b2[:, DK:], A["cmp_v_b2"])):
                        act.dma_start(dst, src.partition_broadcast(CROWS)).then_inc(bias_in, 16)
                elif k == "load_x":
                    act.wait_ge(valued, count(s, i, "values"))
                    act.dma_start(h[:], A["x"].rearrange("(t p) n -> p t n", p=P)).then_inc(xt_in, 16)
                elif k == "done_down":
                    act.wait_ge(free[s.bank], count(s, i, "tile" + s.bank, 1))
                    cols = slice(s.tile * N, (s.tile + 1) * N)
                    act.dma_start(out.rearrange("(t p) n -> p t n", p=P)[:, :, cols], h[:, :, cols]).then_inc(stored, 16)
            act.wait_ge(stored, 16 * NT)

        @block.vector
        def _(dve):
            def fence():
                nc.vector.drain()

            def turn_split(s, i, src, hi, lo, gain=None):
                wait(dve, fill_hi, count(s, i, "sfill", 1))
                for c in range(src.shape[1]):
                    if gain is None:
                        ins = nc.vector.tensor_tensor(lo[:, c, :], src[:, c, :], hi[:, c, :].bitcast(F32), ALU.subtract)
                    else:
                        ins = nc.vector.scalar_tensor_tensor(out=lo[:, c, :], in0=src[:, c, :], scalar=gain[:, c:c + 1],
                                                             in1=hi[:, c, :].bitcast(F32), op0=ALU.mult, op1=ALU.subtract)
                ins.then_inc(fill_out, 1)

            def square_sum(x, acc, j=None):
                j = junk[0:x.shape[0], 0:x.shape[1]] if j is None else j
                nc.vector.tensor_tensor_reduce(j, x, x, 1.0, 0.0, ALU.mult, ALU.add, acc)
                fence()

            nc.vector.memset(junk[:, 0:8], 0.0).then_inc(o_free, 1)
            fence()
            for q in range(NT):
                dve.wait_ge(x_in[q], 16)
                for t in range(TT):
                    square_sum(x_sb[:, t, q * N:(q + 1) * N], hss[:, t * NT + q:t * NT + q + 1], rot[:, 0:2, :].rearrange("p a n -> p (a n)"))
            nc.vector.tensor_reduce(msx, hss.rearrange("p (t n) -> p t n", t=TT), AXX, ALU.add)
            fence()
            nc.vector.tensor_scalar(msx, msx, 1.0 / D, EPS, ALU.mult, ALU.add).then_inc(ms_x, 1)
            first = True
            for s, i in walk(dve, PH):
                k = s.kind
                if k == "unit":
                    if first:
                        for m in range(AHEAD):
                            split_lo(dve, s, i, m, P, SLOT)
                        first = False
                    if s.ahead:
                        split_lo(dve, s, i, AHEAD, *s.ahead)
                elif k == "setup":
                    dve.wait_ge(filled, 1)
                    nc.vector.tensor_copy(gcols[:], QT[:, 0:2 * KD])
                    nc.vector.tensor_copy(peT_k[:], QT[0:HALF, 32:96].rearrange("p (c n) -> p c n", c=2))
                    nc.vector.tensor_copy(peT_v[:], QT[:, 96:128]).then_inc(fill_out, 1)
                elif k == "turn_x":
                    f = FB[s.bank][:, :].rearrange("p (c n) -> p c n", c=2)
                    c0 = 2 * s.pair
                    turn_split(s, i, f, xT_hi[:, c0:c0 + 2, :], xT_lo[:, c0:c0 + 2, :], gcols[:, c0:c0 + 2])
                    if s.pair == KD // 2 - 1:
                        dve.wait_ge(x_rstd, 1)
                        nc.vector.tensor_scalar(hrx, rx, 0.5, None, ALU.mult)
                        fence()
                elif k == "done_krg":
                    dve.wait_ge(free[s.bank], count(s, i, "tile" + s.bank, 1))
                    nc.vector.tensor_scalar(gsig, gsig, 0.5, 0.5, ALU.mult, ALU.add)
                    fence()
                    gv = gsig.rearrange("p (t h b) -> p t h b", t=TT, b=3)
                    for j in range(2):
                        for t in range(TT):
                            nc.vector.tensor_copy(gates[:, :, j, t:t + 1], gv[:, t, :, 1 + j:2 + j])
                        nc.vector.tensor_copy(gates[:, :, j, 2:3], gv[:, j, :, 0:1])
                elif k == "flat":
                    dve.wait_ge(fill_out, count(s, i, "fill"))
                    wait(dve, flat_out, count(s, i, "flat"))
                    n = P if s.which == "v" else HALF
                    if s.which == "v":
                        src, pe = vc_turned, peT_v[:, :]
                    else:
                        c = int(s.which[1])
                        src, pe = kc_turned[:, :, c, :], peT_k[:, c, :]
                    for half in range(2):
                        a = src[:, :, half * CMP_STRIDE:half * CMP_STRIDE + NCMP * CMP_STRIDE].rearrange("p g (b l) -> p l g b", l=CMP_STRIDE)
                        l0 = half * CMP_STRIDE
                        ins = nc.vector.tensor_tensor(flat[0:n, l0:l0 + CMP_STRIDE, :].rearrange("p l (g b) -> p l g b", g=GROUPS), a,
                                                      pe[:, l0:l0 + CMP_STRIDE].unsqueeze(2).unsqueeze(3).to_broadcast([n, CMP_STRIDE, GROUPS, NCMP]),
                                                      ALU.add)
                    ins.then_inc(flat_made, 1)
                    dve.wait_ge(flat_hi, count(s, i, "flat", 1))
                    if s.which == "v":
                        hi, lo = fv[0][:], fv[1][:]
                    else:
                        hi, lo = fk[0][:, c::2, :], fk[1][:, c::2, :]
                    nc.vector.tensor_tensor(lo, flat[0:n], hi.bitcast(F32), ALU.subtract).then_inc(flat_out, 1)
                elif k == "lat_a":
                    b = "AB"[s.which]
                    dve.wait_ge(free[b], count(s, i, "tile" + b))
                    for t in range(TT):
                        square_sum(lat[:, t, s.which, :], ms[:, t:t + 1], rot[:, 0:2, :].rearrange("p a n -> p (a n)"))
                    nc.vector.tensor_scalar(ms[:, 0:2], ms[:, 0:2], 1.0 / RANK, EPS, ALU.mult, ALU.add).then_inc(ms_ready, 1)
                elif k == "lat_b":
                    dve.wait_ge(rstd_ready, count(s, i, "norm_a"))
                    if s.which == 0:
                        dve.wait_ge(const, 16 * (NCONST - NFIRST))
                    for t in range(TT):
                        ins = nc.vector.scalar_tensor_tensor(out=lat[:, t, s.which, :], in0=lat[:, t, s.which, :], scalar=rs[:, t:t + 1],
                                                             in1=g_lat[:, s.which, :], op0=ALU.mult, op1=ALU.mult)
                    ins.then_inc(scaled, 1)
                elif k == "turn_lat":
                    p2 = slice(2 * s.pair, 2 * s.pair + 2)
                    turn_split(s, i, QT[:, :].rearrange("p (c n) -> p c n", c=2), latT[s.which][0][:, p2, :], latT[s.which][1][:, p2, :])
                elif k in ("done_hidden_k", "done_hidden_v"):
                    kk = k[-1]
                    c0, n = (0, HID_K) if kk == "k" else (HID_K, HID_V)
                    x, a = hid[:, c0:c0 + n], hid_a[:, c0:c0 + n]
                    dve.wait_ge(used, count(s, i, "unit"))
                    dve.wait_ge(bias_in, 64)
                    for b, o in enumerate(range(0, n, 512)):
                        w = min(512, n - o)
                        ins = nc.vector.tensor_tensor(hid[:, c0 + o:c0 + o + w], BANK[s.bank][b][0:CROWS, 0:w], b1[:, c0 + o:c0 + o + w], ALU.add)
                    ins.then_inc(free[s.bank], 1)
                    fence()
                    nc.vector.tensor_tensor(a, x, x, ALU.mult)
                    fence()
                    nc.vector.tensor_scalar(a, a, 0.044715, 1.0, ALU.mult, ALU.add)
                    fence()
                    nc.vector.tensor_tensor(a, a, x, ALU.mult).then_inc(made["arg_" + kk], 1)
                    dve.wait_ge(acted["hidden_" + kk], 1)
                    nc.vector.tensor_scalar(a, a, 0.5, 0.5, ALU.mult, ALU.add)
                    fence()
                    nc.vector.tensor_tensor(x, a, x, ALU.mult).then_inc(made["hidden_" + kk], 1)
                    fence()
                elif k == "turn_hidden":
                    n = s.c1 - s.c0
                    wait(dve, fill_hi, count(s, i, "sfill", 1))
                    nc.vector.tensor_tensor(hT[1][:, s.c0:s.c1, :], QT[:, 0:n * CROWS].rearrange("p (c n) -> p c n", c=n),
                                            hT[0][:, s.c0:s.c1, :].bitcast(F32), ALU.subtract).then_inc(fill_out, 1)
                elif k == "done_cmp_k":
                    dve.wait_ge(used, count(s, i, "unit"))
                    nc.vector.tensor_tensor(kc[:], BANK[s.bank][0][0:CROWS, 0:DK], b2[:, 0:DK], ALU.add).then_inc(free[s.bank], 1)
                    fence()
                    square_sum(kc[:], ms[0:CROWS, 0:1])
                    nc.vector.tensor_scalar(ms[0:CROWS, 0:1], ms[0:CROWS, 0:1], 1.0 / DK, EPS, ALU.mult, ALU.add).then_inc(made["cmp_k"], 1)
                elif k == "done_cmp_v":
                    dve.wait_ge(used, count(s, i, "unit"))
                    nc.vector.tensor_tensor(v_c[:], BANK[s.bank][0][0:CROWS, 0:DV], b2[:, DK:], ALU.add).then_inc(free[s.bank], 1)
                elif k == "cmp_norm":
                    dve.wait_ge(cmp_rstd, 1)
                    nc.vector.scalar_tensor_tensor(out=kc[:], in0=kc[:], scalar=rs[0:CROWS, 0:1], in1=g_head[0:CROWS, 3, :],
                                                   op0=ALU.mult, op1=ALU.mult)
                    fence()
                    hw = NSA_ROT // 2
                    x1, x2 = kc[:, 0:hw], kc[:, hw:2 * hw]
                    t = [rot[0:CROWS, 2, 32 * q:32 * q + hw] for q in range(4)]
                    for q, (xx, cs) in enumerate(((x1, cos_c), (x2, sin_c), (x2, cos_c), (x1, sin_c))):
                        nc.vector.tensor_tensor(t[q], xx, cs[:], ALU.mult)
                    fence()
                    nc.vector.tensor_tensor(x1, t[0], t[1], ALU.subtract)
                    nc.vector.tensor_tensor(x2, t[2], t[3], ALU.add).then_inc(cmp_normed, 1)
                elif k == "norm_a":
                    X = head_view(s.which)[0]
                    dve.wait_ge(free["A"], count(s, i, "tileA"))
                    dve.wait_ge(free["B"], count(s, i, "tileB"))
                    if s.which == "mla" and s.lo == HPG:
                        for t in range(TT):
                            nc.vector.tensor_copy(X[:, t, HPG:2 * HPG, MLA_NOPE:DK], kr[:, t, :].unsqueeze(1).to_broadcast([P, HPG, MLA_ROT]))
                        fence()
                    n = s.hi - s.lo
                    for t in range(TT):
                        for q in range(n):
                            square_sum(X[:, t, s.lo + q, :], ms[:, t * n + q:t * n + q + 1])
                    nc.vector.tensor_scalar(ms[:, 0:TT * n], ms[:, 0:TT * n], 1.0 / DK, EPS, ALU.mult, ALU.add).then_inc(ms_ready, 1)
                elif k == "norm_b":
                    X = head_view(s.which)[0]
                    n = s.hi - s.lo
                    dve.wait_ge(rstd_ready, count(s, i, "norm_a"))
                    for t in range(TT):
                        for q in range(n):
                            g = {"mla": 0 if s.lo < 4 else 1, "nsa": 2 if s.lo < 4 else 4 + q}[s.which]
                            x = X[:, t, s.lo + q, :]
                            ins = nc.vector.scalar_tensor_tensor(out=x, in0=x, scalar=rs[:, t * n + q:t * n + q + 1], in1=g_head[:, g, :],
                                                                 op0=ALU.mult, op1=ALU.mult)
                    ins.then_inc(scaled, 1)
                elif k == "turn_head":
                    if s.slot % 2 == 1:
                        wait(dve, filled, count(s, i, "fill", 1))
                        nc.vector.tensor_copy(head_view(s.which)[1][:, s.slot, :], QT[0:HALF, :]).then_inc(fill_out, 1)
                elif k == "scores":
                    dve.wait_ge(scored, count(s, i, "scores", 1))
                    nc.vector.tensor_reduce(mx[:, 0:1], S[:, 0:P], AXX, ALU.max)
                    nc.vector.tensor_reduce(mx[:, 1:2], S[:, P:3 * P], AXX, ALU.max)
                    n = 2
                    if s.which == "nsa":
                        nc.vector.tensor_reduce(mx[:, 2:3], S[:, 3 * P:3 * P + CROWS], AXX, ALU.max)
                        n = 3
                    fence()
                    nc.vector.tensor_scalar(nm[:, 0:n], mx[:, 0:n], -SCALE, FLOOR, ALU.mult, ALU.min).then_inc(negmax, 1)
                elif k == "probs":
                    Pb = Pbs[:, s.job % 2, :]
                    dve.wait_ge(exped, count(s, i, "probs", 1))
                    n = 2 if s.which == "mla" else 3
                    nc.vector.tensor_scalar(rc[:, 0:n], sm[:, 0:n], 1e-30, None, ALU.max)
                    fence()
                    nc.vector.reciprocal(rc[:, 0:n], rc[:, 0:n])
                    fence()
                    if s.which == "nsa":
                        g = gates[:, bass.ds(i * HPG + s.job // 2, 1), s.job % 2, :].rearrange("p a n -> p (a n)")
                        nc.vector.tensor_tensor(rc[:, 0:n], rc[:, 0:n], g, ALU.mult)
                        fence()
                        nc.vector.tensor_scalar(Pb[:, 3 * P:3 * P + CROWS], Pb[:, 3 * P:3 * P + CROWS], rc[:, 2:3], None, ALU.mult)
                    nc.vector.tensor_scalar(Pb[:, 0:P], Pb[:, 0:P], rc[:, 0:1], None, ALU.mult)
                    nc.vector.tensor_scalar(Pb[:, P:3 * P], Pb[:, P:3 * P], rc[:, 1:2], None, ALU.mult).then_inc(probs, 1)
                elif k == "values":
                    if s.last:
                        dve.wait_ge(o_hi, count(s, i, "head", 1))
                        r = s.job if s.which == "mla" else s.job // 2
                        o = om if s.which == "mla" else on
                        hi, lo = (o[q][:, bass.ds(i * HPG + r, 1), :].rearrange("p a n -> p (a n)") for q in range(2))
                        nc.vector.tensor_tensor(lo, OP[:, 0:SEQ], hi.bitcast(F32), ALU.subtract).then_inc(o_free, 1)
                elif k == "done_gate_m":
                    dve.wait_ge(free[s.bank], count(s, i, "tile" + s.bank, 1))
                    m = M[:, :, bass.ds(i * N, N)]
                    nc.vector.tensor_scalar(m, m, 0.5, 0.5, ALU.mult, ALU.add)
                elif k == "done_y_m":
                    dve.wait_ge(used, count(s, i, "unit"))
                    for t in range(TT):
                        m = M[:, t, bass.ds(i * N, N)]
                        ins = nc.vector.tensor_tensor(m, BANK[s.bank][t][:, :], m, ALU.mult)
                    ins.then_inc(free[s.bank], 1)
                elif k == "done_gate_n":
                    dve.wait_ge(free[s.bank], count(s, i, "tile" + s.bank, 1))
                    nc.vector.tensor_scalar(mt[:], mt[:], 0.5, 0.5, ALU.mult, ALU.add)
                    fence()
                elif k == "done_y_n":
                    dve.wait_ge(used, count(s, i, "unit"))
                    for t in range(TT):
                        ins = nc.vector.tensor_tensor(mt[:, t, :], BANK[s.bank][t][:, :], mt[:, t, :], ALU.mult)
                    ins.then_inc(free[s.bank], 1)
                    fence()
                    m = M[:, :, bass.ds(i * N + N * s.tile, N)] if s.tile else M[:, :, 0:N]
                    nc.vector.tensor_tensor(mt[:], mt[:], m, ALU.add).then_inc(made["merged"], 1)
                elif k == "turn_merged":
                    c0 = (i * 4 if s.tile is None else s.tile * 4) + 2 * s.pair
                    turn_split(s, i, FB[s.pair][:, :].rearrange("p (c n) -> p c n", c=2), mT[0][:, bass.ds(c0, 2), :], mT[1][:, bass.ds(c0, 2), :])
                elif k == "done_h":
                    dve.wait_ge(used, count(s, i, "unit"))
                    dve.wait_ge(xt_in, 16)
                    for t in range(TT):
                        hh = h[:, t, s.tile * N:(s.tile + 1) * N]
                        ins = nc.vector.tensor_tensor(hh, BANK[s.bank][t][:, :], hh, ALU.add)
                    ins.then_inc(free[s.bank], 1)
                    fence()
                    for t in range(TT):
                        square_sum(h[:, t, s.tile * N:(s.tile + 1) * N], hss[:, t * NT + s.tile:t * NT + s.tile + 1],
                                   rot[:, 0:2, :].rearrange("p a n -> p (a n)"))
                elif k == "turn_h":
                    c0 = s.tile * 4 + 2 * s.pair
                    turn_split(s, i, FB[s.pair][:, :].rearrange("p (c n) -> p c n", c=2), xT_hi[:, c0:c0 + 2, :], xT_lo[:, c0:c0 + 2, :],
                               gcols[:, KD + c0:KD + c0 + 2])
                elif k == "h_norm":
                    nc.vector.tensor_reduce(msh, hss.rearrange("p (t n) -> p t n", t=TT), AXX, ALU.add)
                    fence()
                    nc.vector.tensor_scalar(msh, msh, 1.0 / D, EPS, ALU.mult, ALU.add).then_inc(h_ms, 1)
                    dve.wait_ge(h_pow, 1)
                    nc.vector.tensor_scalar(rh2, rh, 0.5, None, ALU.mult)
                    fence()
                    nc.vector.tensor_tensor(hs2, rh, rh2, ALU.mult).then_inc(h_rstd, 1)
                elif k == "done_ff_gate":
                    dve.wait_ge(acted["ff"], count(s, i, "ff", 1))
                    for t in range(TT):
                        ins = nc.vector.scalar_tensor_tensor(out=ft[:, t, :], in0=ft[:, t, :], scalar=1.0, in1=BANK["A"][t][:, :],
                                                             op0=ALU.add, op1=ALU.mult)
                    ins.then_inc(free["A"], 1)
                    fence()
                elif k == "done_ff_up":
                    dve.wait_ge(used, count(s, i, "unit"))
                    for t in range(TT):
                        ins = nc.vector.scalar_tensor_tensor(out=ft[:, t, :], in0=ft[:, t, :], scalar=hs2[:, t:t + 1], in1=BANK["B"][t][:, :],
                                                             op0=ALU.mult, op1=ALU.mult)
                    ins.then_inc(free["B"], 1)
                elif k == "turn_ff":
                    c0 = (i * 4 if s.tile is None else s.tile * 4) + 2 * s.pair
                    turn_split(s, i, FB[s.pair][:, :].rearrange("p (c n) -> p c n", c=2), fT[0][:, bass.ds(c0, 2), :], fT[1][:, bass.ds(c0, 2), :])
                elif k == "done_down":
                    dve.wait_ge(used, count(s, i, "unit"))
                    for t in range(TT):
                        hh = h[:, t, s.tile * N:(s.tile + 1) * N]
                        ins = nc.vector.tensor_tensor(hh, BANK[s.bank][t][:, :], hh, ALU.add)
                    ins.then_inc(free[s.bank], 1)

        @block.gpsimd
        def _(pool):
            def fence():
                nc.gpsimd.drain()

            def rsqrt(dst, src, n, rows=P):
                return nc.gpsimd.tensor_tensor(dst, src, mhalf[0:rows, 0:n], ALU.pow)

            nc.gpsimd.memset(mhalf, -0.5)
            fence()
            pool.wait_ge(ms_x, 1)
            rsqrt(rx, msx, TT).then_inc(x_rstd, 1)
            pool.wait_ge(const, 16 * (NCONST - NFIRST))
            for s, i in walk(pool, PH):
                k = s.kind
                if k == "lat_a":
                    pool.wait_ge(ms_ready, count(s, i, "norm_a", 1))
                    rsqrt(rs[:, 0:TT], ms[:, 0:TT], TT).then_inc(rstd_ready, 1)
                elif k == "done_cmp_k":
                    pool.wait_ge(made["cmp_k"], 1)
                    rsqrt(rs[0:CROWS, 0:1], ms[0:CROWS, 0:1], 1, CROWS).then_inc(cmp_rstd, 1)
                elif k == "h_norm":
                    pool.wait_ge(h_ms, 1)
                    rsqrt(rh, msh, TT).then_inc(h_pow, 1)
                elif k == "norm_a":
                    n = TT * (s.hi - s.lo)
                    pool.wait_ge(ms_ready, count(s, i, "norm_a", 1))
                    rsqrt(rs[:, 0:n], ms[:, 0:n], n).then_inc(rstd_ready, 1)
                elif k == "norm_b":
                    X, _, cos, sin, start, hw = head_view(s.which)
                    n = s.hi - s.lo
                    pool.wait_ge(scaled, count(s, i, "norm_b", 1))
                    x1 = X[:, :, s.lo:s.hi, start:start + hw]
                    x2 = X[:, :, s.lo:s.hi, start + hw:start + 2 * hw]
                    c = cos[:].unsqueeze(2).to_broadcast([P, TT, n, hw])
                    sn = sin[:].unsqueeze(2).to_broadcast([P, TT, n, hw])
                    t = [rot[:, q, 0:TT * n * hw].rearrange("p (t n h) -> p t n h", t=TT, n=n) for q in range(4)]
                    nc.gpsimd.tensor_tensor(t[0], x1, c, ALU.mult)
                    nc.gpsimd.tensor_tensor(t[1], x2, sn, ALU.mult)
                    nc.gpsimd.tensor_tensor(t[2], x2, c, ALU.mult)
                    nc.gpsimd.tensor_tensor(t[3], x1, sn, ALU.mult)
                    fence()
                    nc.gpsimd.tensor_tensor(x1, t[0], t[1], ALU.subtract)
                    nc.gpsimd.tensor_tensor(x2, t[2], t[3], ALU.add).then_inc(roped, 1)
                    fence()

        @block.tensor
        def _(pe):
            def turn(dst, src, rows=P):
                return nc.tensor.transpose(dst, src, ident[0:rows, 0:rows])

            def turn_pair(src, cols, bank):
                for c in range(2):
                    for t in range(TT):
                        ins = turn(bank[:, c * SEQ + t * P:c * SEQ + (t + 1) * P], src[:, t, cols + c * P:cols + (c + 1) * P])
                return ins

            for s, i in walk(pe, PH):
                k = s.kind
                if k in PAIRED:
                    pe.wait_ge(fill_out, count(s, i, "fill", -1))
                elif "fill" in s.kinds and k not in ("setup", "turn_x"):
                    pe.wait_ge(fill_out, count(s, i, "fill"))
                if k == "unit":
                    if s.first:
                        wait(pe, free[s.bank], count(s, i, "tile" + s.bank))
                        if s.lhs != "x" or s.weight == "w_ffn_gate":
                            wait(pe, fill_out, count(s, i, "fill"))
                            if s.lhs in ("fk", "fv"):
                                pe.wait_ge(flat_out, 1 if s.lhs == "fv" else 3)
                            if s.lhs in ("om", "on"):
                                pe.wait_ge(o_free, count(s, i, "head", 1))
                        else:
                            wait(pe, fill_out, 1 + KD // 2)
                    elif s.lhs in ("ff", "m") or s.weight == "w_ffn_gate":
                        if s.chunk >= (KF if s.lhs == "ff" else KD) - 4:
                            wait(pe, fill_out, count(s, i, "fill"))
                    pe.wait_ge(split, count(s, i, "unit", 1))
                    sl = slot_of(s)
                    outs = halves(s)
                    M_ = CROWS if s.lhs in ("fk", "fv", "hk", "hv") else P
                    for c in range(s.m):
                        first, last = s.first and c == 0, s.last and c == s.m - 1
                        for t, c0, c1, bank in outs:
                            dst = bank[0:M_, 0:c1 - c0]
                            wh = whi[0:s.rows, sl, c * s.width + c0:c * s.width + c1]
                            wl = wlo[0:s.rows, sl, c * s.width + c0:c * s.width + c1]
                            nc.tensor.matmul(dst, lhsT(s, 0, s.chunk + c, t), wh, start=first, stop=False)
                            nc.tensor.matmul(dst, lhsT(s, 0, s.chunk + c, t), wl, start=False, stop=False)
                            ins = nc.tensor.matmul(dst, lhsT(s, 1, s.chunk + c, t), wh, start=False, stop=last)
                    ins.then_inc(used, 1)
                elif k == "setup":
                    pe.wait_ge(const0, 16 * NFIRST)
                    turn(QT[:, 0:2 * KD], rows_sb[:], 2 * KD)
                    for c in range(2):
                        turn(QT[0:HALF, 32 + 32 * c:64 + 32 * c], pe_k_sb[:, c * HALF:(c + 1) * HALF], CMP_LEN)
                    turn(QT[:, 96:128], pe_v_sb[:], CMP_LEN).then_inc(filled, 1)
                elif k == "turn_x":
                    pe.wait_ge(x_in[s.pair // 2], 16)
                    pe.wait_ge(fill_out, max(1, count(s, i, "fill") - 3))
                    turn_pair(x_sb, 2 * s.pair * P, FB[s.bank]).then_inc(filled, 1)
                elif k == "turn_kc":
                    pe.wait_ge(free["A"], 2)
                    pe.wait_ge(free["B"], 1)
                    for c in range(2):
                        for t in range(TT):
                            o = s.slot * DK + c * HALF
                            ins = turn(QT[0:HALF, c * SEQ + t * P:c * SEQ + (t + 1) * P], kv[:, t, o:o + HALF])
                    ins.then_inc(filled, 1)
                elif k == "turn_vc":
                    turn_pair(kv, GROUPS * DK + 2 * s.slot * P, QT).then_inc(filled, 1)
                elif k == "turn_lat":
                    pe.wait_ge(scaled, count(s, i, "norm_b"))
                    turn_pair(lat[:, :, s.which, :], 2 * s.pair * P, QT).then_inc(filled, 1)
                elif k == "turn_hidden":
                    pe.wait_ge(made["hidden_" + ("k" if s.c0 < 6 else "v")], 1)
                    for c in range(s.c0, s.c1):
                        ins = turn(QT[:, (c - s.c0) * CROWS:(c - s.c0 + 1) * CROWS], hid[:, c * P:(c + 1) * P], CROWS)
                    ins.then_inc(filled, 1)
                elif k == "turn_cmp":
                    pe.wait_ge(cmp_normed, 1)
                    for c in range(2):
                        ins = turn(QT[0:HALF, c * CROWS:(c + 1) * CROWS], kc[:, c * HALF:(c + 1) * HALF], CROWS)
                    ins.then_inc(filled, 1)
                elif k == "turn_head":
                    X = head_view(s.which)[0]
                    pe.wait_ge(roped, count(s, i, "rope"))
                    for c in range(2):
                        for t in range(TT):
                            ins = turn(QT[0:HALF, c * SEQ + t * P:c * SEQ + (t + 1) * P], X[:, t, s.slot, c * HALF:(c + 1) * HALF])
                    ins.then_inc(filled, 1)
                elif k == "scores":
                    T = head_view(s.which)[1]
                    r, kk = (s.job, HPG + s.job) if s.which == "mla" else (s.job // 2, HPG + s.job % 2)
                    pe.wait_ge(fill_out, count(s, i, "fill"))
                    wait(pe, exped, count(s, i, "scores"))
                    def mm(dst, l, rr, **kw):
                        return nc.tensor.matmul(dst, l, rr, skip_group_check=True, **kw)
                    mm(S[:, 0:P], identb[:], maskb[:], start=True, stop=False)
                    mm(S[:, 2 * P:3 * P], identb[:], maskb[:], start=False, stop=False)
                    if s.which == "nsa":
                        tc = s.job % 2
                        SC = S[:, 3 * P:3 * P + CROWS]
                        mm(SC, identb[:], cmaskb[:, tc, bass.ds(i, 1), :].rearrange("p a n -> p (a n)"), start=False, stop=False)
                    for c in range(2):
                        q = [T[:, r, c * SEQ + t * P:c * SEQ + (t + 1) * P] for t in range(TT)]
                        if s.which == "nsa":
                            mm(SC, q[tc], kcT[:, c, :], start=False, stop=c == 1)
                        mm(S[:, 0:P], q[0], T[:, kk, c * SEQ:c * SEQ + P], start=False, stop=c == 1)
                        ins = mm(S[:, P:3 * P], q[1], T[:, kk, c * SEQ:(c + 1) * SEQ], start=False, stop=c == 1)
                    ins.then_inc(scored, 1)
                elif k == "turn_probs":
                    Pb = Pbs[:, s.job % 2, :]
                    pe.wait_ge(probs, count(s, i, "turn_probs", 1))
                    for q in range(3):
                        ins = turn(TP[:, q * P:(q + 1) * P], Pb[:, q * P:(q + 1) * P])
                    if s.which == "nsa":
                        ins = turn(TP[0:CROWS, 3 * P:4 * P], Pb[:, 3 * P:3 * P + CROWS])
                    ins.then_inc(turned, 1)
                elif k == "values":
                    pe.wait_ge(pt_out, count(s, i, "values", 1))
                    if s.which == "mla":
                        V, j, start = v_m, s.job, True
                    else:
                        V, j, start = v_n, s.job % 2, s.job % 2 == 0
                    if start:
                        pe.wait_ge(o_free, count(s, i, "head", 1))
                    stop = s.last
                    nc.tensor.matmul(OP[:, 0:SEQ], V[:, 0, j, :], pT[:, 0:SEQ], start=start, stop=False, skip_group_check=True)
                    ins = nc.tensor.matmul(OP[:, P:SEQ], V[:, 1, j, :], pT[:, SEQ:SEQ + P], start=False, stop=stop, skip_group_check=True)
                    if s.which == "nsa":
                        tc = s.job % 2
                        ins = nc.tensor.matmul(OP[:, tc * P:(tc + 1) * P], v_c[:], pT[0:CROWS, 3 * P:4 * P], start=False, stop=stop,
                                               skip_group_check=True)
                    ins.then_inc(valued, 1)
                elif k == "turn_merged":
                    pe.wait_ge(made["merged"], count(s, i, "merged"))
                    turn_pair(mt, 2 * s.pair * P, FB[s.pair]).then_inc(filled, 1)
                elif k == "turn_h":
                    pe.wait_ge(free["AB"[s.tile % 2]], count(s, i, "tile" + "AB"[s.tile % 2]))
                    turn_pair(h, s.tile * N + 2 * s.pair * P, FB[s.pair]).then_inc(filled, 1)
                elif k == "turn_ff":
                    pe.wait_ge(free["B"], count(s, i, "tileB"))
                    turn_pair(ft, 2 * s.pair * P, FB[s.pair]).then_inc(filled, 1)


_INS = ['x', 'attn_norm_g', 'w_in', 'mla_q_lat_g', 'mla_kv_lat_g', 'mla_w_uq', 'mla_w_uk', 'mla_w_uv',
        'mla_q_norm_g', 'mla_k_norm_g', 'nsa_q_norm_g', 'nsa_k_norm_g', 'cmp_pe_k', 'cmp_pe_v',
        'cmp_k_w1', 'cmp_k_b1', 'cmp_k_w2', 'cmp_k_b2', 'cmp_v_w1', 'cmp_v_b1', 'cmp_v_w2', 'cmp_v_b2',
        'w_proj_mla', 'w_proj_nsa', 'w_out', 'ffn_norm_g', 'w_ffn_gate', 'w_ffn_up', 'w_ffn_down']


def _constants():
    import numpy as np
    bf16 = np.dtype("bfloat16")
    c = {"ident": np.eye(P, dtype=np.float32), "identb": np.eye(P, dtype=bf16)}
    q = np.arange(P)
    c["maskb"] = np.where(q[None, :] <= q[:, None], 0.0, MASKED).astype(bf16)
    end = np.arange(NCMP) * CMP_STRIDE + CMP_LEN - 1
    ok = np.zeros((SEQ, GROUPS, GROUPS, NCMP), bool)
    for g in range(GROUPS):
        ok[:, g, g, :] = end[None, :] <= np.arange(SEQ)[:, None]
    c["cmaskb"] = np.where(ok, 0.0, MASKED).reshape(SEQ, GROUPS, CROWS).astype(bf16)

    def tables(pos, dim):
        inv = np.float32(500000.0) ** (-np.arange(0, dim, 2, dtype=np.float32) / np.float32(dim))
        ang = pos.astype(np.float32)[:, None] * inv[None, :].astype(np.float32)
        return np.cos(ang).astype(np.float32), np.sin(ang).astype(np.float32)
    c["cos_m"], c["sin_m"] = tables(np.arange(SEQ), MLA_ROT)
    c["cos_n"], c["sin_n"] = tables(np.arange(SEQ), NSA_ROT)
    c["cos_c"], c["sin_c"] = tables(np.tile(end, GROUPS), NSA_ROT)
    return c


def kernel(**inputs):
    import numpy as _np
    import concourse.bacc as _bacc
    from concourse import mybir as _mybir
    from concourse.bass_utils import run_bass_kernel_spmd as _run

    nc = _bacc.Bacc("TRN2", target_bir_lowering=False, num_devices=1)
    arrays, aps = {}, {}
    for name in _INS:
        a = _np.ascontiguousarray(inputs[name])
        arrays[f"in_{name}_dram"] = a
        aps[name] = nc.dram_tensor(f"in_{name}_dram", a.shape, _mybir.dt.from_np(a.dtype), kind="ExternalInput").ap()[0]
    for name, a in _constants().items():
        arrays[f"const_{name}_dram"] = a
        aps[name] = nc.dram_tensor(f"const_{name}_dram", a.shape, _mybir.dt.from_np(a.dtype), kind="ExternalInput").ap()
    out = nc.dram_tensor("out_0_dram", (1, SEQ, D), _mybir.dt.float32, kind="ExternalOutput").ap()
    build(nc, aps, out[0])
    r = _run(nc, [arrays], core_ids=[0])
    return r.results[0]["out_0_dram"]
```

```python
from contextlib import ExitStack, nullcontext

import concourse.bass as bass
from concourse import mybir

F32 = mybir.dt.float32
F32R = mybir.dt.float32r
BF16 = mybir.dt.bfloat16
ALU = mybir.AluOpType
ACT = mybir.ActivationFunctionType
AXX = mybir.AxisListType.X

P = 128
D = 2048
SEQ = 256
TT = SEQ // P
KD = D // P
EPS = 1e-6
HEADS, GROUPS = 16, 4
HPG = HEADS // GROUPS
DK, DV = 192, 128
RANK = 512
MLA_NOPE, MLA_ROT, NSA_ROT = 128, 64, 48
CMP_LEN, CMP_STRIDE = 32, 16
NCMP = (SEQ - CMP_LEN) // CMP_STRIDE + 1
CROWS = GROUPS * NCMP
HID_K, HID_V = 4 * DK, 4 * DV
HALF = DK // 2
D_FF = -(-8 * D // (3 * 256)) * 256
KF = D_FF // P
N = 512
NT = D // N
FT = D_FF // N
SCALE = DK ** -0.5
MASKED = -1e34
LOWEST = -1e26

O_KR = 2 * RANK
O_Q = O_KR + MLA_ROT
O_KC = O_Q + HEADS * DK
O_VC = O_KC + GROUPS * DK
O_KS = O_VC + GROUPS * DV
O_VS = O_KS + GROUPS * DK
O_KW = O_VS + GROUPS * DV
O_VW = O_KW + GROUPS * DK
O_GN = O_VW + GROUPS * DV
O_GM = O_GN + HEADS * 3
D_IN = O_GM + 2 * D

RING = 4
SLOT = 1024
AHEAD = 3
NCONST, NFIRST = 22, 5


class Step:
    def __init__(self, kind, kinds=(), bank=None, which=None, tile=None, pair=None, slot=None, job=None, lo=None, hi=None,
                 weight=None, col=None, lhs=None, chunk=None, m=None, width=None, rows=None, step=0, start=0,
                 first=False, last=False, off=None, w=None, c0=None, c1=None, h=None):
        self.kind, self.kinds, self.bank, self.which, self.tile, self.pair = kind, kinds, bank, which, tile, pair
        self.slot, self.job, self.lo, self.hi, self.h = slot, job, lo, hi, h
        self.weight, self.col, self.lhs, self.chunk, self.m, self.width, self.rows = weight, col, lhs, chunk, m, width, rows
        self.step, self.start, self.first, self.last = step, start, first, last
        self.off, self.w, self.c0, self.c1 = off, w, c0, c1
        self.base, self.per, self.ahead = {}, {}, None


class Phase:
    def __init__(self, steps, times=1):
        self.steps, self.times = steps, times


def number(phases):
    seen = {}
    for ph in phases:
        local = dict(seen)
        for s in ph.steps:
            s.base = dict(local)
            for k in s.kinds:
                local[k] = local.get(k, 0) + 1
        per = {k: local[k] - seen.get(k, 0) for k in local}
        for s in ph.steps:
            s.per = per if ph.times > 1 else {}
        for k in local:
            seen[k] = seen.get(k, 0) + per[k] * ph.times
    return phases


def walk(eng, phases):
    for ph in phases:
        with (eng.Fori(0, ph.times) if ph.times > 1 else nullcontext(0)) as i:
            for s in ph.steps:
                yield s, i


def count(s, i, kind, more=0):
    n, per = s.base.get(kind, 0) + more, s.per.get(kind, 0)
    return i * per + n if per else n


def wait(eng, sem, value):
    if isinstance(value, int) and value <= 0:
        return
    eng.wait_ge(sem, value)



def tile_units(out, weight, col, lhs, chunks, width, per_unit, rows=P, k0=0, **about):
    steps = []
    for c in range(0, chunks, per_unit):
        m = min(per_unit, chunks - c)
        steps.append(Step("unit", ("unit",), bank=out, weight=weight, col=col, lhs=lhs, chunk=k0 + c, m=m,
                          width=width, rows=rows, first=c == 0, last=c + m == chunks, **about))
    return steps


def weave(units, extras):
    steps = []
    for k, u in enumerate(units):
        steps.append(u)
        steps += extras.get(k, [])
    for k in sorted(extras):
        if k >= len(units):
            steps += extras[k]
    return steps


def done(bank, what, **about):
    return Step("done_" + what, ("tile" + bank,), bank=bank, **about)


def k_sq(which):
    return Step("k_sq", ("ms",) + ("rope",) * (which == "mla"), which=which)


def k_scale(which):
    return Step("k_scale", ("scale",) + ("rope",) * (which == "nsa"), which=which)


def q_sq(which, h):
    return Step("q_sq", ("ms", "rope"), which=which, h=h)


def turn_heads(which, a, b, before=0):
    return Step("turn_heads", ("fill", "fill"), which=which, lo=a, hi=b, job=before)


def jobs(which, njobs, at, turns):
    extras = {}
    for k in range(njobs + 2):
        st = extras.setdefault(at[k], [])
        if 1 <= k <= njobs:
            st.append(Step("probs", ("probs",), which=which, job=k - 1))
        if k in turns:
            st.insert(0, turn_heads(which, *turns[k], max(0, k - 1)))
        if k < njobs:
            st.append(Step("scores", ("scores",), which=which, job=k, lo=2 if k in turns else 0))
        if k >= 2:
            last = which == "mla" or (k - 2) % 2 == 1
            st.append(Step("values", ("values",) + ("head",) * last, which=which, job=k - 2, last=last))
        if 1 <= k <= njobs:
            st.append(Step("turn_probs", ("turn_probs",), which=which, job=k - 1))
    return extras


def merge_extras(*many):
    out = {}
    for e in many:
        for k, v in e.items():
            out.setdefault(k, []).extend(v)
    return out


def schedule():
    phases = [Phase([Step("setup", ("fill",))] +
                    [Step("turn_x", ("fill", "sfill"), pair=c, bank=c % 4) for c in range(KD // 2)])]

    b = tile_units("A", "w_in", O_KC, "x", KD, N, 2) + [done("A", "kv", off=0, w=N)]
    b += tile_units("B", "w_in", O_KC + N, "x", KD, N, 2) + [done("B", "kv", off=N, w=N)]
    b += tile_units("A", "w_in", O_KC + 2 * N, "x", KD, 256, 4) + [done("A", "kv", off=2 * N, w=256)]
    krg = tile_units("B", "kr_gates", 0, "x", KD, MLA_ROT + 3 * HEADS, 8)
    b += krg + [done("B", "krg")]
    cq = tile_units("A", "w_in", 0, "x", KD, N, 2)
    b += weave(cq, {0: [Step("turn_kc", ("fill",), slot=0)], 1: [Step("turn_kc", ("fill",), slot=1)],
                    2: [Step("turn_kc", ("fill",), slot=2), Step("turn_vc", ("fill",), slot=0)],
                    3: [Step("turn_vc", ("fill",), slot=1), Step("flat", ("flat",), which="v")], 4: [Step("turn_kc", ("fill",), slot=3)],
                    5: [Step("flat", ("flat",), which="k0")], 6: [Step("flat", ("flat",), which="k1")]})
    b += [done("A", "lat", which=0)]
    phases.append(Phase(b))

    fv = tile_units("B", "cmp_v_w1", 0, "fv", CMP_LEN, HID_V, 2)
    c = weave(fv, {1: [Step("gains")], 2: [Step("lat_a", ("ms",), which=0)], 5: [Step("lat_b", ("scale",), which=0)],
                   8: [Step("turn_lat", ("fill", "sfill"), which=0, pair=0)], 10: [Step("turn_lat", ("fill", "sfill"), which=0, pair=1)],
                   12: [Step("load_b")]})
    fk = tile_units("A", "cmp_k_w1", 0, "fk", CMP_LEN * 2, HID_K, 1, rows=HALF)
    c += weave(fk, {0: [done("B", "hidden_v")],
                    20: [Step("turn_hidden", ("fill", "sfill"), c0=6, c1=10)]})
    ckv = tile_units("B", "w_in", RANK, "x", KD, N, 2)
    w2v = tile_units("A", "cmp_v_w2", 0, "hv", HID_V // P, DV, 4)
    w2k = tile_units("A", "cmp_k_w2", 0, "hk", HID_K // P, DK, 3)
    c += weave(ckv, {0: [done("A", "hidden_k")], 1: w2v + [done("A", "cmp_v")],
                     4: [Step("turn_hidden", ("fill", "sfill"), c0=0, c1=4)], 5: [Step("turn_hidden", ("fill", "sfill"), c0=4, c1=6)],
                     6: w2k + [done("A", "cmp_k")],
                     7: [done("B", "lat", which=1), Step("cmp_norm", ("cmp_norm",)), Step("lat_a", ("ms",), which=1),
                         Step("lat_b", ("scale",), which=1),
                         Step("turn_lat", ("fill", "sfill"), which=1, pair=0), Step("turn_lat", ("fill", "sfill"), which=1, pair=1),
                         Step("turn_cmp", ("fill",))]})
    phases.append(Phase(c))

    u = tile_units("A", "mla_w_uk", 0, "ckv", 4, N, 2, step=N)
    u += tile_units("B", "mla_w_uq", 0, "cq", 4, 2 * DK, 2, step=4 * DK)
    u += tile_units("A", "mla_w_uq", 2 * DK, "cq", 4, 2 * DK, 2, step=4 * DK)
    u += tile_units("B", "mla_w_uv", 0, "ckv", 4, N, 2, step=N)
    u += tile_units("A", "w_in", O_GM, "x", KD, N, 2, step=N)
    ex = {1: [done("A", "mla_k"), k_sq("mla")],
          2: [k_scale("mla")],
          3: [done("B", "mla_q", h=0), q_sq("mla", 0)],
          5: [done("A", "mla_q", h=2), q_sq("mla", 2)],
          7: [done("B", "mla_v"), turn_heads("mla", HPG, 0)],
          15: [done("A", "gate_m")]}
    jb = jobs("mla", HPG, [8, 9, 10, 11, 13, 15], {k: (HPG + k + 1, k + 1) for k in range(HPG - 1)})
    phases.append(Phase(weave(u, merge_extras(ex, jb)), GROUPS))

    u = tile_units("A", "ks_kw", 0, "x", KD, 2 * DK, 2, step=DK)
    u += tile_units("B", "vs_vw", 0, "x", KD, 2 * DV, 4, step=DV)
    u += tile_units("A", "w_in", O_Q, "x", KD, 2 * DK, 2, step=4 * DK)
    u += tile_units("B", "w_in", O_Q + 2 * DK, "x", KD, 2 * DK, 2, step=4 * DK)
    u += tile_units("A", "w_proj_mla", 0, "om", KD, N, 2, step=N)
    ex = {7: [done("A", "nsa_k"), k_sq("nsa")],
          9: [k_scale("nsa")],
          11: [done("B", "nsa_v")],
          14: [turn_heads("nsa", 4, 5)],
          19: [done("A", "nsa_q", h=0), q_sq("nsa", 0)],
          22: [turn_heads("nsa", 0, 1)],
          27: [done("B", "nsa_q", h=2), q_sq("nsa", 2)],
          35: [done("A", "y_m")]}
    jb = jobs("nsa", 2 * HPG, [23, 24, 26, 29, 30, 31, 32, 33, 34, 35], {3: (2, 3)})
    phases.append(Phase(weave(u, merge_extras(ex, jb)), GROUPS))

    def merged(back):
        u = tile_units("A", "w_in", O_GM + D, "x", KD, N, 2, step=N, start=0 if not back else N)
        u += tile_units("B", "w_proj_nsa", 0, "on", KD, N, 2, step=N, start=0 if not back else N)
        ex = {7: [done("A", "gate_n")], 15: [Step("done_y_n", ("tileB", "merged"), bank="B", tile=back)]}
        if back:
            ex[1] = [Step("turn_merged", ("fill", "sfill"), pair=0)]
            ex[2] = [Step("turn_merged", ("fill", "sfill"), pair=1)]
        return weave(u, ex)
    phases.append(Phase([Step("load_x")] + merged(0)))
    phases.append(Phase(merged(1), NT - 1))

    g = []
    for n in range(NT):
        bank = "AB"[n % 2]
        what, t = ("turn_h", n - 1) if n else ("turn_merged", NT - 1)
        ex = {k + 1: [Step(what, ("fill", "sfill"), pair=k, tile=t)] for k in range(2)}
        g += weave(tile_units(bank, "w_out", n * N, "m", KD, N, 2), ex) + [done(bank, "h", tile=n)]
    phases.append(Phase(g))

    def ffn(back):
        u = tile_units("A", "w_ffn_gate", 0, "x", KD, N, 2, step=N, start=N if back else 0)
        u += tile_units("B", "w_ffn_up", 0, "x", KD, N, 2, step=N, start=N if back else 0)
        ex = {7: [Step("done_ff_gate", ("tileA", "ff"), bank="A")], 15: [done("B", "ff_up")]}
        if back:
            ex[1] = [Step("turn_ff", ("fill", "sfill"), pair=0)]
            ex[2] = [Step("turn_ff", ("fill", "sfill"), pair=1)]
        else:
            ex[1] = [Step("turn_h", ("fill", "sfill"), pair=0, tile=NT - 1)]
            ex[2] = [Step("turn_h", ("fill", "sfill"), pair=1, tile=NT - 1), Step("h_norm")]
        return weave(u, ex)
    phases.append(Phase(ffn(0)))
    phases.append(Phase(ffn(1), FT - 1))
    d = []
    for n in range(NT):
        bank = "AB"[n % 2]
        u = tile_units(bank, "w_ffn_down", n * N, "ff", KF, N, 2)
        ex = {2: [Step("turn_ff", ("fill", "sfill"), pair=0, tile=FT - 1)], 3: [Step("turn_ff", ("fill", "sfill"), pair=1, tile=FT - 1)]} if n == 0 else {}
        d += weave(u, ex) + [done(bank, "down", tile=n)]
    phases.append(Phase(d))
    return number(phases)


def build(nc, A, out):
    PH = schedule()
    with ExitStack() as ctx:
        def sem(name):
            return ctx.enter_context(nc.semaphore(name))

        base = [nc.sbuf_base]

        def at(name, shape, dt, off):
            off = (off + 31) // 32 * 32
            n = 2 if dt == BF16 else 4
            for s in shape[1:]:
                n *= s
            base[0] = off + n
            return nc.alloc_sbuf_tensor_at(name, list(shape), dt, offset=off)

        def sb(name, shape, dt=F32):
            return at(name, shape, dt, base[0])

        raw = sb("raw", [P, RING, SLOT])
        whi = sb("whi", [P, RING, SLOT], F32R)
        wlo = sb("wlo", [P, RING, SLOT], F32R)
        xT_hi = sb("xT_hi", [P, KD, SEQ], F32R)
        xT_lo = sb("xT_lo", [P, KD, SEQ], F32R)
        PB_OFF = base[0]
        Pbs = sb("probs", [P, 2, N])
        pT = sb("pT", [P, N])
        rot = sb("rot", [P, 4, 128])
        ident = sb("ident", [P, P])
        identb = sb("identb", [P, P], BF16)
        maskb = sb("maskb", [P, P], BF16)
        cmaskb = sb("cmaskb", [P, TT, GROUPS, CROWS], BF16)
        cos_n = sb("cos_n", [P, TT, NSA_ROT // 2])
        sin_n = sb("sin_n", [P, TT, NSA_ROT // 2])
        cos_c = sb("cos_c", [CROWS, NSA_ROT // 2])
        sin_c = sb("sin_c", [CROWS, NSA_ROT // 2])
        g_head = sb("g_head", [P, 6, DK])
        gcols = sb("gcols", [P, 2 * KD])
        kr = sb("kr", [P, TT, MLA_ROT])
        gates = sb("gates", [P, HEADS, 2, 3])
        kcT = sb("kcT_cmp", [HALF, 2, CROWS])
        v_c = sb("v_c", [CROWS, DV])
        junk = sb("junk", [P, 4, DK])
        rot_m = sb("rot_m", [P, 4, TT, MLA_ROT // 2])
        rot_n = sb("rot_n", [P, 4, TT, NSA_ROT // 2])
        small = sb("small", [P, 208])
        FIXED = base[0]
        KB = 1024

        def over(name, shape, dt, kb):
            return at(name, shape, dt, FIXED + int(kb * KB))

        latT = [[over(f"lat{w}_{p}", [P, 4, SEQ], F32R, 4 * (2 * w + k)) for k, p in enumerate(("hi", "lo"))] for w in range(2)]
        x_sb = over("x_sb", [P, TT, D], F32, 16)
        rows_sb = over("rows_sb", [2 * KD, P], F32, 32)
        pe_k_sb = over("pe_k_sb", [CMP_LEN, DK], F32, 32.5)
        pe_v_sb = over("pe_v_sb", [CMP_LEN, DV], F32, 33.25)
        fk = [over(f"fk_{p}", [HALF, 2 * CMP_LEN, CROWS], F32R, 16 + 15 * k) for k, p in enumerate(("hi", "lo"))]
        fv = [over(f"fv_{p}", [P, CMP_LEN, CROWS], F32R, 46 + 7.5 * k) for k, p in enumerate(("hi", "lo"))]
        lat = over("lat", [P, TT, 2, RANK], F32, 61)
        kv = over("kv", [P, TT, 1280], F32, 69)
        kc_turned = over("kc_turned", [HALF, GROUPS, 2, SEQ], F32, 79)
        vc_turned = over("vc_turned", [P, GROUPS, SEQ], F32, 87)
        flat = over("flat", [P, CMP_LEN, CROWS], F32, 91)
        g_lat = over("g_lat", [P, 2, RANK], F32, 98.5)
        cos_m = over("cos_m", [P, TT, MLA_ROT // 2], F32, 102.5)
        sin_m = over("sin_m", [P, TT, MLA_ROT // 2], F32, 102.75)
        peT_k = over("peT_k", [HALF, 2, CMP_LEN], F32, 103)
        peT_v = over("peT_v", [P, CMP_LEN], F32, 103.25)
        hid = over("hid", [CROWS, HID_K + HID_V], F32, 69)
        hid_a = over("hid_a", [CROWS, HID_K + HID_V], F32, 74)
        b1 = over("b1", [CROWS, HID_K + HID_V], F32, 79)
        hT = [over(f"hT_{p}", [P, 10, CROWS], F32R, 84 + 2.5 * k) for k, p in enumerate(("hi", "lo"))]
        kc = over("kc", [CROWS, DK], F32, 89)
        b2 = over("b2", [CROWS, DK + DV], F32, 90)
        M = over("M", [P, TT, D], F32, 16)
        om = [over(f"om_{p}", [P, HEADS, SEQ], F32R, 32 + 16 * k) for k, p in enumerate(("hi", "lo"))]
        qk_m = over("qk_m", [P, TT, 8, DK], F32, 64)
        qkT_m = over("qkT_m", [HALF, 8, 2 * SEQ], F32, 76)
        v_m = over("v_m", [P, TT, HPG, DV], F32, 92)
        on = [over(f"on_{p}", [P, HEADS, SEQ], F32R, 64 + 16 * k) for k, p in enumerate(("hi", "lo"))]
        qkT_n = over("qkT_n", [HALF, 6, 2 * SEQ], F32, 0)
        v_n = over("v_n", [P, TT, 2, DV], F32, 12)
        qk_n = over("qk_n", [P, TT, 6, DK], F32, 96)
        mT = [over(f"mT_{p}", [P, KD, SEQ], F32R, 32 + 16 * k) for k, p in enumerate(("hi", "lo"))]
        mt = over("mt", [P, TT, N], F32, 96)
        h = over("h", [P, TT, D], F32, 0)
        fT = [over(f"fT_{p}", [P, KF, SEQ], F32R, 16 + 44 * k) for k, p in enumerate(("hi", "lo"))]
        ft = at("ft", [P, TT, N], F32, PB_OFF)
        assert FIXED + 105 * KB <= nc.sbuf_usable_end

        ps = [ctx.enter_context(nc.psum_tensor(f"ps{b}", [P, 512], F32)) for b in range(8)]
        BANK = {"A": (ps[0], ps[1]), "B": (ps[2], ps[3])}
        S, TP, OP, QT = ps[4], ps[5], ps[6], ps[7]

        rx, hrx, msx = small[:, 0:2], small[:, 2:4], small[:, 4:6]
        ms, rs = small[:, 8:24], small[:, 24:40]
        mhalf = small[:, 40:56]
        mx, nm, sm, rc = small[:, 56:59], small[:, 59:62], small[:, 62:65], small[:, 65:68]
        hss, rh, rh2 = small[:, 72:80], small[:, 80:82], small[:, 82:84]
        gsig = small[:, 88:88 + 96]
        msh = small[:, 84:86]
        hs2 = small[:, 86:88]
        ms_q, rq = ms[:, 8:16], rs[:, 8:16]
        neg_rq = small[:, 184:200].rearrange("p (r n) -> p r n", n=4)
        ms_kr = small[:, 200:202]

        const = sem("const")
        const0 = sem("const0")
        bias_in = sem("bias_in")
        x_in = [sem(f"x_in{q}") for q in range(NT)]
        xt_in = sem("xt_in")
        ready = sem("ready")
        loaded = [sem(f"loaded{k}") for k in range(RING)]
        hi_made, split, used = sem("hi_made"), sem("split"), sem("used")
        free = {"A": sem("freeA"), "B": sem("freeB")}
        filled, fill_hi, fill_out = sem("filled"), sem("fill_hi"), sem("fill_out")
        ms_ready, rstd_ready, scaled, roped = sem("ms_ready"), sem("rstd_ready"), sem("scaled"), sem("roped")
        x_rstd = sem("x_rstd")
        ms_x = sem("ms_x")
        flat_made, flat_hi, flat_out = sem("flat_made"), sem("flat_hi"), sem("flat_out")
        scored, negmax, exped, probs = sem("scored"), sem("negmax"), sem("exped"), sem("probs_ready")
        turned, pt_out, valued, o_hi, o_free = sem("turned"), sem("pt_out"), sem("valued"), sem("o_hi"), sem("o_free")
        act_tmp, dve_tmp = {}, {}
        acted = {k: sem("acted_" + k) for k in ("hidden_k", "hidden_v", "gate_m", "gate_n", "ff", "krg")}
        made = {k: sem("made_" + k) for k in ("hidden_k", "hidden_v", "cmp_k", "cmp_v", "merged", "h", "ff", "gates", "arg_k", "arg_v")}
        cmp_normed = sem("cmp_normed")
        h_rstd = sem("h_rstd")
        h_ms, h_pow, cmp_rstd = sem("h_ms"), sem("h_pow"), sem("cmp_rstd")
        out_ready, stored = sem("out_ready"), sem("stored")

        block = ctx.enter_context(nc.Block())

        LHS = {"x": (xT_hi, xT_lo), "cq": latT[0], "ckv": latT[1], "fk": fk, "fv": fv, "om": om, "on": on, "m": mT, "ff": fT}

        def lhsT(u, part, c, t):
            if u.lhs == "hk":
                return hT[part][:, c, :]
            if u.lhs == "hv":
                return hT[part][:, HID_K // P + c, :]
            if u.lhs in ("fk", "fv"):
                return LHS[u.lhs][part][:, c, :]
            return LHS[u.lhs][part][:, c, t * P:(t + 1) * P]

        def pieces(u, i, k):
            r0, r1 = u.chunk * u.rows, (u.chunk + u.m) * u.rows
            step = u.step
            dst = raw[0:u.rows, k, 0:u.m * u.width].rearrange("p (c n) -> p c n", c=u.m)

            def src(name, col, width):
                w = A[name][r0:r1]
                w = w[:, bass.ds(i * step + col, width)] if step else w[:, col:col + width]
                return w.rearrange("(c p) n -> p c n", p=u.rows)

            if u.weight == "kr_gates":
                g = HEADS * 3
                return [(dst[:, :, 0:MLA_ROT], src("w_in", O_KR, MLA_ROT)),
                        (dst[:, :, MLA_ROT:], src("w_in", O_GN, g))]
            if u.weight in ("ks_kw", "vs_vw"):
                s0, w0 = (O_KS, O_KW) if u.weight == "ks_kw" else (O_VS, O_VW)
                n = u.width // 2
                return [(dst[:, :, 0:n], src("w_in", s0, n)), (dst[:, :, n:], src("w_in", w0, n))]
            c0 = u.col + u.start
            if u.m % 2:
                n = u.width // 2
                return [(dst[:, :, 0:n], src(u.weight, c0, n)), (dst[:, :, n:], src(u.weight, c0 + n, n))]
            w, n = src(u.weight, c0, u.width), u.m // 2
            return [(dst[:, 0:n, :], w[:, 0:n, :]), (dst[:, n:, :], w[:, n:, :])]

        def slot_of(s, more=0):
            assert s.per.get("unit", 0) % RING == 0
            return (s.base.get("unit", 0) + more) % RING

        def halves(u):
            b = BANK[u.bank]
            if u.lhs == "fk":
                return [(0, 0, 512, b[0]), (0, 512, HID_K, b[1])]
            if u.lhs in ("fv", "hk", "hv"):
                return [(0, 0, u.width, b[0])]
            return [(t, 0, u.width, b[t]) for t in range(TT)]

        @block.sync
        def _(sp):
            for q in range(NT):
                sp.dma_start(x_sb[:, :, q * N:(q + 1) * N], A["x"].rearrange("(t p) n -> p t n", p=P)[:, :, q * N:(q + 1) * N]).then_inc(x_in[q], 16)
            for u, i in walk(sp, PH):
                if u.kind != "unit":
                    continue
                k = slot_of(u)
                wait(sp, split, count(u, i, "unit", 1 - RING))
                for dst, src in pieces(u, i, k):
                    sp.dma_start(dst, src).then_inc(loaded[k], 16)

        for n, ph in enumerate(PH):
            us = [s for s in ph.steps if s.kind == "unit"]
            nxt = []
            for q in PH[n + 1:]:
                nxt += [s for s in q.steps if s.kind == "unit"]
                if len(nxt) >= AHEAD:
                    break
            for j, s in enumerate(us):
                if j + AHEAD < len(us):
                    t = us[j + AHEAD]
                    s.ahead = (t.rows, t.m * t.width)
                elif ph.times > 1:
                    s.ahead = (P, SLOT)
                elif j + AHEAD - len(us) < len(nxt):
                    t = nxt[j + AHEAD - len(us)]
                    s.ahead = (t.rows, t.m * t.width)
                else:
                    s.ahead = None

        def load_count(s, i, more):
            n = s.base.get("unit", 0) + more
            per = s.per.get("unit", 0)
            v = 32 * (n // RING + 1)
            return i * (32 * per // RING) + v if per else v

        def split_hi(act, s, i, more, rows, n):
            k = slot_of(s, more)
            act.wait_ge(loaded[k], load_count(s, i, more))
            wait(act, used, count(s, i, "unit", more + 1 - RING))
            nc.scalar.activation(whi[0:rows, k, 0:n], raw[0:rows, k, 0:n], ACT.Copy).then_inc(hi_made, 1)

        def split_lo(dve, s, i, more, rows, n):
            k = slot_of(s, more)
            wait(dve, hi_made, count(s, i, "unit", more + 1))
            nc.vector.tensor_tensor(wlo[0:rows, k, 0:n], raw[0:rows, k, 0:n], whi[0:rows, k, 0:n].bitcast(F32),
                                    ALU.subtract).then_inc(split, 1)

        FB = [QT, TP, S, OP]
        PAIRED = ("turn_merged", "turn_h", "turn_ff")

        def bank_of_queries(s):
            return "AB"[(s.h == 0) == (s.which == "mla")]

        def head_view(which):
            return (qk_m, qkT_m, rot_m, MLA_NOPE, MLA_ROT // 2) if which == "mla" else (qk_n, qkT_n, rot_n, 0, NSA_ROT // 2)

        def query(s):
            return s.job if s.which == "mla" else s.job // 2

        def branches(s):
            b = [(0, P, 0), (P, 3 * P, 1)]
            return b + [(3 * P, 3 * P + CROWS, s.job % 2)] if s.which == "nsa" else b

        def order(s):
            if s.which == "mla":
                return (0, 1)
            return (1, 2, 0) if s.job % 2 else (0, 1, 2)

        @block.scalar
        def _(act):
            consts = (
                (rows_sb[0:KD, :], A["attn_norm_g"].rearrange("(c p) -> c p", p=P)),
                (rows_sb[KD:2 * KD, :], A["ffn_norm_g"].rearrange("(c p) -> c p", p=P)),
                (pe_k_sb[:], A["cmp_pe_k"]), (pe_v_sb[:], A["cmp_pe_v"]), (ident[:], A["ident"]),
                (identb[:], A["identb"]), (maskb[:], A["maskb"]),
                (cmaskb[:], A["cmaskb"].rearrange("(t p) g c -> p t g c", p=P)),
                (cos_m[:], A["cos_m"].rearrange("(t p) c -> p t c", p=P)), (sin_m[:], A["sin_m"].rearrange("(t p) c -> p t c", p=P)),
                (cos_n[:], A["cos_n"].rearrange("(t p) c -> p t c", p=P)), (sin_n[:], A["sin_n"].rearrange("(t p) c -> p t c", p=P)),
                (cos_c[:], A["cos_c"]), (sin_c[:], A["sin_c"]),
                (g_head[:, 0, :], A["mla_q_norm_g"].partition_broadcast(P)), (g_head[:, 1, :], A["mla_k_norm_g"].partition_broadcast(P)),
                (g_head[:, 2, :], A["nsa_q_norm_g"].partition_broadcast(P)),
                (g_head[:, 3, :], A["nsa_k_norm_g"][0].partition_broadcast(P)),
                (g_head[:, 4, :], A["nsa_k_norm_g"][1].partition_broadcast(P)),
                (g_head[:, 5, :], A["nsa_k_norm_g"][2].partition_broadcast(P)),
                (g_lat[:, 0, :], A["mla_q_lat_g"].partition_broadcast(P)), (g_lat[:, 1, :], A["mla_kv_lat_g"].partition_broadcast(P)),
            )
            assert len(consts) == NCONST
            for n, (dst, src) in enumerate(consts):
                act.dma_start(dst, src).then_inc(const0 if n < NFIRST else const, 16)

            def copy(dst, src, **kw):
                return nc.scalar.activation(dst, src, ACT.Copy, **kw)

            def turn_split(s, i, src, hi, gain=None):
                wait(act, filled, count(s, i, "fill", 1))
                for c in range(src.shape[1]):
                    kw = {"scale": gain[:, c:c + 1]} if gain is not None else {}
                    ins = copy(hi[:, c, :], src[:, c, :], **kw)
                ins.then_inc(fill_hi, 1)

            first = True
            for s, i in walk(act, PH):
                k = s.kind
                if k == "unit":
                    if first:
                        for m in range(AHEAD):
                            split_hi(act, s, i, m, P, SLOT)
                        first = False
                    if s.ahead:
                        split_hi(act, s, i, AHEAD, *s.ahead)
                elif k == "turn_x":
                    f = FB[s.bank][:, :].rearrange("p (c n) -> p c n", c=2)
                    act.wait_ge(fill_out, 1)
                    turn_split(s, i, f, xT_hi[:, 2 * s.pair:2 * s.pair + 2, :], gcols[:, 2 * s.pair:2 * s.pair + 2])
                elif k == "done_kv":
                    act.wait_ge(x_rstd, 1)
                    act.wait_ge(used, count(s, i, "unit"))
                    for t in range(TT):
                        ins = copy(kv[:, t, s.off:s.off + s.w], BANK[s.bank][t][:, 0:s.w], scale=rx[:, t:t + 1])
                    ins.then_inc(free[s.bank], 1)
                elif k == "done_krg":
                    act.wait_ge(used, count(s, i, "unit"))
                    for t in range(TT):
                        copy(kr[:, t, :], BANK[s.bank][t][:, 0:MLA_ROT], scale=rx[:, t:t + 1])
                        ins = nc.scalar.activation(gsig[:, t * 48:t * 48 + 48], BANK[s.bank][t][:, MLA_ROT:MLA_ROT + 48],
                                                   ACT.Tanh, scale=hrx[:, t:t + 1])
                    ins.then_inc(free[s.bank], 1)
                elif k == "done_lat":
                    act.wait_ge(used, count(s, i, "unit"))
                    for t in range(TT):
                        ins = copy(lat[:, t, s.which, :], BANK[s.bank][t][:, :], scale=rx[:, t:t + 1])
                    ins.then_inc(free[s.bank], 1)
                elif k == "turn_kc":
                    wait(act, filled, count(s, i, "fill", 1))
                    copy(kc_turned[:, s.slot, :, :].rearrange("p c n -> p (c n)"), QT[0:HALF, :]).then_inc(fill_out, 1)
                elif k == "turn_vc":
                    wait(act, filled, count(s, i, "fill", 1))
                    copy(vc_turned[:, 2 * s.slot:2 * s.slot + 2, :].rearrange("p c n -> p (c n)"), QT[:, :]).then_inc(fill_out, 1)
                elif k == "flat":
                    act.wait_ge(flat_made, count(s, i, "flat", 1))
                    if s.which == "v":
                        copy(fv[0][:], flat[:]).then_inc(flat_hi, 1)
                    else:
                        c = int(s.which[1])
                        copy(fk[0][:, c::2, :], flat[0:HALF]).then_inc(flat_hi, 1)
                elif k == "turn_lat":
                    turn_split(s, i, QT[:, :].rearrange("p (c n) -> p c n", c=2), latT[s.which][0][:, 2 * s.pair:2 * s.pair + 2, :])
                elif k in ("done_hidden_k", "done_hidden_v"):
                    kk = k[-1]
                    cols = slice(0, HID_K) if kk == "k" else slice(HID_K, HID_K + HID_V)
                    act.wait_ge(made["arg_" + kk], 1)
                    nc.scalar.activation(hid_a[:, cols], hid_a[:, cols], ACT.Tanh,
                                         scale=0.7978845608028654).then_inc(acted["hidden_" + kk], 1)
                elif k == "turn_hidden":
                    wait(act, filled, count(s, i, "fill", 1))
                    n = s.c1 - s.c0
                    copy(hT[0][:, s.c0:s.c1, :], QT[:, 0:n * CROWS].rearrange("p (c n) -> p c n", c=n)).then_inc(fill_hi, 1)
                elif k == "turn_cmp":
                    wait(act, filled, count(s, i, "fill", 1))
                    copy(kcT[:], QT[0:HALF, 0:2 * CROWS].rearrange("p (c n) -> p c n", c=2)).then_inc(fill_out, 1)
                elif k == "done_mla_k":
                    act.wait_ge(used, count(s, i, "unit"))
                    for t in range(TT):
                        ins = copy(qk_m[:, t, 4:8, 0:MLA_NOPE], BANK[s.bank][t][:, :].rearrange("p (h n) -> p h n", h=HPG))
                    ins.then_inc(free[s.bank], 1)
                elif k == "done_mla_q":
                    act.wait_ge(used, count(s, i, "unit"))
                    for t in range(TT):
                        ins = copy(qk_m[:, t, s.h:s.h + 2, :], BANK[s.bank][t][:, 0:2 * DK].rearrange("p (h n) -> p h n", h=2))
                    ins.then_inc(free[s.bank], 1)
                elif k == "done_mla_v":
                    act.wait_ge(used, count(s, i, "unit"))
                    for t in range(TT):
                        ins = copy(v_m[:, t, :, :], BANK[s.bank][t][:, :].rearrange("p (h n) -> p h n", h=HPG))
                    ins.then_inc(free[s.bank], 1)
                elif k in ("done_nsa_k", "done_nsa_q"):
                    act.wait_ge(used, count(s, i, "unit"))
                    h0 = 4 if k == "done_nsa_k" else s.h
                    for t in range(TT):
                        ins = copy(qk_n[:, t, h0:h0 + 2, :], BANK[s.bank][t][:, 0:2 * DK].rearrange("p (h n) -> p h n", h=2),
                                   scale=rx[:, t:t + 1])
                    ins.then_inc(free[s.bank], 1)
                elif k == "done_nsa_v":
                    act.wait_ge(used, count(s, i, "unit"))
                    for t in range(TT):
                        ins = copy(v_n[:, t, :, :], BANK[s.bank][t][:, 0:2 * DV].rearrange("p (h n) -> p h n", h=2),
                                   scale=rx[:, t:t + 1])
                    ins.then_inc(free[s.bank], 1)
                elif k == "done_gate_m":
                    act.wait_ge(used, count(s, i, "unit"))
                    for t in range(TT):
                        ins = nc.scalar.activation(M[:, t, bass.ds(i * N, N)], BANK[s.bank][t][:, :], ACT.Tanh, scale=hrx[:, t:t + 1])
                    ins.then_inc(free[s.bank], 1)
                elif k == "done_gate_n":
                    act.wait_ge(used, count(s, i, "unit"))
                    for t in range(TT):
                        ins = nc.scalar.activation(mt[:, t, :], BANK[s.bank][t][:, :], ACT.Tanh, scale=hrx[:, t:t + 1])
                    ins.then_inc(free[s.bank], 1)
                elif k == "turn_heads":
                    act.wait_ge(filled, count(s, i, "fill", 1))
                    copy(head_view(s.which)[1][:, s.lo, :], QT[0:HALF, :]).then_inc(fill_out, 1)
                elif k == "scores":
                    Pb = Pbs[:, s.job % 2, :]
                    act.wait_ge(negmax, count(s, i, "scores", 1))
                    for n, (c0, c1, tile) in enumerate(branches(s)):
                        m = 2 * query(s) + tile
                        o = order(s)[n]
                        ins = nc.scalar.activation(Pb[:, c0:c1], S[:, c0:c1], ACT.Exp, bias=nm[:, o:o + 1], scale=rq[:, m:m + 1],
                                                   accum_out=sm[:, n:n + 1])
                    ins.then_inc(exped, 1)
                elif k == "turn_probs":
                    act.wait_ge(turned, count(s, i, "turn_probs", 1))
                    if s.which == "mla":
                        copy(pT[:, 0:3 * P], TP[:, 0:3 * P]).then_inc(pt_out, 1)
                    else:
                        copy(pT[:, 0:3 * P], TP[:, 0:3 * P])
                        copy(pT[0:CROWS, 3 * P:4 * P], TP[0:CROWS, 3 * P:4 * P]).then_inc(pt_out, 1)
                elif k == "values":
                    if s.last:
                        act.wait_ge(valued, count(s, i, "values", 1))
                        r = s.job if s.which == "mla" else s.job // 2
                        o = (om if s.which == "mla" else on)[0]
                        copy(o[:, bass.ds(i * HPG + r, 1), :].rearrange("p a n -> p (a n)"), OP[:, 0:SEQ]).then_inc(o_hi, 1)
                elif k == "turn_merged":
                    hi = mT[0]
                    c0 = (i * 4 if s.tile is None else s.tile * 4) + 2 * s.pair
                    turn_split(s, i, FB[s.pair][:, :].rearrange("p (c n) -> p c n", c=2), hi[:, bass.ds(c0, 2), :])
                elif k == "turn_h":
                    c0 = s.tile * 4 + 2 * s.pair
                    turn_split(s, i, FB[s.pair][:, :].rearrange("p (c n) -> p c n", c=2), xT_hi[:, c0:c0 + 2, :], gcols[:, KD + c0:KD + c0 + 2])
                elif k == "turn_ff":
                    c0 = (i * 4 if s.tile is None else s.tile * 4) + 2 * s.pair
                    turn_split(s, i, FB[s.pair][:, :].rearrange("p (c n) -> p c n", c=2), fT[0][:, bass.ds(c0, 2), :])
                elif k == "done_ff_gate":
                    act.wait_ge(h_rstd, 1)
                    act.wait_ge(used, count(s, i, "unit"))
                    act.wait_ge(filled, count(s, i, "fill"))
                    for t in range(TT):
                        ins = nc.scalar.activation(ft[:, t, :], BANK["A"][t][:, :], ACT.Tanh, scale=rh2[:, t:t + 1])
                    ins.then_inc(acted["ff"], 1)
                elif k == "load_b":
                    act.wait_ge(flat_out, 3)
                    for dst, src in ((b1[:, 0:HID_K], A["cmp_k_b1"]), (b1[:, HID_K:], A["cmp_v_b1"]),
                                     (b2[:, 0:DK], A["cmp_k_b2"]), (b2[:, DK:], A["cmp_v_b2"])):
                        act.dma_start(dst, src.partition_broadcast(CROWS)).then_inc(bias_in, 16)
                elif k == "load_x":
                    act.wait_ge(valued, count(s, i, "values"))
                    act.dma_start(h[:], A["x"].rearrange("(t p) n -> p t n", p=P)).then_inc(xt_in, 16)
                elif k == "done_down":
                    act.wait_ge(free[s.bank], count(s, i, "tile" + s.bank, 1))
                    cols = slice(s.tile * N, (s.tile + 1) * N)
                    act.dma_start(out.rearrange("(t p) n -> p t n", p=P)[:, :, cols], h[:, :, cols]).then_inc(stored, 16)
            act.wait_ge(stored, 16 * NT)

        @block.vector
        def _(dve):
            def fence():
                nc.vector.drain()

            def turn_split(s, i, src, hi, lo, gain=None):
                wait(dve, fill_hi, count(s, i, "sfill", 1))
                for c in range(src.shape[1]):
                    if gain is None:
                        ins = nc.vector.tensor_tensor(lo[:, c, :], src[:, c, :], hi[:, c, :].bitcast(F32), ALU.subtract)
                    else:
                        ins = nc.vector.scalar_tensor_tensor(out=lo[:, c, :], in0=src[:, c, :], scalar=gain[:, c:c + 1],
                                                             in1=hi[:, c, :].bitcast(F32), op0=ALU.mult, op1=ALU.subtract)
                ins.then_inc(fill_out, 1)

            def square_sum(x, acc, j):
                wide = not isinstance(j, int)
                nc.vector.tensor_tensor_reduce(j if wide else junk[0:x.shape[0], j, 0:x.shape[1]], x, x, 1.0, 0.0, ALU.mult, ALU.add, acc)
                if wide:
                    fence()

            nc.vector.memset(junk[:, 0, 0:8], 0.0).then_inc(o_free, 1)
            fence()
            for q in range(NT):
                dve.wait_ge(x_in[q], 16)
                for t in range(TT):
                    square_sum(x_sb[:, t, q * N:(q + 1) * N], hss[:, t * NT + q:t * NT + q + 1], rot[:].rearrange("p a n -> p (a n)"))
            nc.vector.tensor_reduce(msx, hss.rearrange("p (t n) -> p t n", t=TT), AXX, ALU.add)
            fence()
            nc.vector.tensor_scalar(msx, msx, 1.0 / D, EPS, ALU.mult, ALU.add).then_inc(ms_x, 1)
            first = True
            for s, i in walk(dve, PH):
                k = s.kind
                if k == "unit":
                    if first:
                        for m in range(AHEAD):
                            split_lo(dve, s, i, m, P, SLOT)
                        first = False
                    if s.ahead:
                        split_lo(dve, s, i, AHEAD, *s.ahead)
                elif k == "setup":
                    dve.wait_ge(filled, 1)
                    nc.vector.tensor_copy(gcols[:], QT[:, 0:2 * KD])
                    nc.vector.tensor_copy(peT_k[:], QT[0:HALF, 32:96].rearrange("p (c n) -> p c n", c=2))
                    nc.vector.tensor_copy(peT_v[:], QT[:, 96:128]).then_inc(fill_out, 1)
                elif k == "turn_x":
                    f = FB[s.bank][:, :].rearrange("p (c n) -> p c n", c=2)
                    c0 = 2 * s.pair
                    turn_split(s, i, f, xT_hi[:, c0:c0 + 2, :], xT_lo[:, c0:c0 + 2, :], gcols[:, c0:c0 + 2])
                    if s.pair == KD // 2 - 1:
                        dve.wait_ge(x_rstd, 1)
                        nc.vector.tensor_scalar(hrx, rx, 0.5, None, ALU.mult)
                        fence()
                elif k == "done_krg":
                    dve.wait_ge(free[s.bank], count(s, i, "tile" + s.bank, 1))
                    nc.vector.tensor_scalar(gsig, gsig, 0.5, 0.5, ALU.mult, ALU.add)
                    fence()
                    gv = gsig.rearrange("p (t h b) -> p t h b", t=TT, b=3)
                    for j in range(2):
                        for t in range(TT):
                            nc.vector.tensor_copy(gates[:, :, j, t:t + 1], gv[:, t, :, 1 + j:2 + j])
                        nc.vector.tensor_copy(gates[:, :, j, 2:3], gv[:, j, :, 0:1])
                elif k == "flat":
                    dve.wait_ge(fill_out, count(s, i, "fill"))
                    wait(dve, flat_out, count(s, i, "flat"))
                    n = P if s.which == "v" else HALF
                    if s.which == "v":
                        src, pe = vc_turned, peT_v[:, :]
                    else:
                        c = int(s.which[1])
                        src, pe = kc_turned[:, :, c, :], peT_k[:, c, :]
                    for half in range(2):
                        a = src[:, :, half * CMP_STRIDE:half * CMP_STRIDE + NCMP * CMP_STRIDE].rearrange("p g (b l) -> p l g b", l=CMP_STRIDE)
                        l0 = half * CMP_STRIDE
                        ins = nc.vector.tensor_tensor(flat[0:n, l0:l0 + CMP_STRIDE, :].rearrange("p l (g b) -> p l g b", g=GROUPS), a,
                                                      pe[:, l0:l0 + CMP_STRIDE].unsqueeze(2).unsqueeze(3).to_broadcast([n, CMP_STRIDE, GROUPS, NCMP]),
                                                      ALU.add)
                    ins.then_inc(flat_made, 1)
                    dve.wait_ge(flat_hi, count(s, i, "flat", 1))
                    if s.which == "v":
                        hi, lo = fv[0][:], fv[1][:]
                    else:
                        hi, lo = fk[0][:, c::2, :], fk[1][:, c::2, :]
                    nc.vector.tensor_tensor(lo, flat[0:n], hi.bitcast(F32), ALU.subtract).then_inc(flat_out, 1)
                elif k == "lat_a":
                    b = "AB"[s.which]
                    dve.wait_ge(free[b], count(s, i, "tile" + b))
                    for t in range(TT):
                        square_sum(lat[:, t, s.which, :], ms[:, t:t + 1], rot[:].rearrange("p a n -> p (a n)"))
                    nc.vector.tensor_scalar(ms[:, 0:2], ms[:, 0:2], 1.0 / RANK, EPS, ALU.mult, ALU.add).then_inc(ms_ready, 1)
                elif k == "lat_b":
                    dve.wait_ge(rstd_ready, count(s, i, "ms"))
                    if s.which == 0:
                        dve.wait_ge(const, 16 * (NCONST - NFIRST))
                    for t in range(TT):
                        ins = nc.vector.scalar_tensor_tensor(out=lat[:, t, s.which, :], in0=lat[:, t, s.which, :], scalar=rs[:, t:t + 1],
                                                             in1=g_lat[:, s.which, :], op0=ALU.mult, op1=ALU.mult)
                    ins.then_inc(scaled, 1)
                elif k == "turn_lat":
                    p2 = slice(2 * s.pair, 2 * s.pair + 2)
                    turn_split(s, i, QT[:, :].rearrange("p (c n) -> p c n", c=2), latT[s.which][0][:, p2, :], latT[s.which][1][:, p2, :])
                elif k in ("done_hidden_k", "done_hidden_v"):
                    kk = k[-1]
                    c0, n = (0, HID_K) if kk == "k" else (HID_K, HID_V)
                    x, a = hid[:, c0:c0 + n], hid_a[:, c0:c0 + n]
                    dve.wait_ge(used, count(s, i, "unit"))
                    dve.wait_ge(bias_in, 64)
                    for b, o in enumerate(range(0, n, 512)):
                        w = min(512, n - o)
                        ins = nc.vector.tensor_tensor(hid[:, c0 + o:c0 + o + w], BANK[s.bank][b][0:CROWS, 0:w], b1[:, c0 + o:c0 + o + w], ALU.add)
                    ins.then_inc(free[s.bank], 1)
                    fence()
                    nc.vector.tensor_tensor(a, x, x, ALU.mult)
                    fence()
                    nc.vector.tensor_scalar(a, a, 0.044715, 1.0, ALU.mult, ALU.add)
                    fence()
                    nc.vector.tensor_tensor(a, a, x, ALU.mult).then_inc(made["arg_" + kk], 1)
                    dve.wait_ge(acted["hidden_" + kk], 1)
                    nc.vector.tensor_scalar(a, a, 0.5, 0.5, ALU.mult, ALU.add)
                    fence()
                    nc.vector.tensor_tensor(x, a, x, ALU.mult).then_inc(made["hidden_" + kk], 1)
                    fence()
                elif k == "turn_hidden":
                    n = s.c1 - s.c0
                    wait(dve, fill_hi, count(s, i, "sfill", 1))
                    nc.vector.tensor_tensor(hT[1][:, s.c0:s.c1, :], QT[:, 0:n * CROWS].rearrange("p (c n) -> p c n", c=n),
                                            hT[0][:, s.c0:s.c1, :].bitcast(F32), ALU.subtract).then_inc(fill_out, 1)
                elif k == "done_cmp_k":
                    dve.wait_ge(used, count(s, i, "unit"))
                    nc.vector.tensor_tensor(kc[:], BANK[s.bank][0][0:CROWS, 0:DK], b2[:, 0:DK], ALU.add).then_inc(free[s.bank], 1)
                    fence()
                    square_sum(kc[:], ms[0:CROWS, 0:1], 0)
                    fence()
                    nc.vector.tensor_scalar(ms[0:CROWS, 0:1], ms[0:CROWS, 0:1], 1.0 / DK, EPS, ALU.mult, ALU.add).then_inc(made["cmp_k"], 1)
                elif k == "done_cmp_v":
                    dve.wait_ge(used, count(s, i, "unit"))
                    nc.vector.tensor_tensor(v_c[:], BANK[s.bank][0][0:CROWS, 0:DV], b2[:, DK:], ALU.add).then_inc(free[s.bank], 1)
                elif k == "cmp_norm":
                    dve.wait_ge(cmp_rstd, 1)
                    nc.vector.scalar_tensor_tensor(out=kc[:], in0=kc[:], scalar=rs[0:CROWS, 0:1], in1=g_head[0:CROWS, 3, :],
                                                   op0=ALU.mult, op1=ALU.mult)
                    fence()
                    hw = NSA_ROT // 2
                    x1, x2 = kc[:, 0:hw], kc[:, hw:2 * hw]
                    t = [rot[0:CROWS, 2, 32 * q:32 * q + hw] for q in range(4)]
                    for q, (xx, cs) in enumerate(((x1, cos_c), (x2, sin_c), (x2, cos_c), (x1, sin_c))):
                        nc.vector.tensor_tensor(t[q], xx, cs[:], ALU.mult)
                    fence()
                    nc.vector.tensor_tensor(x1, t[0], t[1], ALU.subtract)
                    nc.vector.tensor_tensor(x2, t[2], t[3], ALU.add).then_inc(cmp_normed, 1)
                    fence()
                elif k == "gains":
                    dve.wait_ge(const, 16 * (NCONST - NFIRST))
                    def with_query(kg, qg, rotated, plain):
                        nc.vector.scalar_tensor_tensor(out=g_head[:, kg, plain], in0=g_head[:, kg, plain], scalar=SCALE, in1=g_head[:, qg, plain],
                                                       op0=ALU.mult, op1=ALU.mult)
                        nc.vector.tensor_scalar(g_head[:, kg, rotated], g_head[:, kg, rotated], SCALE, None, ALU.mult)

                    def rotation(table, cos, sin, g, start, hw):
                        for n, (cs, g0) in enumerate(((cos, start), (sin, start + hw), (cos, start + hw), (sin, start))):
                            nc.vector.tensor_tensor(table[:, n, :, :], cs[:], g_head[:, g, g0:g0 + hw].unsqueeze(1).to_broadcast([P, TT, hw]), ALU.mult)
                    with_query(1, 0, slice(MLA_NOPE, DK), slice(0, MLA_NOPE))
                    for kg in (3, 4, 5):
                        with_query(kg, 2, slice(0, NSA_ROT), slice(NSA_ROT, DK))
                    rotation(rot_m, cos_m, sin_m, 0, MLA_NOPE, MLA_ROT // 2)
                    rotation(rot_n, cos_n, sin_n, 2, 0, NSA_ROT // 2)
                    fence()
                    hw = MLA_ROT // 2
                    for t in range(TT):
                        square_sum(kr[:, t, :], ms_kr[:, t:t + 1], t)
                    fence()
                    nc.vector.tensor_tensor(kr[:], kr[:], g_head[:, 1, MLA_NOPE:DK].unsqueeze(1).to_broadcast([P, TT, MLA_ROT]), ALU.mult)
                    fence()
                    x1, x2 = kr[:, :, 0:hw], kr[:, :, hw:2 * hw]
                    q4 = [junk[:, q, 0:TT * hw].rearrange("p (t n) -> p t n", t=TT) for q in range(4)]
                    for q, (xx, cs) in enumerate(((x1, cos_m), (x2, sin_m), (x2, cos_m), (x1, sin_m))):
                        nc.vector.tensor_tensor(q4[q], xx, cs[:], ALU.mult)
                    fence()
                    nc.vector.tensor_tensor(x1, q4[0], q4[1], ALU.subtract)
                    nc.vector.tensor_tensor(x2, q4[2], q4[3], ALU.add)
                    fence()
                elif k == "k_sq":
                    X = head_view(s.which)[0]
                    dve.wait_ge(free["A"], count(s, i, "tileA"))
                    n, w = (HPG, MLA_NOPE) if s.which == "mla" else (2, DK)
                    for t in range(TT):
                        for q in range(n):
                            square_sum(X[:, t, 4 + q, 0:w], ms[:, t * n + q:t * n + q + 1], (t * n + q) % 4)
                        if n == 4 or t == 1:
                            fence()
                    if s.which == "mla":
                        for t in range(TT):
                            nc.vector.tensor_scalar(ms[:, t * n:t * n + n], ms[:, t * n:t * n + n], ms_kr[:, t:t + 1], None, ALU.add)
                        fence()
                    nc.vector.tensor_scalar(ms[:, 0:TT * n], ms[:, 0:TT * n], 1.0 / DK, EPS, ALU.mult, ALU.add).then_inc(ms_ready, 1)
                elif k == "k_scale":
                    X = head_view(s.which)[0]
                    n, w = (HPG, MLA_NOPE) if s.which == "mla" else (2, DK)
                    dve.wait_ge(rstd_ready, count(s, i, "ms"))
                    for t in range(TT):
                        for q in range(n):
                            x = X[:, t, 4 + q, 0:w]
                            ins = nc.vector.scalar_tensor_tensor(out=x, in0=x, scalar=rs[:, t * n + q:t * n + q + 1],
                                                                 in1=g_head[:, 1 if s.which == "mla" else 4 + q, 0:w],
                                                                 op0=ALU.mult, op1=ALU.mult)
                    ins.then_inc(scaled, 1)
                elif k == "q_sq":
                    X = head_view(s.which)[0]
                    b = bank_of_queries(s)
                    dve.wait_ge(free[b], count(s, i, "tile" + b))
                    m = ms_q[:, 2 * s.h:2 * s.h + 4]
                    for q in range(2):
                        for t in range(TT):
                            square_sum(X[:, t, s.h + q, :], m[:, 2 * q + t:2 * q + t + 1], 2 * q + t)
                    fence()
                    nc.vector.tensor_scalar(m, m, 1.0 / DK, EPS, ALU.mult, ALU.add).then_inc(ms_ready, 1)
                elif k == "turn_heads":
                    dve.wait_ge(filled, count(s, i, "fill", 2))
                    nc.vector.tensor_copy(head_view(s.which)[1][:, s.hi, :], TP[0:HALF, :]).then_inc(fill_out, 1)
                elif k == "scores":
                    dve.wait_ge(scored, count(s, i, "scores", 1))
                    dve.wait_ge(rstd_ready, count(s, i, "ms"))
                    br = branches(s)
                    for (c0, c1, _), o in zip(br, order(s)):
                        nc.vector.tensor_reduce(mx[:, o:o + 1], S[:, c0:c1], AXX, ALU.max)
                    fence()
                    r, start = query(s), s.job % 2 if s.which == "nsa" else 0
                    nc.vector.scalar_tensor_tensor(out=nm[:, 0:len(br)], in0=mx[:, 0:len(br)], scalar=LOWEST,
                                                   in1=neg_rq[:, r, start:start + len(br)], op0=ALU.max, op1=ALU.mult).then_inc(negmax, 1)
                elif k == "probs":
                    Pb = Pbs[:, s.job % 2, :]
                    dve.wait_ge(exped, count(s, i, "probs", 1))
                    n = 2 if s.which == "mla" else 3
                    nc.vector.tensor_scalar(rc[:, 0:n], sm[:, 0:n], 1e-30, None, ALU.max)
                    fence()
                    nc.vector.reciprocal(rc[:, 0:n], rc[:, 0:n])
                    fence()
                    if s.which == "nsa":
                        g = gates[:, bass.ds(i * HPG + s.job // 2, 1), s.job % 2, :].rearrange("p a n -> p (a n)")
                        nc.vector.tensor_tensor(rc[:, 0:n], rc[:, 0:n], g, ALU.mult)
                        fence()
                        nc.vector.tensor_scalar(Pb[:, 3 * P:3 * P + CROWS], Pb[:, 3 * P:3 * P + CROWS], rc[:, 2:3], None, ALU.mult)
                    nc.vector.tensor_scalar(Pb[:, 0:P], Pb[:, 0:P], rc[:, 0:1], None, ALU.mult)
                    nc.vector.tensor_scalar(Pb[:, P:3 * P], Pb[:, P:3 * P], rc[:, 1:2], None, ALU.mult).then_inc(probs, 1)
                elif k == "values":
                    if s.last:
                        dve.wait_ge(o_hi, count(s, i, "head", 1))
                        r = s.job if s.which == "mla" else s.job // 2
                        o = om if s.which == "mla" else on
                        hi, lo = (o[q][:, bass.ds(i * HPG + r, 1), :].rearrange("p a n -> p (a n)") for q in range(2))
                        nc.vector.tensor_tensor(lo, OP[:, 0:SEQ], hi.bitcast(F32), ALU.subtract).then_inc(o_free, 1)
                elif k == "done_gate_m":
                    dve.wait_ge(free[s.bank], count(s, i, "tile" + s.bank, 1))
                    m = M[:, :, bass.ds(i * N, N)]
                    nc.vector.tensor_scalar(m, m, 0.5, 0.5, ALU.mult, ALU.add)
                elif k == "done_y_m":
                    dve.wait_ge(used, count(s, i, "unit"))
                    for t in range(TT):
                        m = M[:, t, bass.ds(i * N, N)]
                        ins = nc.vector.tensor_tensor(m, BANK[s.bank][t][:, :], m, ALU.mult)
                    ins.then_inc(free[s.bank], 1)
                elif k == "done_gate_n":
                    dve.wait_ge(free[s.bank], count(s, i, "tile" + s.bank, 1))
                    nc.vector.tensor_scalar(mt[:], mt[:], 0.5, 0.5, ALU.mult, ALU.add)
                    fence()
                elif k == "done_y_n":
                    dve.wait_ge(used, count(s, i, "unit"))
                    for t in range(TT):
                        ins = nc.vector.tensor_tensor(mt[:, t, :], BANK[s.bank][t][:, :], mt[:, t, :], ALU.mult)
                    ins.then_inc(free[s.bank], 1)
                    fence()
                    m = M[:, :, bass.ds(i * N + N * s.tile, N)] if s.tile else M[:, :, 0:N]
                    nc.vector.tensor_tensor(mt[:], mt[:], m, ALU.add).then_inc(made["merged"], 1)
                elif k == "turn_merged":
                    c0 = (i * 4 if s.tile is None else s.tile * 4) + 2 * s.pair
                    turn_split(s, i, FB[s.pair][:, :].rearrange("p (c n) -> p c n", c=2), mT[0][:, bass.ds(c0, 2), :], mT[1][:, bass.ds(c0, 2), :])
                elif k == "done_h":
                    dve.wait_ge(used, count(s, i, "unit"))
                    dve.wait_ge(xt_in, 16)
                    for t in range(TT):
                        hh = h[:, t, s.tile * N:(s.tile + 1) * N]
                        ins = nc.vector.tensor_tensor(hh, BANK[s.bank][t][:, :], hh, ALU.add)
                    ins.then_inc(free[s.bank], 1)
                    fence()
                    for t in range(TT):
                        square_sum(h[:, t, s.tile * N:(s.tile + 1) * N], hss[:, t * NT + s.tile:t * NT + s.tile + 1],
                                   rot[:].rearrange("p a n -> p (a n)"))
                elif k == "turn_h":
                    c0 = s.tile * 4 + 2 * s.pair
                    turn_split(s, i, FB[s.pair][:, :].rearrange("p (c n) -> p c n", c=2), xT_hi[:, c0:c0 + 2, :], xT_lo[:, c0:c0 + 2, :],
                               gcols[:, KD + c0:KD + c0 + 2])
                elif k == "h_norm":
                    nc.vector.tensor_reduce(msh, hss.rearrange("p (t n) -> p t n", t=TT), AXX, ALU.add)
                    fence()
                    nc.vector.tensor_scalar(msh, msh, 1.0 / D, EPS, ALU.mult, ALU.add).then_inc(h_ms, 1)
                    dve.wait_ge(h_pow, 1)
                    nc.vector.tensor_scalar(rh2, rh, 0.5, None, ALU.mult)
                    fence()
                    nc.vector.tensor_tensor(hs2, rh, rh2, ALU.mult).then_inc(h_rstd, 1)
                elif k == "done_ff_gate":
                    dve.wait_ge(acted["ff"], count(s, i, "ff", 1))
                    for t in range(TT):
                        ins = nc.vector.scalar_tensor_tensor(out=ft[:, t, :], in0=ft[:, t, :], scalar=1.0, in1=BANK["A"][t][:, :],
                                                             op0=ALU.add, op1=ALU.mult)
                    ins.then_inc(free["A"], 1)
                    fence()
                elif k == "done_ff_up":
                    dve.wait_ge(used, count(s, i, "unit"))
                    for t in range(TT):
                        ins = nc.vector.scalar_tensor_tensor(out=ft[:, t, :], in0=ft[:, t, :], scalar=hs2[:, t:t + 1], in1=BANK["B"][t][:, :],
                                                             op0=ALU.mult, op1=ALU.mult)
                    ins.then_inc(free["B"], 1)
                elif k == "turn_ff":
                    c0 = (i * 4 if s.tile is None else s.tile * 4) + 2 * s.pair
                    turn_split(s, i, FB[s.pair][:, :].rearrange("p (c n) -> p c n", c=2), fT[0][:, bass.ds(c0, 2), :], fT[1][:, bass.ds(c0, 2), :])
                elif k == "done_down":
                    dve.wait_ge(used, count(s, i, "unit"))
                    for t in range(TT):
                        hh = h[:, t, s.tile * N:(s.tile + 1) * N]
                        ins = nc.vector.tensor_tensor(hh, BANK[s.bank][t][:, :], hh, ALU.add)
                    ins.then_inc(free[s.bank], 1)

        @block.gpsimd
        def _(pool):
            def fence():
                nc.gpsimd.drain()

            def rsqrt(dst, src, n, rows=P):
                return nc.gpsimd.tensor_tensor(dst, src, mhalf[0:rows, 0:n], ALU.pow)

            def rotate(X, h0, start, hw, tables, before):
                x1 = X[:, :, h0:h0 + 2, start:start + hw]
                x2 = X[:, :, h0:h0 + 2, start + hw:start + 2 * hw]
                t = [rot[:, q, 0:TT * 2 * hw].rearrange("p (t n h) -> p t n h", t=TT, n=2) for q in range(4)]
                for q, x in enumerate((x1, x2, x2, x1)):
                    nc.gpsimd.tensor_tensor(t[q], x, tables[q].unsqueeze(2).to_broadcast([P, TT, 2, hw]), ALU.mult)
                fence()
                if before:
                    before()
                nc.gpsimd.tensor_tensor(x1, t[0], t[1], ALU.subtract)
                nc.gpsimd.tensor_tensor(x2, t[2], t[3], ALU.add).then_inc(roped, 1)
                fence()

            nc.gpsimd.memset(mhalf, -0.5)
            fence()
            pool.wait_ge(ms_x, 1)
            rsqrt(rx, msx, TT).then_inc(x_rstd, 1)
            pool.wait_ge(const, 16 * (NCONST - NFIRST))
            for s, i in walk(pool, PH):
                k = s.kind
                if k == "lat_a":
                    pool.wait_ge(ms_ready, count(s, i, "ms", 1))
                    rsqrt(rs[:, 0:TT], ms[:, 0:TT], TT).then_inc(rstd_ready, 1)
                elif k == "done_cmp_k":
                    pool.wait_ge(made["cmp_k"], 1)
                    rsqrt(rs[0:CROWS, 0:1], ms[0:CROWS, 0:1], 1, CROWS).then_inc(cmp_rstd, 1)
                elif k == "h_norm":
                    pool.wait_ge(h_ms, 1)
                    rsqrt(rh, msh, TT).then_inc(h_pow, 1)
                elif k == "k_sq":
                    n = TT * (HPG if s.which == "mla" else 2)
                    pool.wait_ge(ms_ready, count(s, i, "ms", 1))
                    rsqrt(rs[:, 0:n], ms[:, 0:n], n).then_inc(rstd_ready, 1)
                    if s.which == "mla":
                        fence()
                        for t in range(TT):
                            ins = nc.gpsimd.tensor_tensor(qk_m[:, t, HPG:2 * HPG, MLA_NOPE:DK],
                                                          kr[:, t, :].unsqueeze(1).to_broadcast([P, HPG, MLA_ROT]),
                                                          rs[:, t * HPG:(t + 1) * HPG].unsqueeze(2).to_broadcast([P, HPG, MLA_ROT]), ALU.mult)
                        ins.then_inc(roped, 1)
                elif k == "k_scale" and s.which == "nsa":
                    pool.wait_ge(scaled, count(s, i, "scale", 1))
                    rotate(qk_n, 4, 0, NSA_ROT // 2, (cos_n[:], sin_n[:], cos_n[:], sin_n[:]), None)
                elif k == "q_sq":
                    X, _, tables, start, hw = head_view(s.which)
                    b = bank_of_queries(s)
                    pool.wait_ge(free[b], count(s, i, "tile" + b))
                    rotate(X, s.h, start, hw, [tables[:, n] for n in range(4)], lambda: pool.wait_ge(ms_ready, count(s, i, "ms", 1)))
                    q = slice(2 * s.h, 2 * s.h + 4)
                    rsqrt(rq[:, q], ms_q[:, q], 4)
                    fence()
                    r = rq[:, q].rearrange("p (r n) -> p r n", n=2)
                    for c in (0, 2):
                        ins = nc.gpsimd.tensor_scalar(neg_rq[:, s.h:s.h + 2, c:c + 2], r, -1.0, None, ALU.mult)
                    ins.then_inc(rstd_ready, 1)

        @block.tensor
        def _(pe):
            def turn(dst, src, rows=P):
                return nc.tensor.transpose(dst, src, ident[0:rows, 0:rows])

            def turn_pair(src, cols, bank):
                for c in range(2):
                    for t in range(TT):
                        ins = turn(bank[:, c * SEQ + t * P:c * SEQ + (t + 1) * P], src[:, t, cols + c * P:cols + (c + 1) * P])
                return ins

            for s, i in walk(pe, PH):
                k = s.kind
                if k in PAIRED:
                    pe.wait_ge(fill_out, count(s, i, "fill", -1))
                elif "fill" in s.kinds and k not in ("setup", "turn_x"):
                    pe.wait_ge(fill_out, count(s, i, "fill"))
                if k == "unit":
                    if s.first:
                        wait(pe, free[s.bank], count(s, i, "tile" + s.bank))
                        if s.lhs != "x" or s.weight == "w_ffn_gate":
                            wait(pe, fill_out, count(s, i, "fill"))
                            if s.lhs in ("fk", "fv"):
                                pe.wait_ge(flat_out, 1 if s.lhs == "fv" else 3)
                            if s.lhs in ("om", "on"):
                                pe.wait_ge(o_free, count(s, i, "head", 1))
                        else:
                            wait(pe, fill_out, 1 + KD // 2)
                    elif s.lhs in ("ff", "m") or s.weight == "w_ffn_gate":
                        if s.chunk >= (KF if s.lhs == "ff" else KD) - 4:
                            wait(pe, fill_out, count(s, i, "fill"))
                    pe.wait_ge(split, count(s, i, "unit", 1))
                    sl = slot_of(s)
                    outs = halves(s)
                    M_ = CROWS if s.lhs in ("fk", "fv", "hk", "hv") else P
                    for c in range(s.m):
                        first, last = s.first and c == 0, s.last and c == s.m - 1
                        for t, c0, c1, bank in outs:
                            dst = bank[0:M_, 0:c1 - c0]
                            wh = whi[0:s.rows, sl, c * s.width + c0:c * s.width + c1]
                            wl = wlo[0:s.rows, sl, c * s.width + c0:c * s.width + c1]
                            nc.tensor.matmul(dst, lhsT(s, 0, s.chunk + c, t), wh, start=first, stop=False)
                            nc.tensor.matmul(dst, lhsT(s, 0, s.chunk + c, t), wl, start=False, stop=False)
                            ins = nc.tensor.matmul(dst, lhsT(s, 1, s.chunk + c, t), wh, start=False, stop=last)
                    ins.then_inc(used, 1)
                elif k == "setup":
                    pe.wait_ge(const0, 16 * NFIRST)
                    turn(QT[:, 0:2 * KD], rows_sb[:], 2 * KD)
                    for c in range(2):
                        turn(QT[0:HALF, 32 + 32 * c:64 + 32 * c], pe_k_sb[:, c * HALF:(c + 1) * HALF], CMP_LEN)
                    turn(QT[:, 96:128], pe_v_sb[:], CMP_LEN).then_inc(filled, 1)
                elif k == "turn_x":
                    pe.wait_ge(x_in[s.pair // 2], 16)
                    pe.wait_ge(fill_out, max(1, count(s, i, "fill") - 3))
                    turn_pair(x_sb, 2 * s.pair * P, FB[s.bank]).then_inc(filled, 1)
                elif k == "turn_kc":
                    pe.wait_ge(free["A"], 2)
                    pe.wait_ge(free["B"], 1)
                    for c in range(2):
                        for t in range(TT):
                            o = s.slot * DK + c * HALF
                            ins = turn(QT[0:HALF, c * SEQ + t * P:c * SEQ + (t + 1) * P], kv[:, t, o:o + HALF])
                    ins.then_inc(filled, 1)
                elif k == "turn_vc":
                    turn_pair(kv, GROUPS * DK + 2 * s.slot * P, QT).then_inc(filled, 1)
                elif k == "turn_lat":
                    pe.wait_ge(scaled, count(s, i, "scale"))
                    turn_pair(lat[:, :, s.which, :], 2 * s.pair * P, QT).then_inc(filled, 1)
                elif k == "turn_hidden":
                    pe.wait_ge(made["hidden_" + ("k" if s.c0 < 6 else "v")], 1)
                    for c in range(s.c0, s.c1):
                        ins = turn(QT[:, (c - s.c0) * CROWS:(c - s.c0 + 1) * CROWS], hid[:, c * P:(c + 1) * P], CROWS)
                    ins.then_inc(filled, 1)
                elif k == "turn_cmp":
                    pe.wait_ge(cmp_normed, 1)
                    for c in range(2):
                        ins = turn(QT[0:HALF, c * CROWS:(c + 1) * CROWS], kc[:, c * HALF:(c + 1) * HALF], CROWS)
                    ins.then_inc(filled, 1)
                elif k == "turn_heads":
                    X = head_view(s.which)[0]
                    pe.wait_ge(roped, count(s, i, "rope"))
                    pe.wait_ge(scaled, count(s, i, "scale"))
                    if s.job:
                        pe.wait_ge(pt_out, count(s, i, "turn_probs"))
                    for slot, bank in ((s.lo, QT), (s.hi, TP)):
                        for c in range(2):
                            for t in range(TT):
                                ins = turn(bank[0:HALF, c * SEQ + t * P:c * SEQ + (t + 1) * P], X[:, t, slot, c * HALF:(c + 1) * HALF])
                        ins.then_inc(filled, 1)
                elif k == "scores":
                    T = head_view(s.which)[1]
                    r, kk = (s.job, HPG + s.job) if s.which == "mla" else (s.job // 2, HPG + s.job % 2)
                    pe.wait_ge(fill_out, count(s, i, "fill", -s.lo))
                    wait(pe, exped, count(s, i, "scores"))
                    def mm(dst, l, rr, **kw):
                        return nc.tensor.matmul(dst, l, rr, skip_group_check=True, **kw)
                    mm(S[:, 0:P], identb[:], maskb[:], start=True, stop=False)
                    mm(S[:, 2 * P:3 * P], identb[:], maskb[:], start=False, stop=False)
                    if s.which == "nsa":
                        tc = s.job % 2
                        SC = S[:, 3 * P:3 * P + CROWS]
                        mm(SC, identb[:], cmaskb[:, tc, bass.ds(i, 1), :].rearrange("p a n -> p (a n)"), start=False, stop=False)
                    for c in range(2):
                        q = [T[:, r, c * SEQ + t * P:c * SEQ + (t + 1) * P] for t in range(TT)]
                        if s.which == "nsa":
                            mm(SC, q[tc], kcT[:, c, :], start=False, stop=c == 1)
                        mm(S[:, 0:P], q[0], T[:, kk, c * SEQ:c * SEQ + P], start=False, stop=c == 1)
                        ins = mm(S[:, P:3 * P], q[1], T[:, kk, c * SEQ:(c + 1) * SEQ], start=False, stop=c == 1)
                    ins.then_inc(scored, 1)
                elif k == "turn_probs":
                    Pb = Pbs[:, s.job % 2, :]
                    pe.wait_ge(probs, count(s, i, "turn_probs", 1))
                    pe.wait_ge(fill_out, count(s, i, "fill"))
                    for q in range(3):
                        ins = turn(TP[:, q * P:(q + 1) * P], Pb[:, q * P:(q + 1) * P])
                    if s.which == "nsa":
                        ins = turn(TP[0:CROWS, 3 * P:4 * P], Pb[:, 3 * P:3 * P + CROWS])
                    ins.then_inc(turned, 1)
                elif k == "values":
                    pe.wait_ge(pt_out, count(s, i, "values", 1))
                    if s.which == "mla":
                        V, j, start = v_m, s.job, True
                    else:
                        V, j, start = v_n, s.job % 2, s.job % 2 == 0
                    if start:
                        pe.wait_ge(o_free, count(s, i, "head", 1))
                    stop = s.last
                    nc.tensor.matmul(OP[:, 0:SEQ], V[:, 0, j, :], pT[:, 0:SEQ], start=start, stop=False, skip_group_check=True)
                    ins = nc.tensor.matmul(OP[:, P:SEQ], V[:, 1, j, :], pT[:, SEQ:SEQ + P], start=False, stop=stop, skip_group_check=True)
                    if s.which == "nsa":
                        tc = s.job % 2
                        ins = nc.tensor.matmul(OP[:, tc * P:(tc + 1) * P], v_c[:], pT[0:CROWS, 3 * P:4 * P], start=False, stop=stop,
                                               skip_group_check=True)
                    ins.then_inc(valued, 1)
                elif k == "turn_merged":
                    pe.wait_ge(made["merged"], count(s, i, "merged"))
                    turn_pair(mt, 2 * s.pair * P, FB[s.pair]).then_inc(filled, 1)
                elif k == "turn_h":
                    pe.wait_ge(free["AB"[s.tile % 2]], count(s, i, "tile" + "AB"[s.tile % 2]))
                    turn_pair(h, s.tile * N + 2 * s.pair * P, FB[s.pair]).then_inc(filled, 1)
                elif k == "turn_ff":
                    pe.wait_ge(free["B"], count(s, i, "tileB"))
                    turn_pair(ft, 2 * s.pair * P, FB[s.pair]).then_inc(filled, 1)


_INS = ['x', 'attn_norm_g', 'w_in', 'mla_q_lat_g', 'mla_kv_lat_g', 'mla_w_uq', 'mla_w_uk', 'mla_w_uv',
        'mla_q_norm_g', 'mla_k_norm_g', 'nsa_q_norm_g', 'nsa_k_norm_g', 'cmp_pe_k', 'cmp_pe_v',
        'cmp_k_w1', 'cmp_k_b1', 'cmp_k_w2', 'cmp_k_b2', 'cmp_v_w1', 'cmp_v_b1', 'cmp_v_w2', 'cmp_v_b2',
        'w_proj_mla', 'w_proj_nsa', 'w_out', 'ffn_norm_g', 'w_ffn_gate', 'w_ffn_up', 'w_ffn_down']


def _constants():
    import numpy as np
    bf16 = np.dtype("bfloat16")
    c = {"ident": np.eye(P, dtype=np.float32), "identb": np.eye(P, dtype=bf16)}
    q = np.arange(P)
    c["maskb"] = np.where(q[None, :] <= q[:, None], 0.0, MASKED).astype(bf16)
    end = np.arange(NCMP) * CMP_STRIDE + CMP_LEN - 1
    ok = np.zeros((SEQ, GROUPS, GROUPS, NCMP), bool)
    for g in range(GROUPS):
        ok[:, g, g, :] = end[None, :] <= np.arange(SEQ)[:, None]
    c["cmaskb"] = np.where(ok, 0.0, MASKED).reshape(SEQ, GROUPS, CROWS).astype(bf16)

    def tables(pos, dim):
        inv = np.float32(500000.0) ** (-np.arange(0, dim, 2, dtype=np.float32) / np.float32(dim))
        ang = pos.astype(np.float32)[:, None] * inv[None, :].astype(np.float32)
        return np.cos(ang).astype(np.float32), np.sin(ang).astype(np.float32)
    c["cos_m"], c["sin_m"] = tables(np.arange(SEQ), MLA_ROT)
    c["cos_n"], c["sin_n"] = tables(np.arange(SEQ), NSA_ROT)
    c["cos_c"], c["sin_c"] = tables(np.tile(end, GROUPS), NSA_ROT)
    return c


def kernel(**inputs):
    import numpy as _np
    import concourse.bacc as _bacc
    from concourse import mybir as _mybir
    from concourse.bass_utils import run_bass_kernel_spmd as _run

    nc = _bacc.Bacc("TRN2", target_bir_lowering=False, num_devices=1)
    arrays, aps = {}, {}
    for name in _INS:
        a = _np.ascontiguousarray(inputs[name])
        arrays[f"in_{name}_dram"] = a
        aps[name] = nc.dram_tensor(f"in_{name}_dram", a.shape, _mybir.dt.from_np(a.dtype), kind="ExternalInput").ap()[0]
    for name, a in _constants().items():
        arrays[f"const_{name}_dram"] = a
        aps[name] = nc.dram_tensor(f"const_{name}_dram", a.shape, _mybir.dt.from_np(a.dtype), kind="ExternalInput").ap()
    out = nc.dram_tensor("out_0_dram", (1, SEQ, D), _mybir.dt.float32, kind="ExternalOutput").ap()
    build(nc, aps, out[0])
    r = _run(nc, [arrays], core_ids=[0])
    return r.results[0]["out_0_dram"]
```

```python
from contextlib import ExitStack, nullcontext

import concourse.bass as bass
from concourse import mybir

F32 = mybir.dt.float32
F32R = mybir.dt.float32r
BF16 = mybir.dt.bfloat16
ALU = mybir.AluOpType
ACT = mybir.ActivationFunctionType
AXX = mybir.AxisListType.X

P = 128
D = 2048
SEQ = 256
TT = SEQ // P
KD = D // P
EPS = 1e-6
HEADS, GROUPS = 16, 4
HPG = HEADS // GROUPS
DK, DV = 192, 128
RANK = 512
MLA_NOPE, MLA_ROT, NSA_ROT = 128, 64, 48
CMP_LEN, CMP_STRIDE = 32, 16
NCMP = (SEQ - CMP_LEN) // CMP_STRIDE + 1
CROWS = GROUPS * NCMP
LO_ROW = 64
BOTH = LO_ROW + CROWS
FK_CHUNKS = CMP_LEN * DK // P
HID_K, HID_V = 4 * DK, 4 * DV
HALF = DK // 2
D_FF = -(-8 * D // (3 * 256)) * 256
KF = D_FF // P
N = 512
NT = D // N
FT = D_FF // N
SCALE = DK ** -0.5
MASKED = -1e34
LOWEST = -1e26

O_KR = 2 * RANK
O_Q = O_KR + MLA_ROT
O_KC = O_Q + HEADS * DK
O_VC = O_KC + GROUPS * DK
O_KS = O_VC + GROUPS * DV
O_VS = O_KS + GROUPS * DK
O_KW = O_VS + GROUPS * DV
O_VW = O_KW + GROUPS * DK
O_GN = O_VW + GROUPS * DV
O_GM = O_GN + HEADS * 3
D_IN = O_GM + 2 * D

K_COLS = (0, P, 2 * P - DK)

RING = 4
EXTRA = 2
SLOT = 1024
AHEAD = 3
CKV_EARLY = 5
FIRST_WIDTH = 4 * DK
NCONST, NFIRST = 23, 3


class Step:
    def __init__(self, kind, kinds=(), bank=None, which=None, tile=None, pair=None, slot=None, job=None, lo=None, hi=None,
                 weight=None, col=None, lhs=None, chunk=None, m=None, width=None, rows=None, step=0, start=0,
                 first=False, last=False, c0=None, c1=None, h=None):
        self.kind, self.kinds, self.bank, self.which, self.tile, self.pair = kind, kinds, bank, which, tile, pair
        self.slot, self.job, self.lo, self.hi, self.h = slot, job, lo, hi, h
        self.weight, self.col, self.lhs, self.chunk, self.m, self.width, self.rows = weight, col, lhs, chunk, m, width, rows
        self.step, self.start, self.first, self.last = step, start, first, last
        self.c0, self.c1 = c0, c1
        self.base, self.per, self.ahead, self.after = {}, {}, None, None


class Phase:
    def __init__(self, steps, times=1):
        self.steps, self.times = steps, times


def transfers(u):
    return 1 if u.lhs == "fk" else 2


def number(phases):
    seen, last = {}, {}
    total = sum(s.kind == "unit" for s in phases[0].steps)
    for ph in phases:
        local = dict(seen)
        for s in ph.steps:
            s.base = dict(local)
            if s.kind == "unit":
                n = s.base.get("unit", 0)
                more = ph is phases[0] and n < total - 2 * RING
                s.slot = n % (RING + EXTRA if more else RING)
                s.after = last.get(s.slot, 0) if ph is phases[0] else None
                last[s.slot] = n + 1
                s.kinds = ("unit",) + (f"load{s.slot}",) * transfers(s)
            for k in s.kinds:
                local[k] = local.get(k, 0) + 1
        per = {k: local[k] - seen.get(k, 0) for k in local}
        for s in ph.steps:
            s.per = per if ph.times > 1 else {}
        for k in local:
            seen[k] = seen.get(k, 0) + per[k] * ph.times
    return phases


def walk(eng, phases):
    for ph in phases:
        with (eng.Fori(0, ph.times) if ph.times > 1 else nullcontext(0)) as i:
            for s in ph.steps:
                yield s, i


def count(s, i, kind, more=0):
    n, per = s.base.get(kind, 0) + more, s.per.get(kind, 0)
    return i * per + n if per else n


def wait(eng, sem, value):
    if isinstance(value, int) and value <= 0:
        return
    eng.wait_ge(sem, value)



def tile_units(out, weight, col, lhs, chunks, width, per_unit, rows=P, k0=0, **about):
    steps = []
    for c in range(0, chunks, per_unit):
        m = min(per_unit, chunks - c)
        steps.append(Step("unit", ("unit",), bank=out, weight=weight, col=col, lhs=lhs, chunk=k0 + c, m=m,
                          width=width, rows=rows, first=c == 0, last=c + m == chunks, **about))
    return steps


def weave(units, extras):
    steps = []
    for k, u in enumerate(units):
        steps.append(u)
        steps += extras.get(k, [])
    for k in sorted(extras):
        if k >= len(units):
            steps += extras[k]
    return steps


def done(bank, what, taken=False, **about):
    half = what in ("krg", "gate_m", "y_m")
    return Step("done_" + what, ("tile" + bank,) + ("taken",) * taken + ("half",) * half, bank=bank, **about)


def k_sq(which):
    return Step("k_sq", ("ms",) + ("rope",) * (which == "mla"), which=which, bank="A")


def k_scale(which):
    return Step("k_scale", ("scale",) + ("rope",) * (which == "nsa"), which=which)


def q_sq(which, h):
    return Step("q_sq", ("ms", "rope"), which=which, h=h, bank="AB"[(h == 0) == (which == "mla")])


def turn_heads(which, a, b, before=0):
    return Step("turn_heads", ("fill", "fill"), which=which, lo=a, hi=b, job=before)


def jobs(which, njobs, at, turns):
    extras = {}
    for k in range(njobs + 2):
        st = extras.setdefault(at[k], [])
        if k in turns:
            st.append(turn_heads(which, *turns[k], max(0, k - 1)))
        if k < njobs:
            st.append(Step("scores", ("scores",), which=which, job=k, lo=2 if k in turns else 0))
        if k >= 2:
            last = which == "mla" or (k - 2) % 2 == 1
            st.append(Step("values", ("values",) + ("head",) * last, which=which, job=k - 2, last=last))
        if 1 <= k <= njobs:
            st.append(Step("turn_probs", ("turn_probs",), which=which, job=k - 1))
        if k < njobs:
            st.append(Step("probs", ("probs",), which=which, job=k))
    return extras


def merge_extras(*many):
    out = {}
    for e in many:
        for k, v in e.items():
            out.setdefault(k, []).extend(v)
    return out


def schedule():
    def turn_x(c):
        return Step("turn_x", ("fill", "sfill"), pair=c, bank=c % 4)
    first = tile_units("A", "w_in", O_KC, "x", KD, 2 * DK, 2)
    for c, u in enumerate(first):
        u.pair = c
    ex = {c: [turn_x(c + 2)] for c in range(KD // 2 - 2)}
    for q in range(NT):
        ex[q + NT] = ex.get(q + NT, []) + [Step("x_squares", tile=q)]
    b = [Step("setup", ("fill",)), turn_x(0), turn_x(1)] + weave(first, ex)

    def flat(which):
        return [[Step("flat_make", ("flat_make",), which=which)], [Step("flat_hi", ("flat_hi",), which=which)],
                [Step("flat_lo", ("flat_lo",), which=which)]]

    def turned(kind, slot=0, part=0):
        return [Step("turn_" + kind, ("fill",), slot=slot, c0=part)]
    k0, k1, k2, v = flat("k0"), flat("k1"), flat("k2"), flat("v")
    b += weave(tile_units("B", "w_in", O_KC + 2 * DK, "x", KD, 2 * DK, 2),
               {0: [Step("x_ms")], 2: [done("A", "kc", slot=0)], 3: turned("kc", 0, 0), 4: turned("kc", 0, 1), 5: turned("kc", 0, 2),
                6: [Step("gains")]})
    b += [done("B", "kc", slot=1)]
    b += weave(tile_units("A", "w_in", O_VC, "x", KD, N, 2),
               {0: turned("pe") + turned("kc", 1, 0), 1: turned("kc", 1, 1), 2: turned("kc", 1, 2) + k0[0], 3: k0[1], 4: k0[2] + k1[0],
                5: k1[1], 6: k1[2] + k2[0], 7: k2[1] + k2[2]})
    b += [done("A", "vc")]

    def lat_turn(which, pair):
        return [Step("turn_lat", ("fill", "sfill"), which=which, pair=pair)]
    fk = tile_units("B", "cmp_k_w1", 0, "fk", FK_CHUNKS, HID_K, 1)
    cq = tile_units("A", "w_in", 0, "x", KD, N, 2)
    ckv = tile_units("A", "w_in", RANK, "x", KD, N, 2)
    ex = {1 + 3 * n: [u] for n, u in enumerate(cq)}
    ex[22].append(done("A", "lat", which=0))
    ex.update({3: turned("vc", 0), 5: turned("vc", 1), 8: v[0], 11: v[1], 14: v[2], 17: [Step("load_b")],
               25: [Step("lat_a", ("ms",), which=0)], 29: [Step("lat_b", ("scale",), which=0)], 33: lat_turn(0, 0), 35: lat_turn(0, 1)})
    for n in range(CKV_EARLY):
        ex.setdefault(27 + 4 * n, []).append(ckv[n])
    b += weave(fk, ex)
    fv = tile_units("B", "cmp_v_w1", 0, "fv", CMP_LEN, HID_V, 2)
    w2k = tile_units("A", "cmp_k_w2", 0, "hk", HID_K // P, DK, 3)
    w2v = tile_units("B", "cmp_v_w2", 0, "hv", HID_V // P, DV, 4)
    late = ckv[CKV_EARLY:]
    b += [done("B", "hidden_k"), late[0], Step("tanh", which="k")]
    b += weave(fv, {0: [late[1], Step("gelu", which="k")], 1: [late[2]], 2: [done("A", "lat", which=1)],
                    3: [Step("turn_hidden", ("fill", "sfill"), c0=0, c1=4)], 4: [Step("turn_hidden", ("fill", "sfill"), c0=4, c1=6)],
                    5: [Step("lat_a", ("ms",), which=1)], 6: w2k + [done("A", "cmp_k")], 7: [Step("lat_b", ("scale",), which=1)],
                    8: [Step("cmp_norm", ("cmp_norm",))], 9: lat_turn(1, 0), 10: lat_turn(1, 1), 12: [Step("turn_cmp", ("fill",))]})
    krg = tile_units("A", "kr_gates", 0, "x", KD, MLA_ROT + 3 * HEADS, 8)
    b += [done("B", "hidden_v"), krg[0], Step("tanh", which="v"), Step("gelu", which="v"), krg[1],
          Step("turn_hidden", ("fill", "sfill"), c0=6, c1=10), done("A", "krg")]
    b += w2v + [done("B", "cmp_v"), Step("shared_key")]
    phases = [Phase(b)]

    u = tile_units("A", "mla_w_uk", 0, "ckv", 4, N, 2, step=N)
    u += tile_units("B", "mla_w_uq", 0, "cq", 4, 2 * DK, 2, step=4 * DK)
    u += tile_units("A", "mla_w_uq", 2 * DK, "cq", 4, 2 * DK, 2, step=4 * DK)
    u += tile_units("B", "mla_w_uv", 0, "ckv", 4, N, 2, step=N)
    u += tile_units("A", "w_in", O_GM, "x", KD, N, 2, step=N)
    ex = {1: [done("A", "mla_k", taken=True), k_sq("mla")],
          4: [k_scale("mla")],
          3: [done("B", "mla_q", taken=True, h=0), q_sq("mla", 0)],
          5: [done("A", "mla_q", taken=True, h=2), q_sq("mla", 2)],
          7: [done("B", "mla_v"), turn_heads("mla", HPG, 0)],
          15: [done("A", "gate_m")]}
    jb = jobs("mla", HPG, [8, 9, 10, 11, 13, 15], {k: (HPG + k + 1, k + 1) for k in range(HPG - 1)})
    phases.append(Phase(weave(u, merge_extras(ex, jb)), GROUPS))

    u = tile_units("A", "ks_kw", 0, "x", KD, 2 * DK, 2, step=DK)
    u += tile_units("B", "vs_vw", 0, "x", KD, 2 * DV, 4, step=DV)
    u += tile_units("A", "w_in", O_Q, "x", KD, 2 * DK, 2, step=4 * DK)
    u += tile_units("B", "w_in", O_Q + 2 * DK, "x", KD, 2 * DK, 2, step=4 * DK)
    u += tile_units("A", "w_proj_mla", 0, "om", KD, N, 2, step=N)
    ex = {7: [done("A", "nsa_k", taken=True), k_sq("nsa")],
          9: [k_scale("nsa")],
          11: [done("B", "nsa_v")],
          14: [turn_heads("nsa", 4, 5)],
          19: [done("A", "nsa_q", taken=True, h=0), q_sq("nsa", 0)],
          22: [turn_heads("nsa", 0, 1)],
          27: [done("B", "nsa_q", taken=True, h=2), q_sq("nsa", 2)],
          35: [done("A", "y_m")]}
    jb = jobs("nsa", 2 * HPG, [23, 24, 26, 29, 30, 31, 32, 33, 34, 35], {3: (2, 3)})
    phases.append(Phase(weave(u, merge_extras(ex, jb)), GROUPS))

    def merged(back):
        u = tile_units("A", "w_in", O_GM + D, "x", KD, N, 2, step=N, start=0 if not back else N)
        u += tile_units("B", "w_proj_nsa", 0, "on", KD, N, 2, step=N, start=0 if not back else N)
        ex = {7: [done("A", "gate_n")], 15: [Step("done_y_n", ("tileB", "merged"), bank="B", tile=back)]}
        if back:
            ex[1] = [Step("turn_merged", ("fill", "sfill"), pair=0)]
            ex[2] = [Step("turn_merged", ("fill", "sfill"), pair=1)]
        return weave(u, ex)
    phases.append(Phase([Step("load_x")] + merged(0)))
    phases.append(Phase(merged(1), NT - 1))

    g = []
    for n in range(NT):
        bank = "AB"[n % 2]
        what, t = ("turn_h", n - 1) if n else ("turn_merged", NT - 1)
        ex = {k + 1: [Step(what, ("fill", "sfill"), pair=k, tile=t)] for k in range(2)}
        g += weave(tile_units(bank, "w_out", n * N, "m", KD, N, 2), ex) + [done(bank, "h", tile=n)]
    phases.append(Phase(g))

    def ffn(back):
        u = tile_units("A", "w_ffn_gate", 0, "x", KD, N, 2, step=N, start=N if back else 0)
        u += tile_units("B", "w_ffn_up", 0, "x", KD, N, 2, step=N, start=N if back else 0)
        ex = {7: [Step("done_ff_gate", ("tileA", "ff"), bank="A")], 15: [done("B", "ff_up")]}
        if back:
            ex[1] = [Step("turn_ff", ("fill", "sfill"), pair=0)]
            ex[2] = [Step("turn_ff", ("fill", "sfill"), pair=1)]
        else:
            ex[1] = [Step("turn_h", ("fill", "sfill"), pair=0, tile=NT - 1)]
            ex[2] = [Step("turn_h", ("fill", "sfill"), pair=1, tile=NT - 1), Step("h_norm")]
        return weave(u, ex)
    phases.append(Phase(ffn(0)))
    phases.append(Phase(ffn(1), FT - 1))
    d = []
    for n in range(NT):
        bank = "AB"[n % 2]
        u = tile_units(bank, "w_ffn_down", n * N, "ff", KF, N, 2)
        ex = {2: [Step("turn_ff", ("fill", "sfill"), pair=0, tile=FT - 1)], 3: [Step("turn_ff", ("fill", "sfill"), pair=1, tile=FT - 1)]} if n == 0 else {}
        d += weave(u, ex) + [done(bank, "down", tile=n)]
    phases.append(Phase(d))
    return number(phases)


def build(nc, A, out):
    PH = schedule()
    with ExitStack() as ctx:
        def sem(name):
            return ctx.enter_context(nc.semaphore(name))

        base = [nc.sbuf_base]

        def at(name, shape, dt, off):
            off = (off + 31) // 32 * 32
            n = 2 if dt == BF16 else 4
            for s in shape[1:]:
                n *= s
            base[0] = off + n
            return nc.alloc_sbuf_tensor_at(name, list(shape), dt, offset=off)

        def sb(name, shape, dt=F32):
            return at(name, shape, dt, base[0])

        raw = sb("raw", [P, RING, SLOT])
        whi = sb("whi", [P, RING, SLOT], F32R)
        wlo = sb("wlo", [P, RING, SLOT], F32R)
        xT_hi = sb("xT_hi", [P, KD, SEQ], F32R)
        xT_lo = sb("xT_lo", [P, KD, SEQ], F32R)
        PB_OFF = base[0]
        Pbs = sb("probs", [P, 2, N])
        pT = sb("pT", [P, N])
        squares = sb("squares", [P, 8, DK], BF16)
        after = base[0]
        raw_more = at("raw_more", [P, EXTRA, SLOT], F32, PB_OFF)
        assert base[0] <= after
        base[0] = after
        rot = sb("rot", [P, 4, 128])
        ident = sb("ident", [P, P])
        identb = sb("identb", [P, P], BF16)
        maskb = sb("maskb", [P, P], BF16)
        cmaskb = sb("cmaskb", [P, TT, GROUPS, CROWS], BF16)
        cos_n = sb("cos_n", [P, TT, NSA_ROT // 2])
        sin_n = sb("sin_n", [P, TT, NSA_ROT // 2])
        cos_c = sb("cos_c", [CROWS, NSA_ROT // 2])
        sin_c = sb("sin_c", [CROWS, NSA_ROT // 2])
        g_head = sb("g_head", [P, 6, DK])
        gcols = sb("gcols", [P, 2 * KD])
        kr = sb("kr", [P, TT, MLA_ROT])
        gates = sb("gates", [P, HEADS, 2, 3])
        kcT = sb("kcT_cmp", [HALF, 2, CROWS])
        v_c = sb("v_c", [CROWS, DV])
        rot_m = sb("rot_m", [P, 4, TT, MLA_ROT // 2])
        rot_n = sb("rot_n", [P, 4, TT, NSA_ROT // 2])
        small = sb("small", [P, 216])
        FIXED = base[0]
        KB = 1024

        def over(name, shape, dt, kb):
            return at(name, shape, dt, FIXED + int(kb * KB))

        latT = [[over(f"lat{w}_{p}", [P, 4, SEQ], F32R, 4 * (2 * w + k)) for k, p in enumerate(("hi", "lo"))] for w in range(2)]
        x_sb = over("x_sb", [P, TT, D], F32, 16)
        rows_sb = over("rows_sb", [2 * KD, P], F32, 32)
        pe_k_sb = over("pe_k_sb", [CMP_LEN, 2 * P], F32, 32.5)
        pe_v_sb = over("pe_v_sb", [CMP_LEN, DV], F32, 33.5)
        fk = over("fk", [P, FK_CHUNKS, BOTH], F32R, 16)
        fv = over("fv", [P, CMP_LEN, BOTH], F32R, 39.25)
        lat = over("lat", [P, TT, 2, RANK], F32, 54.75)
        kc_in = over("kc_in", [P, TT, GROUPS, 2 * P], F32, 62.75)
        vc_in = over("vc_in", [P, TT, GROUPS * DV], F32, 70.75)
        kc_turned = over("kc_turned", [P, GROUPS, 3, SEQ], F32, 74.75)
        vc_turned = over("vc_turned", [P, GROUPS, SEQ], F32, 86.75)
        flat = over("flat", [P, CMP_LEN, CROWS], F32, 90.75)
        g_lat = over("g_lat", [P, 2, RANK], F32, 98.25)
        cos_m = over("cos_m", [P, TT, MLA_ROT // 2], F32, 102.5)
        sin_m = over("sin_m", [P, TT, MLA_ROT // 2], F32, 102.75)
        peT_k = over("peT_k", [P, 3, CMP_LEN // 2], F32, 103)
        peT_v = over("peT_v", [P, CMP_LEN], F32, 103.25)
        junk = over("junk", [P, 4, 64], F32, 103.5)
        hid = over("hid", [CROWS, HID_K + HID_V], F32, 62.75)
        hid_a = over("hid_a", [CROWS, HID_K + HID_V], F32, 67.75)
        hid_lo = over("hid_lo", [CROWS, HID_K + HID_V], F32, 90.75)
        b1 = over("b1", [CROWS, HID_K + HID_V], F32, 74.75)
        hT = [over(f"hT_{p}", [P, 10, CROWS], F32R, 79.75 + 2.5 * k) for k, p in enumerate(("hi", "lo"))]
        kc = over("kc", [CROWS, DK], F32, 84.75)
        b2 = over("b2", [CROWS, DK + DV], F32, 86.75)
        M = over("M", [P, TT, D], F32, 16)
        om = [over(f"om_{p}", [P, HEADS, SEQ], F32R, 32 + 16 * k) for k, p in enumerate(("hi", "lo"))]
        qk_m = over("qk_m", [P, TT, 8, DK], F32, 64)
        qkT_m = over("qkT_m", [HALF, 8, 2 * SEQ], F32, 76)
        v_m = over("v_m", [P, TT, HPG, DV], F32, 92)
        on = [over(f"on_{p}", [P, HEADS, SEQ], F32R, 64 + 16 * k) for k, p in enumerate(("hi", "lo"))]
        qkT_n = over("qkT_n", [HALF, 6, 2 * SEQ], F32, 0)
        v_n = over("v_n", [P, TT, 2, DV], F32, 12)
        qk_n = over("qk_n", [P, TT, 6, DK], F32, 96)
        mT = [over(f"mT_{p}", [P, KD, SEQ], F32R, 32 + 16 * k) for k, p in enumerate(("hi", "lo"))]
        mt = over("mt", [P, TT, N], F32, 96)
        h = over("h", [P, TT, D], F32, 0)
        fT = [over(f"fT_{p}", [P, KF, SEQ], F32R, 16 + 44 * k) for k, p in enumerate(("hi", "lo"))]
        ft = at("ft", [P, TT, N], F32, PB_OFF)
        assert FIXED + 105 * KB <= nc.sbuf_usable_end

        ps = [ctx.enter_context(nc.psum_tensor(f"ps{b}", [P, 512], F32)) for b in range(8)]
        BANK = {"A": (ps[0], ps[1]), "B": (ps[2], ps[3])}
        S, TP, OP, QT = ps[4], ps[5], ps[6], ps[7]

        rx, half_rx, msx = small[:, 0:2], small[:, 2:4], small[:, 4:6]
        ms, rs = small[:, 8:24], small[:, 24:40]
        mhalf = small[:, 40:56]
        mx, nm, sm, rc = small[:, 56:59], small[:, 59:62], small[:, 62:65], small[:, 65:68]
        hss, rh, rh2 = small[:, 72:80], small[:, 80:82], small[:, 82:84]
        gsig = small[:, 88:88 + 96]
        msh = small[:, 84:86]
        hs2 = small[:, 86:88]
        ms_q, rq = ms[:, 8:16], rs[:, 8:16]
        neg_rq = small[:, 184:200].rearrange("p (r n) -> p r n", n=4)
        ms_kr = small[:, 200:202]
        eps = small[:, 204:208]
        spare = small[:, 208:209]
        norm_x = small[:, 202:204]

        const = sem("const")
        const0 = sem("const0")
        bias_in = sem("bias_in")
        x_in = [sem(f"x_in{q}") for q in range(NT)]
        xt_in = sem("xt_in")
        loaded = [sem(f"loaded{k}") for k in range(RING + EXTRA)]
        hi_made, split, used = sem("hi_made"), sem("split"), sem("used")
        free = {"A": sem("freeA"), "B": sem("freeB")}
        filled, fill_hi, fill_out = sem("filled"), sem("fill_hi"), sem("fill_out")
        taken, half_free = sem("taken"), sem("half_free")
        ms_ready, rstd_ready, scaled, roped = sem("ms_ready"), sem("rstd_ready"), sem("scaled"), sem("roped")
        x_rstd, half_rstd = sem("x_rstd"), sem("half_rstd")
        ms_x = sem("ms_x")
        flat_made, flat_hi, flat_out = sem("flat_made"), sem("flat_hi"), sem("flat_out")
        scored, negmax, exped, probs = sem("scored"), sem("negmax"), sem("exped"), sem("probs_ready")
        turned, pt_out, valued, o_hi, o_free = sem("turned"), sem("pt_out"), sem("valued"), sem("o_hi"), sem("o_free")
        acted = {k: sem("acted_" + k) for k in ("hidden_k", "hidden_v", "ff")}
        made = {k: sem("made_" + k) for k in ("hidden_k", "hidden_v", "cmp_k", "merged", "arg_k", "arg_v", "shared_key", "low_k", "low_v")}
        cmp_normed = sem("cmp_normed")
        h_rstd = sem("h_rstd")
        h_ms, h_pow, cmp_rstd = sem("h_ms"), sem("h_pow"), sem("cmp_rstd")
        stored = sem("stored")

        block = ctx.enter_context(nc.Block())

        LHS = {"x": (xT_hi, xT_lo), "cq": latT[0], "ckv": latT[1], "fk": fk, "fv": fv, "om": om, "on": on, "m": mT, "ff": fT}

        def lhsT(u, part, c, t):
            if u.lhs == "hk":
                return hT[part][:, c, :]
            if u.lhs == "hv":
                return hT[part][:, HID_K // P + c, :]
            if u.lhs in ("fk", "fv"):
                return LHS[u.lhs][:, c, :]
            return LHS[u.lhs][part][:, c, t * P:(t + 1) * P]

        def pieces(u, i, k):
            r0, r1 = u.chunk * u.rows, (u.chunk + u.m) * u.rows
            step = u.step
            dst = raw_slot(k)[0:u.rows, 0:u.m * u.width].rearrange("p (c n) -> p c n", c=u.m)

            def src(name, col, width):
                w = A[name][r0:r1]
                w = w[:, bass.ds(i * step + col, width)] if step else w[:, col:col + width]
                return w.rearrange("(c p) n -> p c n", p=u.rows)

            if u.weight == "kr_gates":
                g = HEADS * 3
                return [(dst[:, :, 0:MLA_ROT], src("w_in", O_KR, MLA_ROT)),
                        (dst[:, :, MLA_ROT:], src("w_in", O_GN, g))]
            if u.weight in ("ks_kw", "vs_vw"):
                s0, w0 = (O_KS, O_KW) if u.weight == "ks_kw" else (O_VS, O_VW)
                n = u.width // 2
                return [(dst[:, :, 0:n], src("w_in", s0, n)), (dst[:, :, n:], src("w_in", w0, n))]
            c0 = u.col + u.start
            if transfers(u) == 1:
                return [(dst, src(u.weight, c0, u.width))]
            if u.m % 2:
                n = u.width // 2
                return [(dst[:, :, 0:n], src(u.weight, c0, n)), (dst[:, :, n:], src(u.weight, c0 + n, n))]
            w, n = src(u.weight, c0, u.width), u.m // 2
            return [(dst[:, 0:n, :], w[:, 0:n, :]), (dst[:, n:, :], w[:, n:, :])]

        def raw_slot(k):
            return raw[:, k, :] if k < RING else raw_more[:, k - RING, :]

        def slot_of(s, more=0):
            assert s.per.get("unit", 0) % RING == 0
            return (s.base.get("unit", 0) + more) % RING

        def halves(u):
            b = BANK[u.bank]
            if u.lhs == "fk":
                return [(0, 0, 512, b[0]), (0, 512, HID_K, b[1])]
            if u.lhs in ("fv", "hk", "hv"):
                return [(0, 0, u.width, b[0])]
            return [(t, 0, u.width, b[t]) for t in range(TT)]

        consts = (
            (rows_sb[0:KD, :], A["attn_norm_g"].rearrange("(c p) -> c p", p=P)),
            (rows_sb[KD:2 * KD, :], A["ffn_norm_g"].rearrange("(c p) -> c p", p=P)),
            (ident[:], A["ident"]), (pe_k_sb[:, 0:DK], A["cmp_pe_k"]), (pe_k_sb[:, DK:], A["cmp_pe_k"][:, 0:2 * P - DK]), (pe_v_sb[:], A["cmp_pe_v"]),
            (identb[:], A["identb"]), (maskb[:], A["maskb"]),
            (cmaskb[:], A["cmaskb"].rearrange("(t p) g c -> p t g c", p=P)),
            (cos_m[:], A["cos_m"].rearrange("(t p) c -> p t c", p=P)), (sin_m[:], A["sin_m"].rearrange("(t p) c -> p t c", p=P)),
            (cos_n[:], A["cos_n"].rearrange("(t p) c -> p t c", p=P)), (sin_n[:], A["sin_n"].rearrange("(t p) c -> p t c", p=P)),
            (cos_c[:], A["cos_c"]), (sin_c[:], A["sin_c"]),
            (g_head[:, 0, :], A["mla_q_norm_g"].partition_broadcast(P)), (g_head[:, 1, :], A["mla_k_norm_g"].partition_broadcast(P)),
            (g_head[:, 2, :], A["nsa_q_norm_g"].partition_broadcast(P)),
            (g_head[:, 3, :], A["nsa_k_norm_g"][0].partition_broadcast(P)),
            (g_head[:, 4, :], A["nsa_k_norm_g"][1].partition_broadcast(P)),
            (g_head[:, 5, :], A["nsa_k_norm_g"][2].partition_broadcast(P)),
            (g_lat[:, 0, :], A["mla_q_lat_g"].partition_broadcast(P)), (g_lat[:, 1, :], A["mla_kv_lat_g"].partition_broadcast(P)),
        )
        assert len(consts) == NCONST

        @block.sync
        def _(sp):
            for u, i in walk(sp, PH):
                if u.kind != "unit":
                    continue
                q = u.pair
                if q is not None and q < NT:
                    sp.dma_start(x_sb[:, :, q * N:(q + 1) * N], A["x"].rearrange("(t p) n -> p t n", p=P)[:, :, q * N:(q + 1) * N]).then_inc(x_in[q], 16)
                k = u.slot
                wait(sp, split, count(u, i, "unit", 1 - RING) if u.after is None else u.after)
                for dst, src in pieces(u, i, k):
                    sp.dma_start(dst, src).then_inc(loaded[k], 16)
                n = NFIRST + 2 * (u.base.get("unit", 0) - RING - EXTRA)
                if not u.per and n >= NFIRST:
                    for dst, src in consts[n:n + 2]:
                        sp.dma_start(dst, src).then_inc(const, 16)

        def landed(u):
            return u.base.get(f"load{u.slot}", 0) + transfers(u)

        for n, ph in enumerate(PH):
            us = [s for s in ph.steps if s.kind == "unit"]
            nxt = []
            for q in PH[n + 1:]:
                nxt += [s for s in q.steps if s.kind == "unit"]
                if len(nxt) >= AHEAD:
                    break
            for j, s in enumerate(us):
                if j + AHEAD < len(us):
                    t = us[j + AHEAD]
                    s.ahead = (t.rows, t.m * t.width, landed(t), t.slot)
                elif ph.times > 1:
                    t = us[j + AHEAD - len(us)]
                    s.ahead = (P, SLOT, landed(t) + t.per[f"load{t.slot}"], t.slot)
                elif j + AHEAD - len(us) < len(nxt):
                    t = nxt[j + AHEAD - len(us)]
                    s.ahead = (t.rows, t.m * t.width, landed(t), t.slot)
                else:
                    s.ahead = None

        def split_hi(act, s, i, more, rows, n, loads, r):
            k = slot_of(s, more)
            per = s.per.get(f"load{r}", 0)
            act.wait_ge(loaded[r], i * (16 * per) + 16 * loads if per else 16 * loads)
            wait(act, used, count(s, i, "unit", more + 1 - RING))
            nc.scalar.activation(whi[0:rows, k, 0:n], raw_slot(r)[0:rows, 0:n], ACT.Copy).then_inc(hi_made, 1)

        def split_lo(dve, s, i, more, rows, n, loads, r):
            k = slot_of(s, more)
            wait(dve, hi_made, count(s, i, "unit", more + 1))
            nc.vector.tensor_tensor(wlo[0:rows, k, 0:n], raw_slot(r)[0:rows, 0:n], whi[0:rows, k, 0:n].bitcast(F32),
                                    ALU.subtract).then_inc(split, 1)

        FB = [QT, TP, S, OP]
        PAIRED = ("turn_merged", "turn_h", "turn_ff")

        def head_view(which):
            return (qk_m, qkT_m, rot_m, MLA_NOPE, MLA_ROT // 2) if which == "mla" else (qk_n, qkT_n, rot_n, 0, NSA_ROT // 2)

        def flat_part(s, part):
            c = slice(part * LO_ROW, part * LO_ROW + CROWS)
            return fv[:, :, c] if s.which == "v" else fk[:, int(s.which[1])::3, c]

        def flat_of(s):
            return flat[:] if s.which == "v" else flat[:, 0:CMP_LEN // 2, :]

        def hidden_cols(which):
            return slice(0, HID_K) if which == "k" else slice(HID_K, HID_K + HID_V)

        def query(s):
            return s.job if s.which == "mla" else s.job // 2

        def branches(s):
            b = [(0, P, 0), (P, 3 * P, 1)]
            return b + [(3 * P, 3 * P + CROWS, s.job % 2)] if s.which == "nsa" else b

        def order(s):
            if s.which == "mla":
                return (0, 1)
            return (1, 2, 0) if s.job % 2 else (0, 1, 2)

        @block.scalar
        def _(act):
            for dst, src in consts[:NFIRST]:
                act.dma_start(dst, src).then_inc(const0, 16)

            def copy(dst, src, **kw):
                return nc.scalar.activation(dst, src, ACT.Copy, **kw)

            def turn_split(s, i, src, hi, gain=None):
                wait(act, filled, count(s, i, "fill", 1))
                for c in range(src.shape[1]):
                    kw = {"scale": gain[:, c:c + 1]} if gain is not None else {}
                    ins = copy(hi[:, c, :], src[:, c, :], **kw)
                ins.then_inc(fill_hi, 1)

            first = True
            for s, i in walk(act, PH):
                k = s.kind
                if k == "unit":
                    if first:
                        for m in range(1, AHEAD):
                            split_hi(act, s, i, m, P, FIRST_WIDTH, 2, m)
                        first = False
                    if s.ahead:
                        split_hi(act, s, i, AHEAD, *s.ahead)
                elif k == "setup":
                    split_hi(act, s, i, 0, P, FIRST_WIDTH, 2, 0)
                elif k == "turn_x":
                    f = FB[s.bank][:, :].rearrange("p (c n) -> p c n", c=2)
                    act.wait_ge(fill_out, 1)
                    turn_split(s, i, f, xT_hi[:, 2 * s.pair:2 * s.pair + 2, :], gcols[:, 2 * s.pair:2 * s.pair + 2])
                elif k == "done_kc":
                    act.wait_ge(x_rstd, 1)
                    act.wait_ge(used, KD // 2 if s.slot == 0 else count(s, i, "unit"))
                    for t in range(TT):
                        b, dst = BANK[s.bank][t], kc_in[:, t, 2 * s.slot:2 * s.slot + 2, :]
                        x = b[:, 0:2 * DK].rearrange("p (g n) -> p g n", g=2)
                        copy(dst[:, :, 0:DK], x, scale=rx[:, t:t + 1])
                        ins = copy(dst[:, :, DK:], x[:, :, 0:2 * P - DK], scale=rx[:, t:t + 1])
                    ins.then_inc(free[s.bank], 1)
                elif k == "done_vc":
                    act.wait_ge(used, count(s, i, "unit"))
                    for t in range(TT):
                        ins = copy(vc_in[:, t, :], BANK[s.bank][t][:, :], scale=rx[:, t:t + 1])
                    ins.then_inc(free[s.bank], 1)
                elif k == "done_krg":
                    act.wait_ge(used, count(s, i, "unit"))
                    act.wait_ge(half_rstd, 1)
                    for t in range(TT):
                        copy(kr[:, t, :], BANK[s.bank][t][:, 0:MLA_ROT], scale=rx[:, t:t + 1])
                        ins = nc.scalar.activation(gsig[:, t * 48:t * 48 + 48], BANK[s.bank][t][:, MLA_ROT:MLA_ROT + 48],
                                                   ACT.Tanh, scale=half_rx[:, t:t + 1])
                    ins.then_inc(free[s.bank], 1)
                elif k == "done_lat":
                    act.wait_ge(used, count(s, i, "unit"))
                    for t in range(TT):
                        ins = copy(lat[:, t, s.which, :], BANK[s.bank][t][:, :], scale=rx[:, t:t + 1])
                    ins.then_inc(free[s.bank], 1)
                elif k == "turn_kc":
                    wait(act, filled, count(s, i, "fill", 1))
                    src = QT[:, :].rearrange("p (g n) -> p g n", g=2)
                    dst = kc_turned[:, 2 * s.slot:2 * s.slot + 2, s.c0, :]
                    if s.c0 == 1:
                        copy(dst[0:64], src[0:64])
                        copy(dst[64:P, :, 0:SEQ - 1], src[64:P, :, 1:SEQ]).then_inc(fill_out, 1)
                    else:
                        copy(dst, src).then_inc(fill_out, 1)
                elif k == "turn_vc":
                    wait(act, filled, count(s, i, "fill", 1))
                    copy(vc_turned[:, 2 * s.slot:2 * s.slot + 2, :].rearrange("p c n -> p (c n)"), QT[:, :]).then_inc(fill_out, 1)
                elif k == "flat_hi":
                    act.wait_ge(flat_made, count(s, i, "flat_make"))
                    copy(flat_part(s, 0), flat_of(s)).then_inc(flat_hi, 1)
                elif k == "turn_lat":
                    turn_split(s, i, QT[:, :].rearrange("p (c n) -> p c n", c=2), latT[s.which][0][:, 2 * s.pair:2 * s.pair + 2, :])
                elif k in ("done_hidden_k", "done_hidden_v"):
                    cols = hidden_cols(k[-1])
                    act.wait_ge(used, count(s, i, "unit"))
                    for b, o in enumerate(range(cols.start, cols.stop, N)):
                        w = min(N, cols.stop - o)
                        ins = copy(hid_lo[:, o:o + w], BANK[s.bank][b][LO_ROW:BOTH, 0:w])
                    ins.then_inc(made["low_" + k[-1]], 1)
                elif k == "tanh":
                    act.wait_ge(made["arg_" + s.which], 1)
                    a = hid_a[:, hidden_cols(s.which)]
                    nc.scalar.activation(a, a, ACT.Tanh, scale=0.7978845608028654).then_inc(acted["hidden_" + s.which], 1)
                elif k == "turn_hidden":
                    wait(act, filled, count(s, i, "fill", 1))
                    n = s.c1 - s.c0
                    copy(hT[0][:, s.c0:s.c1, :], QT[:, 0:n * CROWS].rearrange("p (c n) -> p c n", c=n)).then_inc(fill_hi, 1)
                elif k == "turn_cmp":
                    wait(act, filled, count(s, i, "fill", 1))
                    copy(kcT[:], QT[0:HALF, 0:2 * CROWS].rearrange("p (c n) -> p c n", c=2)).then_inc(fill_out, 1)
                elif k == "done_mla_k":
                    act.wait_ge(used, count(s, i, "unit"))
                    for t in range(TT):
                        ins = copy(qk_m[:, t, 4:8, 0:MLA_NOPE], BANK[s.bank][t][:, :].rearrange("p (h n) -> p h n", h=HPG))
                    ins.then_inc(taken, 1)
                elif k == "done_mla_q":
                    act.wait_ge(used, count(s, i, "unit"))
                    for t in range(TT):
                        ins = copy(qk_m[:, t, s.h:s.h + 2, :], BANK[s.bank][t][:, 0:2 * DK].rearrange("p (h n) -> p h n", h=2))
                    ins.then_inc(taken, 1)
                elif k in ("k_sq", "q_sq"):
                    n, w = (HPG, MLA_NOPE) if s.which == "mla" and k == "k_sq" else (2, DK)
                    nc.scalar.drain()
                    for t in range(TT):
                        for q in range(n):
                            m = ms[:, t * n + q:t * n + q + 1] if k == "k_sq" else ms_q[:, 2 * (s.h + q) + t:2 * (s.h + q) + t + 1]
                            ins = nc.scalar.activation(squares[:, t * n + q, 0:w], BANK[s.bank][t][:, q * w:(q + 1) * w], ACT.Square,
                                                       scale=DK ** -0.5 if s.which == "mla" else norm_x[:, t:t + 1], accum_out=m)
                    ins.then_inc(free[s.bank], 1)
                elif k == "done_mla_v":
                    act.wait_ge(used, count(s, i, "unit"))
                    for t in range(TT):
                        ins = copy(v_m[:, t, :, :], BANK[s.bank][t][:, :].rearrange("p (h n) -> p h n", h=HPG))
                    ins.then_inc(free[s.bank], 1)
                elif k in ("done_nsa_k", "done_nsa_q"):
                    act.wait_ge(used, count(s, i, "unit"))
                    h0 = 4 if k == "done_nsa_k" else s.h
                    for t in range(TT):
                        ins = copy(qk_n[:, t, h0:h0 + 2, :], BANK[s.bank][t][:, 0:2 * DK].rearrange("p (h n) -> p h n", h=2),
                                   scale=rx[:, t:t + 1])
                    ins.then_inc(taken, 1)
                elif k == "done_nsa_v":
                    act.wait_ge(used, count(s, i, "unit"))
                    for t in range(TT):
                        ins = copy(v_n[:, t, :, :], BANK[s.bank][t][:, 0:2 * DV].rearrange("p (h n) -> p h n", h=2),
                                   scale=rx[:, t:t + 1])
                    ins.then_inc(free[s.bank], 1)
                elif k == "done_gate_m":
                    act.wait_ge(used, count(s, i, "unit"))
                    for t in range(TT):
                        ins = nc.scalar.activation(M[:, t, bass.ds(i * N, N)], BANK[s.bank][t][:, :], ACT.Tanh, scale=half_rx[:, t:t + 1])
                        ins.then_inc(free[s.bank] if t else half_free, 1)
                elif k == "done_gate_n":
                    act.wait_ge(used, count(s, i, "unit"))
                    for t in range(TT):
                        ins = nc.scalar.activation(mt[:, t, :], BANK[s.bank][t][:, :], ACT.Tanh, scale=half_rx[:, t:t + 1])
                    ins.then_inc(free[s.bank], 1)
                elif k == "turn_heads":
                    act.wait_ge(filled, count(s, i, "fill", 1))
                    copy(head_view(s.which)[1][:, s.lo, :], QT[0:HALF, :]).then_inc(fill_out, 1)
                elif k == "scores":
                    Pb = Pbs[:, s.job % 2, :]
                    act.wait_ge(negmax, count(s, i, "scores", 1))
                    for n, (c0, c1, tile) in enumerate(branches(s)):
                        m = 2 * query(s) + tile
                        o = order(s)[n]
                        ins = nc.scalar.activation(Pb[:, c0:c1], S[:, c0:c1], ACT.Exp, bias=nm[:, o:o + 1], scale=rq[:, m:m + 1],
                                                   accum_out=sm[:, n:n + 1])
                    ins.then_inc(exped, 1)
                elif k == "turn_probs":
                    act.wait_ge(turned, count(s, i, "turn_probs", 1))
                    if s.which == "mla":
                        copy(pT[:, 0:3 * P], TP[:, 0:3 * P]).then_inc(pt_out, 1)
                    else:
                        copy(pT[:, 0:3 * P], TP[:, 0:3 * P])
                        copy(pT[0:CROWS, 3 * P:4 * P], TP[0:CROWS, 3 * P:4 * P]).then_inc(pt_out, 1)
                elif k == "values":
                    if s.last:
                        act.wait_ge(valued, count(s, i, "values", 1))
                        r = s.job if s.which == "mla" else s.job // 2
                        o = (om if s.which == "mla" else on)[0]
                        copy(o[:, bass.ds(i * HPG + r, 1), :].rearrange("p a n -> p (a n)"), OP[:, 0:SEQ]).then_inc(o_hi, 1)
                elif k == "turn_merged":
                    hi = mT[0]
                    c0 = (i * 4 if s.tile is None else s.tile * 4) + 2 * s.pair
                    turn_split(s, i, FB[s.pair][:, :].rearrange("p (c n) -> p c n", c=2), hi[:, bass.ds(c0, 2), :])
                elif k == "turn_h":
                    c0 = s.tile * 4 + 2 * s.pair
                    turn_split(s, i, FB[s.pair][:, :].rearrange("p (c n) -> p c n", c=2), xT_hi[:, c0:c0 + 2, :], gcols[:, KD + c0:KD + c0 + 2])
                elif k == "turn_ff":
                    c0 = (i * 4 if s.tile is None else s.tile * 4) + 2 * s.pair
                    turn_split(s, i, FB[s.pair][:, :].rearrange("p (c n) -> p c n", c=2), fT[0][:, bass.ds(c0, 2), :])
                elif k == "done_ff_gate":
                    act.wait_ge(h_rstd, 1)
                    act.wait_ge(used, count(s, i, "unit"))
                    act.wait_ge(filled, count(s, i, "fill"))
                    for t in range(TT):
                        ins = nc.scalar.activation(ft[:, t, :], BANK["A"][t][:, :], ACT.Tanh, scale=rh2[:, t:t + 1])
                    ins.then_inc(acted["ff"], 1)
                elif k == "load_b":
                    act.wait_ge(flat_out, 4)
                    for dst, src in ((b1[:, 0:HID_K], A["cmp_k_b1"]), (b1[:, HID_K:], A["cmp_v_b1"]),
                                     (b2[:, 0:DK], A["cmp_k_b2"]), (b2[:, DK:], A["cmp_v_b2"])):
                        act.dma_start(dst, src.partition_broadcast(CROWS)).then_inc(bias_in, 16)
                elif k == "load_x":
                    act.wait_ge(valued, count(s, i, "values"))
                    act.dma_start(h[:], A["x"].rearrange("(t p) n -> p t n", p=P)).then_inc(xt_in, 16)
                elif k == "done_down":
                    act.wait_ge(free[s.bank], count(s, i, "tile" + s.bank, 1))
                    cols = slice(s.tile * N, (s.tile + 1) * N)
                    act.dma_start(out.rearrange("(t p) n -> p t n", p=P)[:, :, cols], h[:, :, cols]).then_inc(stored, 16)
            act.wait_ge(stored, 16 * NT)

        @block.vector
        def _(dve):
            def fence():
                nc.vector.drain()

            def turn_split(s, i, src, hi, lo, gain=None):
                wait(dve, fill_hi, count(s, i, "sfill", 1))
                for c in range(src.shape[1]):
                    if gain is None:
                        ins = nc.vector.tensor_tensor(lo[:, c, :], src[:, c, :], hi[:, c, :].bitcast(F32), ALU.subtract)
                    else:
                        ins = nc.vector.scalar_tensor_tensor(out=lo[:, c, :], in0=src[:, c, :], scalar=gain[:, c:c + 1],
                                                             in1=hi[:, c, :].bitcast(F32), op0=ALU.mult, op1=ALU.subtract)
                ins.then_inc(fill_out, 1)

            def square_sum(x, acc, j):
                nc.vector.tensor_tensor_reduce(j, x, x, 1.0, 0.0, ALU.mult, ALU.add, acc)
                fence()

            nc.vector.memset(ms_kr, 0.0).then_inc(o_free, 1)
            fence()
            first = True
            for s, i in walk(dve, PH):
                k = s.kind
                if k == "unit":
                    if first:
                        for m in range(1, AHEAD):
                            split_lo(dve, s, i, m, P, FIRST_WIDTH, 2, m)
                        first = False
                    if s.ahead:
                        split_lo(dve, s, i, AHEAD, *s.ahead)
                elif k == "setup":
                    dve.wait_ge(filled, 1)
                    nc.vector.tensor_copy(gcols[:], QT[:, 0:2 * KD]).then_inc(fill_out, 1)
                    split_lo(dve, s, i, 0, P, FIRST_WIDTH, 2, 0)
                elif k == "turn_pe":
                    dve.wait_ge(filled, count(s, i, "fill", 1))
                    q3 = QT[:, 0:3 * CMP_LEN].rearrange("p (c l o) -> p c l o", c=3, o=2)
                    nc.vector.tensor_copy(peT_k[:, 0, :], q3[:, 0, :, 0])
                    nc.vector.tensor_copy(peT_k[0:64, 1, :], q3[0:64, 1, :, 0])
                    nc.vector.tensor_copy(peT_k[64:P, 1, :], q3[64:P, 1, :, 1])
                    nc.vector.tensor_copy(peT_k[:, 2, :], q3[:, 2, :, 1])
                    nc.vector.tensor_copy(peT_v[:], QT[:, 96:128]).then_inc(fill_out, 1)
                elif k == "turn_x":
                    f = FB[s.bank][:, :].rearrange("p (c n) -> p c n", c=2)
                    c0 = 2 * s.pair
                    turn_split(s, i, f, xT_hi[:, c0:c0 + 2, :], xT_lo[:, c0:c0 + 2, :], gcols[:, c0:c0 + 2])
                elif k == "x_squares":
                    dve.wait_ge(x_in[s.tile], 16)
                    q = s.tile
                    for t in range(TT):
                        square_sum(x_sb[:, t, q * N:(q + 1) * N], hss[:, t * NT + q:t * NT + q + 1], rot[:].rearrange("p a n -> p (a n)"))
                elif k == "x_ms":
                    nc.vector.tensor_reduce(msx, hss.rearrange("p (t n) -> p t n", t=TT), AXX, ALU.add)
                    fence()
                    nc.vector.tensor_scalar(msx, msx, 1.0 / D, EPS, ALU.mult, ALU.add).then_inc(ms_x, 1)
                elif k == "done_kc" and s.slot == 0:
                    dve.wait_ge(x_rstd, 1)
                    nc.vector.tensor_scalar(norm_x, rx, DK ** -0.5, None, ALU.mult)
                    nc.vector.tensor_scalar(half_rx, rx, 0.5, None, ALU.mult).then_inc(half_rstd, 1)
                elif k == "done_krg":
                    dve.wait_ge(free[s.bank], count(s, i, "tile" + s.bank, 1))
                    nc.vector.tensor_scalar(gsig, gsig, 0.5, 0.5, ALU.mult, ALU.add)
                    fence()
                    nc.vector.memset(spare, 0.0).then_inc(half_free, 1)
                    gv = gsig.rearrange("p (t h b) -> p t h b", t=TT, b=3)
                    for j in range(2):
                        for t in range(TT):
                            nc.vector.tensor_copy(gates[:, :, j, t:t + 1], gv[:, t, :, 1 + j:2 + j])
                        nc.vector.tensor_copy(gates[:, :, j, 2:3], gv[:, j, :, 0:1])
                elif k == "flat_make":
                    dve.wait_ge(fill_out, count(s, i, "fill"))
                    if s.which == "k0":
                        nc.vector.memset(fk[:, :, CROWS:LO_ROW].bitcast(F32), 0.0)
                        nc.vector.memset(fv[:, :, CROWS:LO_ROW].bitcast(F32), 0.0)
                    wait(dve, flat_out, count(s, i, "flat_lo"))
                    for half in range(2):
                        t0 = half * CMP_STRIDE
                        if s.which == "v":
                            src, pe, step, l0 = vc_turned, peT_v, 1, 0
                        else:
                            c = int(s.which[1])
                            src, pe, step, l0 = kc_turned[:, :, c, :], peT_k[:, c, :], 2, c // 2
                        a = src[:, :, t0:t0 + NCMP * CMP_STRIDE].rearrange("p g (b l) -> p l g b", l=CMP_STRIDE)[:, l0::step]
                        n = CMP_STRIDE // step
                        ins = nc.vector.tensor_tensor(flat[:, half * n:half * n + n, :].rearrange("p l (g b) -> p l g b", g=GROUPS), a,
                                                      pe[:, half * n:half * n + n].unsqueeze(2).unsqueeze(3).to_broadcast([P, n, GROUPS, NCMP]),
                                                      ALU.add)
                    ins.then_inc(flat_made, 1)
                elif k == "flat_lo":
                    dve.wait_ge(flat_hi, count(s, i, "flat_hi"))
                    nc.vector.tensor_tensor(flat_part(s, 1), flat_of(s), flat_part(s, 0).bitcast(F32),
                                            ALU.subtract).then_inc(flat_out, 1)
                elif k == "lat_a":
                    dve.wait_ge(free["A"], count(s, i, "tileA"))
                    for t in range(TT):
                        square_sum(lat[:, t, s.which, :], ms[:, t:t + 1], rot[:].rearrange("p a n -> p (a n)"))
                    nc.vector.tensor_scalar(ms[:, 0:2], ms[:, 0:2], 1.0 / RANK, EPS, ALU.mult, ALU.add).then_inc(ms_ready, 1)
                elif k == "lat_b":
                    dve.wait_ge(rstd_ready, count(s, i, "ms"))
                    for t in range(TT):
                        ins = nc.vector.scalar_tensor_tensor(out=lat[:, t, s.which, :], in0=lat[:, t, s.which, :], scalar=rs[:, t:t + 1],
                                                             in1=g_lat[:, s.which, :], op0=ALU.mult, op1=ALU.mult)
                    ins.then_inc(scaled, 1)
                elif k == "turn_lat":
                    p2 = slice(2 * s.pair, 2 * s.pair + 2)
                    turn_split(s, i, QT[:, :].rearrange("p (c n) -> p c n", c=2), latT[s.which][0][:, p2, :], latT[s.which][1][:, p2, :])
                elif k in ("done_hidden_k", "done_hidden_v"):
                    cols = hidden_cols(k[-1])
                    c0, n = cols.start, cols.stop - cols.start
                    x, a = hid[:, cols], hid_a[:, cols]
                    dve.wait_ge(used, count(s, i, "unit"))
                    dve.wait_ge(bias_in, 64)
                    for b, o in enumerate(range(0, n, 512)):
                        w = min(512, n - o)
                        ins = nc.vector.tensor_tensor(hid[:, c0 + o:c0 + o + w], BANK[s.bank][b][0:CROWS, 0:w], b1[:, c0 + o:c0 + o + w], ALU.add)
                    fence()
                    dve.wait_ge(made["low_" + k[-1]], 1)
                    nc.vector.tensor_tensor(x, x, hid_lo[:, cols], ALU.add).then_inc(free[s.bank], 1)
                    fence()
                    nc.vector.tensor_tensor(a, x, x, ALU.mult)
                    fence()
                    nc.vector.tensor_scalar(a, a, 0.044715, 1.0, ALU.mult, ALU.add)
                    fence()
                    nc.vector.tensor_tensor(a, a, x, ALU.mult).then_inc(made["arg_" + k[-1]], 1)
                elif k == "gelu":
                    x, a = hid[:, hidden_cols(s.which)], hid_a[:, hidden_cols(s.which)]
                    dve.wait_ge(acted["hidden_" + s.which], 1)
                    nc.vector.tensor_scalar(a, a, 0.5, 0.5, ALU.mult, ALU.add)
                    fence()
                    nc.vector.tensor_tensor(x, a, x, ALU.mult).then_inc(made["hidden_" + s.which], 1)
                    fence()
                elif k == "turn_hidden":
                    n = s.c1 - s.c0
                    wait(dve, fill_hi, count(s, i, "sfill", 1))
                    nc.vector.tensor_tensor(hT[1][:, s.c0:s.c1, :], QT[:, 0:n * CROWS].rearrange("p (c n) -> p c n", c=n),
                                            hT[0][:, s.c0:s.c1, :].bitcast(F32), ALU.subtract).then_inc(fill_out, 1)
                elif k == "done_cmp_k":
                    dve.wait_ge(used, count(s, i, "unit"))
                    nc.vector.tensor_tensor(kc[:], BANK[s.bank][0][0:CROWS, 0:DK], b2[:, 0:DK], ALU.add).then_inc(free[s.bank], 1)
                    fence()
                    square_sum(kc[:], ms[0:CROWS, 8:9], junk[0:CROWS].rearrange("p a n -> p (a n)")[:, 0:DK])
                    nc.vector.tensor_scalar(ms[0:CROWS, 8:9], ms[0:CROWS, 8:9], 1.0 / DK, EPS, ALU.mult, ALU.add).then_inc(made["cmp_k"], 1)
                elif k == "done_cmp_v":
                    dve.wait_ge(used, count(s, i, "unit"))
                    nc.vector.tensor_tensor(v_c[:], BANK[s.bank][0][0:CROWS, 0:DV], b2[:, DK:], ALU.add).then_inc(free[s.bank], 1)
                elif k == "cmp_norm":
                    dve.wait_ge(cmp_rstd, 1)
                    nc.vector.scalar_tensor_tensor(out=kc[:], in0=kc[:], scalar=rs[0:CROWS, 8:9], in1=g_head[0:CROWS, 3, :],
                                                   op0=ALU.mult, op1=ALU.mult)
                    fence()
                    hw = NSA_ROT // 2
                    x1, x2 = kc[:, 0:hw], kc[:, hw:2 * hw]
                    t = [rot[0:CROWS, 2, 32 * q:32 * q + hw] for q in range(4)]
                    for q, (xx, cs) in enumerate(((x1, cos_c), (x2, sin_c), (x2, cos_c), (x1, sin_c))):
                        nc.vector.tensor_tensor(t[q], xx, cs[:], ALU.mult)
                    fence()
                    nc.vector.tensor_tensor(x1, t[0], t[1], ALU.subtract)
                    nc.vector.tensor_tensor(x2, t[2], t[3], ALU.add).then_inc(cmp_normed, 1)
                    fence()
                elif k == "gains":
                    dve.wait_ge(const, 16 * (NCONST - NFIRST))
                    def with_query(kg, qg, rotated, plain):
                        nc.vector.scalar_tensor_tensor(out=g_head[:, kg, plain], in0=g_head[:, kg, plain], scalar=SCALE, in1=g_head[:, qg, plain],
                                                       op0=ALU.mult, op1=ALU.mult)
                        nc.vector.tensor_scalar(g_head[:, kg, rotated], g_head[:, kg, rotated], SCALE, None, ALU.mult)

                    def rotation(table, cos, sin, g, start, hw):
                        for n, (cs, g0) in enumerate(((cos, start), (sin, start + hw), (cos, start + hw), (sin, start))):
                            nc.vector.tensor_tensor(table[:, n, :, :], cs[:], g_head[:, g, g0:g0 + hw].unsqueeze(1).to_broadcast([P, TT, hw]), ALU.mult)
                    with_query(1, 0, slice(MLA_NOPE, DK), slice(0, MLA_NOPE))
                    for kg in (3, 4, 5):
                        with_query(kg, 2, slice(0, NSA_ROT), slice(NSA_ROT, DK))
                    rotation(rot_m, cos_m, sin_m, 0, MLA_NOPE, MLA_ROT // 2)
                    rotation(rot_n, cos_n, sin_n, 2, 0, NSA_ROT // 2)
                    fence()
                elif k == "shared_key":
                    dve.wait_ge(free["A"], count(s, i, "tileA"))
                    hw = MLA_ROT // 2
                    for t in range(TT):
                        square_sum(kr[:, t, :], ms_kr[:, t:t + 1], junk[:, t, :])
                    nc.vector.tensor_scalar(ms_kr, ms_kr, 1.0 / DK, EPS, ALU.mult, ALU.add)
                    nc.vector.tensor_tensor(kr[:], kr[:], g_head[:, 1, MLA_NOPE:DK].unsqueeze(1).to_broadcast([P, TT, MLA_ROT]), ALU.mult)
                    fence()
                    x1, x2 = kr[:, :, 0:hw], kr[:, :, hw:2 * hw]
                    q4 = [junk[:, q, 0:TT * hw].rearrange("p (t n) -> p t n", t=TT) for q in range(4)]
                    for q, (xx, cs) in enumerate(((x1, cos_m), (x2, sin_m), (x2, cos_m), (x1, sin_m))):
                        nc.vector.tensor_tensor(q4[q], xx, cs[:], ALU.mult)
                    fence()
                    nc.vector.tensor_tensor(x1, q4[0], q4[1], ALU.subtract)
                    nc.vector.tensor_tensor(x2, q4[2], q4[3], ALU.add).then_inc(made["shared_key"], 1)
                    fence()
                elif k == "k_scale":
                    X = head_view(s.which)[0]
                    n, w = (HPG, MLA_NOPE) if s.which == "mla" else (2, DK)
                    dve.wait_ge(rstd_ready, count(s, i, "ms"))
                    for t in range(TT):
                        for q in range(n):
                            x = X[:, t, 4 + q, 0:w]
                            ins = nc.vector.scalar_tensor_tensor(out=x, in0=x, scalar=rs[:, t * n + q:t * n + q + 1],
                                                                 in1=g_head[:, 1 if s.which == "mla" else 4 + q, 0:w],
                                                                 op0=ALU.mult, op1=ALU.mult)
                    ins.then_inc(scaled, 1)
                elif k == "turn_heads":
                    dve.wait_ge(filled, count(s, i, "fill", 2))
                    nc.vector.tensor_copy(head_view(s.which)[1][:, s.hi, :], TP[0:HALF, :]).then_inc(fill_out, 1)
                elif k == "scores":
                    dve.wait_ge(scored, count(s, i, "scores", 1))
                    dve.wait_ge(rstd_ready, count(s, i, "ms"))
                    br = branches(s)
                    for (c0, c1, _), o in zip(br, order(s)):
                        nc.vector.tensor_reduce(mx[:, o:o + 1], S[:, c0:c1], AXX, ALU.max)
                    fence()
                    r, start = query(s), s.job % 2 if s.which == "nsa" else 0
                    nc.vector.scalar_tensor_tensor(out=nm[:, 0:len(br)], in0=mx[:, 0:len(br)], scalar=LOWEST,
                                                   in1=neg_rq[:, r, start:start + len(br)], op0=ALU.max, op1=ALU.mult).then_inc(negmax, 1)
                elif k == "probs":
                    Pb = Pbs[:, s.job % 2, :]
                    dve.wait_ge(exped, count(s, i, "probs", 1))
                    n = 2 if s.which == "mla" else 3
                    nc.vector.tensor_scalar(rc[:, 0:n], sm[:, 0:n], 1e-30, None, ALU.max)
                    fence()
                    nc.vector.reciprocal(rc[:, 0:n], rc[:, 0:n])
                    fence()
                    if s.which == "nsa":
                        g = gates[:, bass.ds(i * HPG + s.job // 2, 1), s.job % 2, :].rearrange("p a n -> p (a n)")
                        nc.vector.tensor_tensor(rc[:, 0:n], rc[:, 0:n], g, ALU.mult)
                        fence()
                        nc.vector.tensor_scalar(Pb[:, 3 * P:3 * P + CROWS], Pb[:, 3 * P:3 * P + CROWS], rc[:, 2:3], None, ALU.mult)
                    nc.vector.tensor_scalar(Pb[:, 0:P], Pb[:, 0:P], rc[:, 0:1], None, ALU.mult)
                    nc.vector.tensor_scalar(Pb[:, P:3 * P], Pb[:, P:3 * P], rc[:, 1:2], None, ALU.mult).then_inc(probs, 1)
                elif k == "values":
                    if s.last:
                        dve.wait_ge(o_hi, count(s, i, "head", 1))
                        r = s.job if s.which == "mla" else s.job // 2
                        o = om if s.which == "mla" else on
                        hi, lo = (o[q][:, bass.ds(i * HPG + r, 1), :].rearrange("p a n -> p (a n)") for q in range(2))
                        nc.vector.tensor_tensor(lo, OP[:, 0:SEQ], hi.bitcast(F32), ALU.subtract).then_inc(o_free, 1)
                elif k == "done_gate_m":
                    dve.wait_ge(free[s.bank], count(s, i, "tile" + s.bank, 1))
                    m = M[:, :, bass.ds(i * N, N)]
                    nc.vector.tensor_scalar(m, m, 0.5, 0.5, ALU.mult, ALU.add)
                elif k == "done_y_m":
                    dve.wait_ge(used, count(s, i, "unit"))
                    for t in range(TT):
                        m = M[:, t, bass.ds(i * N, N)]
                        ins = nc.vector.tensor_tensor(m, BANK[s.bank][t][:, :], m, ALU.mult)
                        ins.then_inc(free[s.bank] if t else half_free, 1)
                elif k == "done_gate_n":
                    dve.wait_ge(free[s.bank], count(s, i, "tile" + s.bank, 1))
                    nc.vector.tensor_scalar(mt[:], mt[:], 0.5, 0.5, ALU.mult, ALU.add)
                    fence()
                elif k == "done_y_n":
                    dve.wait_ge(used, count(s, i, "unit"))
                    for t in range(TT):
                        ins = nc.vector.tensor_tensor(mt[:, t, :], BANK[s.bank][t][:, :], mt[:, t, :], ALU.mult)
                    ins.then_inc(free[s.bank], 1)
                    fence()
                    m = M[:, :, bass.ds(i * N + N * s.tile, N)] if s.tile else M[:, :, 0:N]
                    nc.vector.tensor_tensor(mt[:], mt[:], m, ALU.add).then_inc(made["merged"], 1)
                elif k == "turn_merged":
                    c0 = (i * 4 if s.tile is None else s.tile * 4) + 2 * s.pair
                    turn_split(s, i, FB[s.pair][:, :].rearrange("p (c n) -> p c n", c=2), mT[0][:, bass.ds(c0, 2), :], mT[1][:, bass.ds(c0, 2), :])
                elif k == "done_h":
                    dve.wait_ge(used, count(s, i, "unit"))
                    dve.wait_ge(xt_in, 16)
                    for t in range(TT):
                        hh = h[:, t, s.tile * N:(s.tile + 1) * N]
                        ins = nc.vector.tensor_tensor(hh, BANK[s.bank][t][:, :], hh, ALU.add)
                    ins.then_inc(free[s.bank], 1)
                    fence()
                    for t in range(TT):
                        square_sum(h[:, t, s.tile * N:(s.tile + 1) * N], hss[:, t * NT + s.tile:t * NT + s.tile + 1],
                                   rot[:].rearrange("p a n -> p (a n)"))
                elif k == "turn_h":
                    c0 = s.tile * 4 + 2 * s.pair
                    turn_split(s, i, FB[s.pair][:, :].rearrange("p (c n) -> p c n", c=2), xT_hi[:, c0:c0 + 2, :], xT_lo[:, c0:c0 + 2, :],
                               gcols[:, KD + c0:KD + c0 + 2])
                elif k == "h_norm":
                    nc.vector.tensor_reduce(msh, hss.rearrange("p (t n) -> p t n", t=TT), AXX, ALU.add)
                    fence()
                    nc.vector.tensor_scalar(msh, msh, 1.0 / D, EPS, ALU.mult, ALU.add).then_inc(h_ms, 1)
                    dve.wait_ge(h_pow, 1)
                    nc.vector.tensor_scalar(rh2, rh, 0.5, None, ALU.mult)
                    fence()
                    nc.vector.tensor_tensor(hs2, rh, rh2, ALU.mult).then_inc(h_rstd, 1)
                elif k == "done_ff_gate":
                    dve.wait_ge(acted["ff"], count(s, i, "ff", 1))
                    for t in range(TT):
                        ins = nc.vector.scalar_tensor_tensor(out=ft[:, t, :], in0=ft[:, t, :], scalar=1.0, in1=BANK["A"][t][:, :],
                                                             op0=ALU.add, op1=ALU.mult)
                    ins.then_inc(free["A"], 1)
                    fence()
                elif k == "done_ff_up":
                    dve.wait_ge(used, count(s, i, "unit"))
                    for t in range(TT):
                        ins = nc.vector.scalar_tensor_tensor(out=ft[:, t, :], in0=ft[:, t, :], scalar=hs2[:, t:t + 1], in1=BANK["B"][t][:, :],
                                                             op0=ALU.mult, op1=ALU.mult)
                    ins.then_inc(free["B"], 1)
                elif k == "turn_ff":
                    c0 = (i * 4 if s.tile is None else s.tile * 4) + 2 * s.pair
                    turn_split(s, i, FB[s.pair][:, :].rearrange("p (c n) -> p c n", c=2), fT[0][:, bass.ds(c0, 2), :], fT[1][:, bass.ds(c0, 2), :])
                elif k == "done_down":
                    dve.wait_ge(used, count(s, i, "unit"))
                    for t in range(TT):
                        hh = h[:, t, s.tile * N:(s.tile + 1) * N]
                        ins = nc.vector.tensor_tensor(hh, BANK[s.bank][t][:, :], hh, ALU.add)
                    ins.then_inc(free[s.bank], 1)

        @block.gpsimd
        def _(pool):
            def fence():
                nc.gpsimd.drain()

            def rsqrt(dst, src, n, rows=P):
                return nc.gpsimd.tensor_tensor(dst, src, mhalf[0:rows, 0:n], ALU.pow)

            def rotate(X, h0, start, hw, tables):
                x1 = X[:, :, h0:h0 + 2, start:start + hw]
                x2 = X[:, :, h0:h0 + 2, start + hw:start + 2 * hw]
                t = [rot[:, q, 0:TT * 2 * hw].rearrange("p (t n h) -> p t n h", t=TT, n=2) for q in range(4)]
                for q, x in enumerate((x1, x2, x2, x1)):
                    nc.gpsimd.tensor_tensor(t[q], x, tables[q].unsqueeze(2).to_broadcast([P, TT, 2, hw]), ALU.mult)
                fence()
                nc.gpsimd.tensor_tensor(x1, t[0], t[1], ALU.subtract)
                nc.gpsimd.tensor_tensor(x2, t[2], t[3], ALU.add).then_inc(roped, 1)
                fence()

            nc.gpsimd.memset(mhalf, -0.5)
            nc.gpsimd.memset(eps, EPS)
            fence()
            pool.wait_ge(ms_x, 1)
            rsqrt(rx, msx, TT).then_inc(x_rstd, 1)
            pool.wait_ge(const, 16 * (NCONST - NFIRST))
            for s, i in walk(pool, PH):
                k = s.kind
                if k == "lat_a":
                    pool.wait_ge(ms_ready, count(s, i, "ms", 1))
                    rsqrt(rs[:, 0:TT], ms[:, 0:TT], TT).then_inc(rstd_ready, 1)
                elif k == "done_cmp_k":
                    pool.wait_ge(made["cmp_k"], 1)
                    rsqrt(rs[0:CROWS, 8:9], ms[0:CROWS, 8:9], 1, CROWS).then_inc(cmp_rstd, 1)
                elif k == "h_norm":
                    pool.wait_ge(h_ms, 1)
                    rsqrt(rh, msh, TT).then_inc(h_pow, 1)
                elif k == "shared_key":
                    pool.wait_ge(made["shared_key"], 1)
                elif k == "k_sq":
                    n = HPG if s.which == "mla" else 2
                    m = ms[:, 0:TT * n]
                    pool.wait_ge(free["A"], count(s, i, "tileA"))
                    if s.which == "mla":
                        m = m.rearrange("p (t n) -> p t n", n=n)
                        nc.gpsimd.tensor_tensor(m, m, ms_kr.unsqueeze(2).to_broadcast([P, TT, n]), ALU.add)
                    else:
                        nc.gpsimd.tensor_tensor(m, m, eps, ALU.add)
                    fence()
                    rsqrt(rs[:, 0:TT * n], ms[:, 0:TT * n], TT * n).then_inc(rstd_ready, 1)
                    if s.which == "mla":
                        fence()
                        for t in range(TT):
                            ins = nc.gpsimd.tensor_tensor(qk_m[:, t, HPG:2 * HPG, MLA_NOPE:DK],
                                                          kr[:, t, :].unsqueeze(1).to_broadcast([P, HPG, MLA_ROT]),
                                                          rs[:, t * HPG:(t + 1) * HPG].unsqueeze(2).to_broadcast([P, HPG, MLA_ROT]), ALU.mult)
                        ins.then_inc(roped, 1)
                elif k == "k_scale" and s.which == "nsa":
                    pool.wait_ge(scaled, count(s, i, "scale", 1))
                    rotate(qk_n, 4, 0, NSA_ROT // 2, (cos_n[:], sin_n[:], cos_n[:], sin_n[:]))
                elif k == "q_sq":
                    X, _, tables, start, hw = head_view(s.which)
                    pool.wait_ge(taken, count(s, i, "taken"))
                    rotate(X, s.h, start, hw, [tables[:, n] for n in range(4)])
                    q = slice(2 * s.h, 2 * s.h + 4)
                    pool.wait_ge(free[s.bank], count(s, i, "tile" + s.bank))
                    nc.gpsimd.tensor_tensor(ms_q[:, q], ms_q[:, q], eps, ALU.add)
                    fence()
                    rsqrt(rq[:, q], ms_q[:, q], 4)
                    fence()
                    r = rq[:, q].rearrange("p (r n) -> p r n", n=2)
                    for c in (0, 2):
                        ins = nc.gpsimd.tensor_scalar(neg_rq[:, s.h:s.h + 2, c:c + 2], r, -1.0, None, ALU.mult)
                    ins.then_inc(rstd_ready, 1)

        @block.tensor
        def _(pe):
            def turn(dst, src, rows=P):
                return nc.tensor.transpose(dst, src, ident[0:rows, 0:rows])

            def turn_pair(src, cols, bank):
                for c in range(2):
                    for t in range(TT):
                        ins = turn(bank[:, c * SEQ + t * P:c * SEQ + (t + 1) * P], src[:, t, cols + c * P:cols + (c + 1) * P])
                return ins

            for s, i in walk(pe, PH):
                k = s.kind
                if k in PAIRED:
                    pe.wait_ge(fill_out, count(s, i, "fill", -1))
                elif "fill" in s.kinds and k not in ("setup", "turn_x"):
                    pe.wait_ge(fill_out, count(s, i, "fill"))
                if k == "unit":
                    if s.first:
                        split_banks = bool(s.per) and s.weight in ("mla_w_uk", "ks_kw")
                        if split_banks:
                            pe.wait_ge(half_free, count(s, i, "half"))
                        else:
                            wait(pe, free[s.bank], count(s, i, "tile" + s.bank))
                        if s.pair is not None:
                            pe.wait_ge(fill_out, 2 + s.pair)
                        elif s.lhs != "x" or s.weight == "w_ffn_gate":
                            wait(pe, fill_out, count(s, i, "fill"))
                            if s.lhs in ("fk", "fv"):
                                pe.wait_ge(flat_out, 4 if s.lhs == "fv" else 3)
                            if s.lhs in ("om", "on"):
                                pe.wait_ge(o_free, count(s, i, "head", 1))
                        else:
                            wait(pe, fill_out, 1 + KD // 2)
                    elif s.pair is not None:
                        pe.wait_ge(fill_out, 2 + s.pair)
                    elif s.lhs in ("ff", "m") or s.weight == "w_ffn_gate":
                        if s.chunk >= (KF if s.lhs == "ff" else KD) - 4:
                            wait(pe, fill_out, count(s, i, "fill"))
                    pe.wait_ge(split, count(s, i, "unit", 1))
                    sl = slot_of(s)
                    outs = halves(s)
                    M_ = {"fk": BOTH, "fv": BOTH, "hk": CROWS, "hv": CROWS}.get(s.lhs, P)
                    for c in range(s.m):
                        first, last = s.first and c == 0, s.last and c == s.m - 1
                        for t, c0, c1, bank in outs:
                            dst = bank[0:M_, 0:c1 - c0]
                            if s.first and c == 0 and t and split_banks:
                                pe.wait_ge(free[s.bank], count(s, i, "tile" + s.bank))
                            wh = whi[0:s.rows, sl, c * s.width + c0:c * s.width + c1]
                            wl = wlo[0:s.rows, sl, c * s.width + c0:c * s.width + c1]
                            nc.tensor.matmul(dst, lhsT(s, 0, s.chunk + c, t), wh, start=first, stop=False)
                            if M_ == BOTH:
                                ins = nc.tensor.matmul(dst, lhsT(s, 0, s.chunk + c, t), wl, start=False, stop=last)
                                continue
                            nc.tensor.matmul(dst, lhsT(s, 0, s.chunk + c, t), wl, start=False, stop=False)
                            ins = nc.tensor.matmul(dst, lhsT(s, 1, s.chunk + c, t), wh, start=False, stop=last)
                    ins.then_inc(used, 1)
                elif k == "setup":
                    pe.wait_ge(const0, 16 * NFIRST)
                    turn(QT[:, 0:2 * KD], rows_sb[:], 2 * KD).then_inc(filled, 1)
                elif k == "turn_pe":
                    pe.wait_ge(const, 16 * (NCONST - NFIRST))
                    for c, c0 in enumerate(K_COLS):
                        turn(QT[:, c * CMP_LEN:(c + 1) * CMP_LEN], pe_k_sb[:, c0:c0 + P], CMP_LEN)
                    turn(QT[:, 96:128], pe_v_sb[:], CMP_LEN).then_inc(filled, 1)
                elif k == "turn_x":
                    pe.wait_ge(x_in[s.pair // 2], 16)
                    pe.wait_ge(fill_out, max(1, count(s, i, "fill") - 3))
                    turn_pair(x_sb, 2 * s.pair * P, FB[s.bank]).then_inc(filled, 1)
                elif k == "turn_kc":
                    pe.wait_ge(free["A"], count(s, i, "tileA"))
                    pe.wait_ge(free["B"], count(s, i, "tileB"))
                    c0 = K_COLS[s.c0]
                    for g in range(2):
                        for t in range(TT):
                            ins = turn(QT[:, g * SEQ + t * P:g * SEQ + (t + 1) * P], kc_in[:, t, 2 * s.slot + g, c0:c0 + P])
                    ins.then_inc(filled, 1)
                elif k == "turn_vc":
                    pe.wait_ge(free["A"], count(s, i, "tileA"))
                    turn_pair(vc_in, 2 * s.slot * P, QT).then_inc(filled, 1)
                elif k == "turn_lat":
                    pe.wait_ge(scaled, count(s, i, "scale"))
                    turn_pair(lat[:, :, s.which, :], 2 * s.pair * P, QT).then_inc(filled, 1)
                elif k == "turn_hidden":
                    pe.wait_ge(made["hidden_" + ("k" if s.c0 < 6 else "v")], 1)
                    for c in range(s.c0, s.c1):
                        ins = turn(QT[:, (c - s.c0) * CROWS:(c - s.c0 + 1) * CROWS], hid[:, c * P:(c + 1) * P], CROWS)
                    ins.then_inc(filled, 1)
                elif k == "turn_cmp":
                    pe.wait_ge(cmp_normed, 1)
                    for c in range(2):
                        ins = turn(QT[0:HALF, c * CROWS:(c + 1) * CROWS], kc[:, c * HALF:(c + 1) * HALF], CROWS)
                    ins.then_inc(filled, 1)
                elif k == "turn_heads":
                    X = head_view(s.which)[0]
                    pe.wait_ge(roped, count(s, i, "rope"))
                    pe.wait_ge(scaled, count(s, i, "scale"))
                    if s.job:
                        pe.wait_ge(pt_out, count(s, i, "turn_probs"))
                    for slot, bank in ((s.lo, QT), (s.hi, TP)):
                        for c in range(2):
                            for t in range(TT):
                                ins = turn(bank[0:HALF, c * SEQ + t * P:c * SEQ + (t + 1) * P], X[:, t, slot, c * HALF:(c + 1) * HALF])
                        ins.then_inc(filled, 1)
                elif k == "scores":
                    T = head_view(s.which)[1]
                    r, kk = (s.job, HPG + s.job) if s.which == "mla" else (s.job // 2, HPG + s.job % 2)
                    pe.wait_ge(fill_out, count(s, i, "fill", -s.lo))
                    wait(pe, exped, count(s, i, "scores"))
                    def mm(dst, l, rr, **kw):
                        return nc.tensor.matmul(dst, l, rr, skip_group_check=True, **kw)
                    mm(S[:, 0:P], identb[:], maskb[:], start=True, stop=False)
                    mm(S[:, 2 * P:3 * P], identb[:], maskb[:], start=False, stop=False)
                    if s.which == "nsa":
                        tc = s.job % 2
                        SC = S[:, 3 * P:3 * P + CROWS]
                        mm(SC, identb[:], cmaskb[:, tc, bass.ds(i, 1), :].rearrange("p a n -> p (a n)"), start=False, stop=False)
                    for c in range(2):
                        q = [T[:, r, c * SEQ + t * P:c * SEQ + (t + 1) * P] for t in range(TT)]
                        if s.which == "nsa":
                            mm(SC, q[tc], kcT[:, c, :], start=False, stop=c == 1)
                        mm(S[:, 0:P], q[0], T[:, kk, c * SEQ:c * SEQ + P], start=False, stop=c == 1)
                        ins = mm(S[:, P:3 * P], q[1], T[:, kk, c * SEQ:(c + 1) * SEQ], start=False, stop=c == 1)
                    ins.then_inc(scored, 1)
                elif k == "turn_probs":
                    Pb = Pbs[:, s.job % 2, :]
                    pe.wait_ge(probs, count(s, i, "turn_probs", 1))
                    pe.wait_ge(fill_out, count(s, i, "fill"))
                    for q in range(3):
                        ins = turn(TP[:, q * P:(q + 1) * P], Pb[:, q * P:(q + 1) * P])
                    if s.which == "nsa":
                        ins = turn(TP[0:CROWS, 3 * P:4 * P], Pb[:, 3 * P:3 * P + CROWS])
                    ins.then_inc(turned, 1)
                elif k == "values":
                    pe.wait_ge(pt_out, count(s, i, "values", 1))
                    if s.which == "mla":
                        V, j, start = v_m, s.job, True
                    else:
                        V, j, start = v_n, s.job % 2, s.job % 2 == 0
                    if start:
                        pe.wait_ge(o_free, count(s, i, "head", 1))
                    stop = s.last
                    nc.tensor.matmul(OP[:, 0:SEQ], V[:, 0, j, :], pT[:, 0:SEQ], start=start, stop=False, skip_group_check=True)
                    ins = nc.tensor.matmul(OP[:, P:SEQ], V[:, 1, j, :], pT[:, SEQ:SEQ + P], start=False, stop=stop, skip_group_check=True)
                    if s.which == "nsa":
                        tc = s.job % 2
                        ins = nc.tensor.matmul(OP[:, tc * P:(tc + 1) * P], v_c[:], pT[0:CROWS, 3 * P:4 * P], start=False, stop=stop,
                                               skip_group_check=True)
                    ins.then_inc(valued, 1)
                elif k == "turn_merged":
                    pe.wait_ge(made["merged"], count(s, i, "merged"))
                    turn_pair(mt, 2 * s.pair * P, FB[s.pair]).then_inc(filled, 1)
                elif k == "turn_h":
                    pe.wait_ge(free["AB"[s.tile % 2]], count(s, i, "tile" + "AB"[s.tile % 2]))
                    turn_pair(h, s.tile * N + 2 * s.pair * P, FB[s.pair]).then_inc(filled, 1)
                elif k == "turn_ff":
                    pe.wait_ge(free["B"], count(s, i, "tileB"))
                    turn_pair(ft, 2 * s.pair * P, FB[s.pair]).then_inc(filled, 1)


_INS = ['x', 'attn_norm_g', 'w_in', 'mla_q_lat_g', 'mla_kv_lat_g', 'mla_w_uq', 'mla_w_uk', 'mla_w_uv',
        'mla_q_norm_g', 'mla_k_norm_g', 'nsa_q_norm_g', 'nsa_k_norm_g', 'cmp_pe_k', 'cmp_pe_v',
        'cmp_k_w1', 'cmp_k_b1', 'cmp_k_w2', 'cmp_k_b2', 'cmp_v_w1', 'cmp_v_b1', 'cmp_v_w2', 'cmp_v_b2',
        'w_proj_mla', 'w_proj_nsa', 'w_out', 'ffn_norm_g', 'w_ffn_gate', 'w_ffn_up', 'w_ffn_down']


def _constants():
    import numpy as np
    bf16 = np.dtype("bfloat16")
    c = {"ident": np.eye(P, dtype=np.float32), "identb": np.eye(P, dtype=bf16)}
    q = np.arange(P)
    c["maskb"] = np.where(q[None, :] <= q[:, None], 0.0, MASKED).astype(bf16)
    end = np.arange(NCMP) * CMP_STRIDE + CMP_LEN - 1
    ok = np.zeros((SEQ, GROUPS, GROUPS, NCMP), bool)
    for g in range(GROUPS):
        ok[:, g, g, :] = end[None, :] <= np.arange(SEQ)[:, None]
    c["cmaskb"] = np.where(ok, 0.0, MASKED).reshape(SEQ, GROUPS, CROWS).astype(bf16)

    def tables(pos, dim):
        inv = np.float32(500000.0) ** (-np.arange(0, dim, 2, dtype=np.float32) / np.float32(dim))
        ang = pos.astype(np.float32)[:, None] * inv[None, :].astype(np.float32)
        return np.cos(ang).astype(np.float32), np.sin(ang).astype(np.float32)
    c["cos_m"], c["sin_m"] = tables(np.arange(SEQ), MLA_ROT)
    c["cos_n"], c["sin_n"] = tables(np.arange(SEQ), NSA_ROT)
    c["cos_c"], c["sin_c"] = tables(np.tile(end, GROUPS), NSA_ROT)
    return c


def kernel(**inputs):
    import numpy as _np
    import concourse.bacc as _bacc
    from concourse import mybir as _mybir
    from concourse.bass_utils import run_bass_kernel_spmd as _run

    nc = _bacc.Bacc("TRN2", target_bir_lowering=False, num_devices=1)
    arrays, aps = {}, {}
    for name in _INS:
        a = _np.ascontiguousarray(inputs[name])
        arrays[f"in_{name}_dram"] = a
        aps[name] = nc.dram_tensor(f"in_{name}_dram", a.shape, _mybir.dt.from_np(a.dtype), kind="ExternalInput").ap()[0]
    for name, a in _constants().items():
        arrays[f"const_{name}_dram"] = a
        aps[name] = nc.dram_tensor(f"const_{name}_dram", a.shape, _mybir.dt.from_np(a.dtype), kind="ExternalInput").ap()
    out = nc.dram_tensor("out_0_dram", (1, SEQ, D), _mybir.dt.float32, kind="ExternalOutput").ap()
    build(nc, aps, out[0])
    r = _run(nc, [arrays], core_ids=[0])
    return r.results[0]["out_0_dram"]
```
